# Optimizing a Trainium2 kernel written in Bass

```python
import jax, jax.numpy as jnp
from jax import lax
import numpy as np

D_MODEL = 1024
BATCH = 1
SEQ = 512
DEPTH = 2

GRID_W = 64
CTX_LEN = 256
HEAD_DIM = 64
NORM_EPS = 1e-6
POOL_WIDTH = D_MODEL // 4
POOL_WINDOWS = (2, 4, 8, 16)
POOL_GROUP = POOL_WIDTH // 4
GLA_WIDTH = D_MODEL // 4
GLA_DK = 64
GLA_DV = 64
GLA_HEADS = GLA_WIDTH // GLA_DV
GLA_GATE_RANK = 16
GLA_GATE_NORM = 16.0
GLA_CHUNK = 64
ATTN_WIDTH = D_MODEL // 2
ATTN_Q_HEADS = ATTN_WIDTH // HEAD_DIM
ATTN_KV_HEADS = ATTN_Q_HEADS // 4
ATTN_KV_WIDTH = ATTN_KV_HEADS * HEAD_DIM
Q_BLOCK = 128
ROPE_THETA = 10000.0
MLP_HIDDEN = 4 * D_MODEL
IN_SIZES = (POOL_WIDTH,
            GLA_HEADS * GLA_DK, GLA_HEADS * GLA_DK,
            GLA_WIDTH, GLA_WIDTH,
            GLA_GATE_RANK, GLA_GATE_RANK,
            ATTN_WIDTH, ATTN_KV_WIDTH, ATTN_KV_WIDTH)
IN_WIDTH = sum(IN_SIZES)
MIX_WIDTH = POOL_WIDTH + GLA_WIDTH + ATTN_WIDTH


def rmsnorm(x, g):
    xf = x.astype(jnp.float32)
    y = xf * lax.rsqrt(jnp.mean(xf * xf, axis=-1, keepdims=True) + NORM_EPS)
    return (y * g).astype(x.dtype)

def modulation(cvec, w_mod, b_mod):
    m = (jax.nn.silu(cvec) @ w_mod + b_mod)[..., None, :]
    return jnp.split(m, 6, axis=-1)

def split_in(u):
    idx = np.cumsum(np.array(IN_SIZES))[:-1].tolist()
    return jnp.split(u, idx, axis=-1)

def pool_mixer(p, w_pool, s_pool):
    B, N, _ = p.shape
    pg = p.reshape(B, N, 4, POOL_GROUP)
    pf = pg.astype(jnp.float32)
    P = jnp.concatenate([jnp.zeros((B, 1, 4, POOL_GROUP), jnp.float32), jnp.cumsum(pf, axis=1)], axis=1)
    t = np.arange(N)
    outs = []
    for gi, w in enumerate(POOL_WINDOWS):
        lo = np.clip(t - w // 2, 0, N - 1)
        hi = np.clip(t + w // 2 - 1, 0, N - 1)
        cnt = jnp.asarray((hi - lo + 1)[None, :, None], jnp.float32)
        Pg = P[:, :, gi]
        mean = (Pg[:, hi + 1] - Pg[:, lo]) / cnt
        outs.append(mean - pf[:, :, gi])
    m = jnp.stack(outs, axis=2)
    y = jnp.einsum('bngc,gcd->bngd', m, w_pool.astype(jnp.float32))
    return (y.reshape(B, N, POOL_WIDTH) * s_pool).astype(p.dtype)

def gla_features(q, k, v, r_f, r_b, w_gate, b_gate):
    B, N, _ = q.shape
    f32 = jnp.float32
    heads = lambda a: a.astype(f32).reshape(B, N, GLA_HEADS, -1)
    wg = w_gate.astype(f32)
    bg = b_gate.astype(f32)
    la_f = jax.nn.log_sigmoid(r_f.astype(f32) @ wg[0] + bg[0]) / GLA_GATE_NORM
    la_b = jax.nn.log_sigmoid(r_b.astype(f32) @ wg[1] + bg[1]) / GLA_GATE_NORM
    return heads(q) * GLA_DK ** -0.5, heads(k), heads(v), heads(la_f), heads(la_b)

def gla_chunk_scan(q, k, v, la, s0, strict):
    B, N, H, _ = q.shape
    C = GLA_CHUNK
    nc = N // C
    to_chunks = lambda a: a.reshape(B, nc, C, H, a.shape[-1]).transpose(1, 0, 3, 2, 4)
    mask = np.tril(np.ones((C, C), bool), k=-1 if strict else 0)[:, :, None]

    def step(S, inp):
        qc, kc, vc, lc = inp
        b = jnp.cumsum(lc, axis=2)
        o_inter = jnp.einsum('bhid,bhde->bhie', qc * jnp.exp(b), S)
        diff = b[:, :, :, None, :] - b[:, :, None, :, :]
        decay = jnp.exp(jnp.where(mask, diff, -jnp.inf))
        A = jnp.einsum('bhid,bhjd,bhijd->bhij', qc, kc, decay)
        o = o_inter + jnp.einsum('bhij,bhje->bhie', A, vc)
        bl = b[:, :, -1:, :]
        S_new = jnp.exp(bl[:, :, 0, :, None]) * S + jnp.einsum('bhjd,bhje->bhde', kc * jnp.exp(bl - b), vc)
        return S_new, o

    S, o = lax.scan(step, s0, (to_chunks(q), to_chunks(k), to_chunks(v), to_chunks(la)))
    return o.transpose(1, 0, 3, 2, 4).reshape(B, N, H, -1), S

def gla_bidir(q, k, v, la_f, la_b, s_f, s_b):
    o_f, s_f_new = gla_chunk_scan(q, k, v, la_f, s_f, strict=False)
    rev = lambda a: a[:, ::-1]
    o_b, s_b_new = gla_chunk_scan(rev(q), rev(k), rev(v), rev(la_b), s_b, strict=True)
    return o_f + rev(o_b), s_f_new, s_b_new

def gla_output(o, g, g_gla, out_dtype):
    B, N = o.shape[:2]
    gate = jax.nn.silu(g.astype(jnp.float32)).reshape(B, N, GLA_HEADS, GLA_DV)
    return (rmsnorm(o, g_gla) * gate).reshape(B, N, GLA_WIDTH).astype(out_dtype)

def attn_qkv(q, k, v, g_q, g_k):
    B, N, _ = q.shape
    q = rmsnorm(q.reshape(B, N, ATTN_Q_HEADS, HEAD_DIM), g_q)
    k = rmsnorm(k.reshape(B, N, ATTN_KV_HEADS, HEAD_DIM), g_k)
    return q, k, v.reshape(B, N, ATTN_KV_HEADS, HEAD_DIM)

def axial_rope(x, rows, cols):
    half = HEAD_DIM // 2
    inv = ROPE_THETA ** (-jnp.arange(0, half, 2, dtype=jnp.float32) / half)

    def rot(xh, pos):
        ang = pos.astype(jnp.float32)[:, None] * inv
        cos = jnp.cos(ang)[None, :, None, :]
        sin = jnp.sin(ang)[None, :, None, :]
        x1, x2 = jnp.split(xh.astype(jnp.float32), 2, axis=-1)
        return jnp.concatenate([x1 * cos - x2 * sin, x1 * sin + x2 * cos], axis=-1)

    xr, xc = jnp.split(x, 2, axis=-1)
    return jnp.concatenate([rot(xr, rows), rot(xc, cols)], axis=-1).astype(x.dtype)

def gqa_attend(qb, k, v):
    s = jnp.einsum('bqhgd,bkhd->bhgqk', qb, k, preferred_element_type=jnp.float32) * HEAD_DIM ** -0.5
    p = jax.nn.softmax(s, axis=-1)
    return jnp.einsum('bhgqk,bkhd->bqhgd', p.astype(v.dtype), v)

def latent_attention(q, k_all, v_all):
    B, N = q.shape[:2]
    G = ATTN_Q_HEADS // ATTN_KV_HEADS
    nb = N // Q_BLOCK
    qb = q.reshape(B, nb, Q_BLOCK, ATTN_KV_HEADS, G, HEAD_DIM).swapaxes(0, 1)
    ob = lax.map(lambda blk: gqa_attend(blk, k_all, v_all), qb)
    return ob.swapaxes(0, 1).reshape(B, N, ATTN_WIDTH)

def context_attention(q, k, v):
    B, L = q.shape[:2]
    G = ATTN_Q_HEADS // ATTN_KV_HEADS
    return gqa_attend(q.reshape(B, L, ATTN_KV_HEADS, G, HEAD_DIM), k, v).reshape(B, L, ATTN_WIDTH)

def squared_relu_mlp(h, w_up, w_down):
    return jnp.square(jax.nn.relu(h @ w_up)) @ w_down

def trunk_layer(x, cx, c, c_ctx, rows, cols, w_mod, b_mod, g_mix, w_in, w_pool, s_pool, w_gate, b_gate,
                g_gla, g_q, g_k, w_out, g_mlp, w_up, w_down, update_ctx):
    sh1, sc1, ga1, sh2, sc2, ga2 = modulation(c, w_mod, b_mod)
    sh1c, sc1c, ga1c, sh2c, sc2c, ga2c = modulation(c_ctx[None], w_mod, b_mod)

    u = (rmsnorm(x, g_mix) * (1 + sc1) + sh1) @ w_in
    uc = (rmsnorm(cx, g_mix) * (1 + sc1c) + sh1c) @ w_in
    p, gq, gk, gv, gg, rf, rb, aq, ak, av = split_in(u)
    pc, gqc, gkc, gvc, ggc, rfc, rbc, aqc, akc, avc = split_in(uc)

    B = x.shape[0]
    s_zero = jnp.zeros((B, GLA_HEADS, GLA_DK, GLA_DV), jnp.float32)
    o_gc, s_f, s_b = gla_bidir(*gla_features(gqc, gkc, gvc, rfc, rbc, w_gate, b_gate), s_zero, s_zero)
    o_gl, _, _ = gla_bidir(*gla_features(gq, gk, gv, rf, rb, w_gate, b_gate), s_f, s_b)

    qc_, kc_, vc_ = attn_qkv(aqc, akc, avc, g_q, g_k)
    ql, kl, vl = attn_qkv(aq, ak, av, g_q, g_k)
    ql = axial_rope(ql, rows, cols)
    kl = axial_rope(kl, rows, cols)
    k_all = jnp.concatenate([kc_, kl], axis=1)
    v_all = jnp.concatenate([vc_, vl], axis=1)

    mix = jnp.concatenate([pool_mixer(p, w_pool, s_pool),
                           gla_output(o_gl, gg, g_gla, x.dtype),
                           latent_attention(ql, k_all, v_all)], axis=-1) @ w_out
    x = x + ga1 * mix
    x = x + ga2 * squared_relu_mlp(rmsnorm(x, g_mlp) * (1 + sc2) + sh2, w_up, w_down)

    if update_ctx:
        mix_c = jnp.concatenate([pool_mixer(pc, w_pool, s_pool),
                                 gla_output(o_gc, ggc, g_gla, cx.dtype),
                                 context_attention(qc_, kc_, vc_)], axis=-1) @ w_out
        cx = cx + ga1c * mix_c
        cx = cx + ga2c * squared_relu_mlp(rmsnorm(cx, g_mlp) * (1 + sc2c) + sh2c, w_up, w_down)
    return x, cx

def first_inputs(seed: int = 0) -> dict:
    key = jax.random.key(seed)
    ks = jax.random.split(key, 20)
    D = D_MODEL
    nrm = lambda k, shape, scale: jax.random.normal(k, shape, jnp.float32) * scale
    return {
        "x": nrm(ks[0], (BATCH, SEQ, D), 1.0),
        "c": nrm(ks[1], (BATCH, D), 1.0),
        "ctx": nrm(ks[2], (BATCH, CTX_LEN, D), 1.0),
        "c_ctx": nrm(ks[3], (D,), 1.0),
        "w_mod": nrm(ks[4], (DEPTH, D, 6 * D), 0.5 * D ** -0.5),
        "b_mod": nrm(ks[5], (DEPTH, 6 * D), 0.01),
        "g_mix": 1.0 + nrm(ks[6], (DEPTH, D), 0.05),
        "w_in": nrm(ks[7], (DEPTH, D, IN_WIDTH), D ** -0.5),
        "w_pool": nrm(ks[8], (DEPTH, 4, POOL_GROUP, POOL_GROUP), POOL_GROUP ** -0.5),
        "s_pool": 1.0 + nrm(ks[9], (DEPTH, POOL_WIDTH), 0.1),
        "w_gate": nrm(ks[10], (DEPTH, 2, GLA_GATE_RANK, GLA_HEADS * GLA_DK), GLA_GATE_RANK ** -0.5),
        "b_gate": nrm(ks[11], (DEPTH, 2, GLA_HEADS * GLA_DK), 0.1),
        "g_gla": 1.0 + nrm(ks[12], (DEPTH, GLA_DV), 0.05),
        "g_q": 1.0 + nrm(ks[13], (DEPTH, HEAD_DIM), 0.05),
        "g_k": 1.0 + nrm(ks[14], (DEPTH, HEAD_DIM), 0.05),
        "w_out": nrm(ks[15], (DEPTH, MIX_WIDTH, D), MIX_WIDTH ** -0.5),
        "g_mlp": 1.0 + nrm(ks[16], (DEPTH, D), 0.05),
        "w_up": nrm(ks[17], (DEPTH, D, MLP_HIDDEN), D ** -0.5),
        "w_down": nrm(ks[18], (DEPTH, MLP_HIDDEN, D), MLP_HIDDEN ** -0.5),
        "g_final": 1.0 + nrm(ks[19], (D,), 0.05),
    }

def first_block(x, c, ctx, c_ctx, w_mod, b_mod, g_mix, w_in, w_pool, s_pool, w_gate, b_gate,
              g_gla, g_q, g_k, w_out, g_mlp, w_up, w_down, g_final):
    n_tok = x.shape[1]
    ROWS = n_tok // GRID_W
    rows = jnp.repeat(jnp.arange(ROWS, dtype=jnp.int32), GRID_W)
    cols = jnp.tile(jnp.arange(GRID_W, dtype=jnp.int32), ROWS)
    cx = ctx
    for l in range(DEPTH):
        x, cx = trunk_layer(x, cx, c, c_ctx, rows, cols, w_mod[l], b_mod[l], g_mix[l], w_in[l],
                            w_pool[l], s_pool[l], w_gate[l], b_gate[l], g_gla[l], g_q[l], g_k[l],
                            w_out[l], g_mlp[l], w_up[l], w_down[l], update_ctx=(l < DEPTH - 1))
    return rmsnorm(x, g_final)


DEPTH_2 = 1

SSM_EXPAND = 2
SSM_D_INNER = SSM_EXPAND * D_MODEL
SSM_HEAD_DIM = 64
SSM_N_HEADS = SSM_D_INNER // SSM_HEAD_DIM
SSM_N_GROUPS = 8
SSM_D_STATE = 128
SSM_CHUNK = 128
SSM_CONV_DIM = SSM_D_INNER + 2 * SSM_N_GROUPS * SSM_D_STATE
GDN_HEAD_K = 128
GDN_HEAD_V = 128
GDN_N_QK_HEADS = D_MODEL // GDN_HEAD_K
GDN_N_V_HEADS = 2 * GDN_N_QK_HEADS
GDN_KEY_DIM = GDN_N_QK_HEADS * GDN_HEAD_K
GDN_VAL_DIM = GDN_N_V_HEADS * GDN_HEAD_V
GDN_CHUNK = 64
GDN_CONV_DIM = 2 * GDN_KEY_DIM + GDN_VAL_DIM
CONV_K = 4
MLP_HIDDEN_2 = 4 * D_MODEL
EPS = 1e-6
IN_SPLIT_SIZES = (SSM_D_INNER, SSM_CONV_DIM, SSM_N_HEADS, GDN_CONV_DIM, GDN_VAL_DIM,
                  GDN_N_V_HEADS, GDN_N_V_HEADS, D_MODEL, D_MODEL)
IN_PROJ_DIM = sum(IN_SPLIT_SIZES)


def rmsnorm_2(x, w):
    xf = x.astype(jnp.float32)
    y = xf * lax.rsqrt(jnp.mean(xf * xf, axis=-1, keepdims=True) + EPS)
    return (y * w.astype(jnp.float32)).astype(x.dtype)

def l2norm(x):
    return x * lax.rsqrt(jnp.sum(x * x, axis=-1, keepdims=True) + EPS)

def causal_depthwise_conv(x, w):
    return lax.conv_general_dilated(
        x, w[:, None, :].astype(x.dtype), window_strides=(1,), padding=[(CONV_K - 1, 0)],
        dimension_numbers=('NWC', 'WIO', 'NWC'), feature_group_count=x.shape[-1])

def ssd_chunked_scan(xh, dt, A, Bm, Cm):
    Bsz, S, H, P = xh.shape
    G, N = Bm.shape[-2:]
    hg = H // G
    L = SSM_CHUNK
    nc = S // L
    xdt = jnp.moveaxis((xh * dt[..., None]).reshape(Bsz, nc, L, G, hg, P), 1, 0)
    a = jnp.moveaxis((dt * A).reshape(Bsz, nc, L, G, hg), 1, 0)
    Bc = jnp.moveaxis(Bm.reshape(Bsz, nc, L, G, N), 1, 0)
    Cc = jnp.moveaxis(Cm.reshape(Bsz, nc, L, G, N), 1, 0)
    causal = jnp.tril(jnp.ones((L, L), dtype=bool))[None, :, :, None, None]

    def step(state, inp):
        xc, ac, bc, cc = inp
        acum = jnp.cumsum(ac, axis=1)
        seg = acum[:, :, None] - acum[:, None, :]
        decay = jnp.exp(jnp.where(causal, seg, -jnp.inf))
        cb = jnp.einsum('blgn,bsgn->blsg', cc, bc)
        y_diag = jnp.einsum('blsg,blsgh,bsghp->blghp', cb, decay, xc)
        y_off = jnp.einsum('blgn,bghpn->blghp', cc, state) * jnp.exp(acum)[..., None]
        a_last = acum[:, -1]
        w_s = jnp.exp(a_last[:, None] - acum)
        new_state = state * jnp.exp(a_last)[..., None, None] + jnp.einsum(
            'bsgn,bsgh,bsghp->bghpn', bc, w_s, xc)
        return new_state, y_diag + y_off

    state0 = jnp.zeros((Bsz, G, hg, P, N), dtype=jnp.float32)
    _, y = lax.scan(step, state0, (xdt, a, Bc, Cc))
    return jnp.moveaxis(y, 0, 1).reshape(Bsz, S, H, P)

def gated_delta_rule_chunked(q, k, v, g, beta):
    Bsz, S, H, dk = q.shape
    dv = v.shape[-1]
    L = GDN_CHUNK
    nc = S // L
    q = q * (dk ** -0.5)

    def chunks(t):
        t = t.reshape((Bsz, nc, L, H) + t.shape[3:])
        return jnp.moveaxis(t, (1, 3), (0, 2))

    causal = jnp.tril(jnp.ones((L, L), dtype=bool))
    strict = jnp.tril(jnp.ones((L, L), dtype=bool), -1)
    eye = jnp.eye(L, dtype=jnp.float32)

    def step(state, inp):
        qc, kc, vc, gc, bc = inp
        gcum = jnp.cumsum(gc, axis=-1)
        dmat = jnp.exp(jnp.where(causal, gcum[..., :, None] - gcum[..., None, :], -jnp.inf))
        kb = kc * bc[..., None]
        a_low = jnp.where(strict, jnp.einsum('bhid,bhjd->bhij', kb, kc) * dmat, 0.0)
        rhs = jnp.concatenate([vc * bc[..., None], kb * jnp.exp(gcum)[..., None]], axis=-1)
        sol = lax.linalg.triangular_solve(eye + a_low, rhs, left_side=True, lower=True,
                                          unit_diagonal=True)
        u, w = sol[..., :dv], sol[..., dv:]
        attn = jnp.einsum('bhid,bhjd->bhij', qc, kc) * dmat
        v_new = u - jnp.einsum('bhlk,bhkv->bhlv', w, state)
        o = jnp.einsum('bhlk,bhkv->bhlv', qc * jnp.exp(gcum)[..., None], state) + jnp.einsum(
            'bhij,bhjv->bhiv', attn, v_new)
        g_last = gcum[..., -1]
        k_dec = kc * jnp.exp(g_last[..., None] - gcum)[..., None]
        new_state = state * jnp.exp(g_last)[..., None, None] + jnp.einsum(
            'bhlk,bhlv->bhkv', k_dec, v_new)
        return new_state, o

    state0 = jnp.zeros((Bsz, H, dk, dv), dtype=jnp.float32)
    _, o = lax.scan(step, state0, (chunks(q), chunks(k), chunks(v), chunks(g), chunks(beta)))
    return jnp.moveaxis(o, (0, 2), (1, 3)).reshape(Bsz, S, H, dv)

def mamba2_branch(z, xbc, dt_raw, conv_w, conv_b, dt_bias, A_log, d_skip, norm_w):
    f32 = jnp.float32
    Bsz, S, _ = xbc.shape
    xbc = jax.nn.silu(causal_depthwise_conv(xbc, conv_w) + conv_b)
    xs, Bm, Cm = jnp.split(xbc, [SSM_D_INNER, SSM_D_INNER + SSM_N_GROUPS * SSM_D_STATE], axis=-1)
    xh = xs.reshape(Bsz, S, SSM_N_HEADS, SSM_HEAD_DIM).astype(f32)
    dt = jax.nn.softplus(dt_raw.astype(f32) + dt_bias.astype(f32))
    A = -jnp.exp(A_log.astype(f32))
    y = ssd_chunked_scan(xh, dt, A,
                         Bm.reshape(Bsz, S, SSM_N_GROUPS, SSM_D_STATE).astype(f32),
                         Cm.reshape(Bsz, S, SSM_N_GROUPS, SSM_D_STATE).astype(f32))
    y = y + d_skip.astype(f32)[:, None] * xh
    y = y.reshape(Bsz, S, SSM_D_INNER) * jax.nn.silu(z.astype(f32))
    y = rmsnorm_2(y.reshape(Bsz, S, SSM_N_GROUPS, -1), norm_w.reshape(SSM_N_GROUPS, -1))
    return y.reshape(Bsz, S, SSM_D_INNER).astype(z.dtype)

def gated_deltanet_branch(qkv, z, b, a, conv_w, dt_bias, A_log, norm_w):
    f32 = jnp.float32
    Bsz, S, _ = qkv.shape
    qkv = jax.nn.silu(causal_depthwise_conv(qkv, conv_w))
    q, k, v = jnp.split(qkv, [GDN_KEY_DIM, 2 * GDN_KEY_DIM], axis=-1)
    rep = GDN_N_V_HEADS // GDN_N_QK_HEADS
    q = jnp.repeat(l2norm(q.reshape(Bsz, S, GDN_N_QK_HEADS, GDN_HEAD_K).astype(f32)), rep, axis=2)
    k = jnp.repeat(l2norm(k.reshape(Bsz, S, GDN_N_QK_HEADS, GDN_HEAD_K).astype(f32)), rep, axis=2)
    v = v.reshape(Bsz, S, GDN_N_V_HEADS, GDN_HEAD_V).astype(f32)
    beta = jax.nn.sigmoid(b.astype(f32))
    g = -jnp.exp(A_log.astype(f32)) * jax.nn.softplus(a.astype(f32) + dt_bias.astype(f32))
    o = gated_delta_rule_chunked(q, k, v, g, beta)
    o = rmsnorm_2(o, norm_w) * jax.nn.silu(z.reshape(Bsz, S, GDN_N_V_HEADS, GDN_HEAD_V).astype(f32))
    return o.reshape(Bsz, S, GDN_VAL_DIM).astype(z.dtype)

def second_inputs(seed: int = 0) -> dict:
    key = jax.random.key(seed)
    ks = jax.random.split(key, 26)
    f32 = jnp.float32
    nrm = lambda k, shape, scale: jax.random.normal(k, shape, f32) * scale
    gain = lambda k, shape: 1.0 + 0.02 * jax.random.normal(k, shape, f32)

    def inv_softplus_dt(k, shape):
        dt = jnp.exp(jax.random.uniform(k, shape, f32, np.log(1e-3), np.log(1e-1)))
        return dt + jnp.log(-jnp.expm1(-dt))

    Dm = D_MODEL
    return {
        'x': jax.random.normal(ks[0], (BATCH, SEQ, Dm), f32),
        'c': jax.random.normal(ks[1], (BATCH, Dm), f32),
        'w_ada': nrm(ks[2], (DEPTH_2, Dm, 6 * Dm), 0.5 * Dm ** -0.5),
        'b_ada': nrm(ks[3], (DEPTH_2, 6 * Dm), 0.02),
        'norm_mix_pre': gain(ks[4], (DEPTH_2, Dm)),
        'norm_mix_post': gain(ks[5], (DEPTH_2, Dm)),
        'w_in': nrm(ks[6], (DEPTH_2, Dm, IN_PROJ_DIM), Dm ** -0.5),
        'ssm_conv_w': nrm(ks[7], (DEPTH_2, CONV_K, SSM_CONV_DIM), CONV_K ** -0.5),
        'ssm_conv_b': nrm(ks[8], (DEPTH_2, SSM_CONV_DIM), 0.02),
        'ssm_dt_bias': inv_softplus_dt(ks[9], (DEPTH_2, SSM_N_HEADS)),
        'ssm_A_log': jnp.log(jax.random.uniform(ks[10], (DEPTH_2, SSM_N_HEADS), f32, 1.0, 16.0)),
        'ssm_D': gain(ks[11], (DEPTH_2, SSM_N_HEADS)),
        'ssm_norm_w': gain(ks[12], (DEPTH_2, SSM_D_INNER)),
        'gdn_conv_w': nrm(ks[13], (DEPTH_2, CONV_K, GDN_CONV_DIM), CONV_K ** -0.5),
        'gdn_dt_bias': inv_softplus_dt(ks[14], (DEPTH_2, GDN_N_V_HEADS)),
        'gdn_A_log': jnp.log(jax.random.uniform(ks[15], (DEPTH_2, GDN_N_V_HEADS), f32, 1.0, 16.0)),
        'gdn_norm_w': gain(ks[16], (DEPTH_2, GDN_HEAD_V)),
        'w_ssm_up': nrm(ks[17], (DEPTH_2, SSM_D_INNER, Dm), SSM_D_INNER ** -0.5),
        'w_gdn_up': nrm(ks[18], (DEPTH_2, GDN_VAL_DIM, Dm), GDN_VAL_DIM ** -0.5),
        'w_out': nrm(ks[19], (DEPTH_2, Dm, Dm), Dm ** -0.5),
        'norm_mlp_pre': gain(ks[20], (DEPTH_2, Dm)),
        'norm_mlp_post': gain(ks[21], (DEPTH_2, Dm)),
        'w_mlp_up': nrm(ks[22], (DEPTH_2, Dm, MLP_HIDDEN_2), Dm ** -0.5),
        'w_mlp_down': nrm(ks[23], (DEPTH_2, MLP_HIDDEN_2, Dm), MLP_HIDDEN_2 ** -0.5),
    }

def second_block(x, c, w_ada, b_ada, norm_mix_pre, norm_mix_post, w_in, ssm_conv_w, ssm_conv_b,
              ssm_dt_bias, ssm_A_log, ssm_D, ssm_norm_w, gdn_conv_w, gdn_dt_bias, gdn_A_log,
              gdn_norm_w, w_ssm_up, w_gdn_up, w_out, norm_mlp_pre, norm_mlp_post, w_mlp_up,
              w_mlp_down):
    offsets = [int(o) for o in np.cumsum(IN_SPLIT_SIZES)[:-1]]
    c_act = jax.nn.silu(c)
    for l in range(DEPTH_2):
        mod = c_act @ w_ada[l] + b_ada[l]
        sh1, sc1, g1, sh2, sc2, g2 = [m[:, None, :] for m in jnp.split(mod, 6, axis=-1)]

        h = rmsnorm_2(x, norm_mix_pre[l]) * (1.0 + sc1) + sh1
        proj = h @ w_in[l]
        (z_ssm, xbc, dt_raw, qkv, z_gdn, b_gdn, a_gdn,
         gate_ssm, gate_gdn) = jnp.split(proj, offsets, axis=-1)
        y_ssm = mamba2_branch(z_ssm, xbc, dt_raw, ssm_conv_w[l], ssm_conv_b[l], ssm_dt_bias[l],
                              ssm_A_log[l], ssm_D[l], ssm_norm_w[l]) @ w_ssm_up[l]
        y_gdn = gated_deltanet_branch(qkv, z_gdn, b_gdn, a_gdn, gdn_conv_w[l], gdn_dt_bias[l],
                                      gdn_A_log[l], gdn_norm_w[l]) @ w_gdn_up[l]
        merged = jax.nn.sigmoid(gate_ssm) * y_ssm + jax.nn.sigmoid(gate_gdn) * y_gdn
        x = x + g1 * rmsnorm_2(merged @ w_out[l], norm_mix_post[l])

        h = rmsnorm_2(x, norm_mlp_pre[l]) * (1.0 + sc2) + sh2
        y = jnp.square(jax.nn.relu(h @ w_mlp_up[l])) @ w_mlp_down[l]
        x = x + g2 * rmsnorm_2(y, norm_mlp_post[l])
    return x


_first_inputs = second_inputs


def second_inputs(seed=0):
    import zlib

    import numpy as np

    out = dict(_first_inputs(seed))
    spreads = {}
    factors = {'norm_mix_pre': 6.338,
     'norm_mix_post': 8.0,
     'ssm_conv_b': 64.0,
     'ssm_D': 64.0,
     'ssm_norm_w': 64.0,
     'gdn_A_log': 3.613,
     'gdn_norm_w': 22.835,
     'norm_mlp_pre': 27.248,
     'norm_mlp_post': 32.682}
    for name, (base, spread) in spreads.items():
        noise = np.random.default_rng([zlib.crc32(name.encode()), seed]).standard_normal(out[name].shape)
        drawn = base * np.exp(spread * noise) if base else spread * noise
        out[name] = __import__('jax').numpy.asarray(drawn.astype(out[name].dtype))
    for name, factor in factors.items():
        out[name] = (out[name] * factor).astype(out[name].dtype)
    return out


_narrow_inputs = second_inputs


def second_inputs(seed=0):

    out = dict(_narrow_inputs(seed))
    wider = {'ssm_D': 12.0, 'ssm_norm_w': 5.6, 'gdn_norm_w': 3.52, 'norm_mlp_post': 3.25}
    for name, times in wider.items():
        mean = out[name].mean()
        out[name] = (mean + times * (out[name] - mean)).astype(out[name].dtype)
    return out


def setup_inputs(seed=0):
    out = dict(first_inputs(seed))
    for name, value in second_inputs(seed + 1).items():
        if name != "x":
            out[name + "_2"] = value
    return out


def reference(
    x, c, ctx, c_ctx, w_mod, b_mod, g_mix, w_in, w_pool, s_pool, w_gate, b_gate, g_gla, g_q,
    g_k, w_out, g_mlp, w_up, w_down, g_final, c_2, w_ada_2, b_ada_2, norm_mix_pre_2,
    norm_mix_post_2, w_in_2, ssm_conv_w_2, ssm_conv_b_2, ssm_dt_bias_2, ssm_A_log_2, ssm_D_2,
    ssm_norm_w_2, gdn_conv_w_2, gdn_dt_bias_2, gdn_A_log_2, gdn_norm_w_2, w_ssm_up_2,
    w_gdn_up_2, w_out_2, norm_mlp_pre_2, norm_mlp_post_2, w_mlp_up_2, w_mlp_down_2,
):
    x = first_block(
        x, c, ctx, c_ctx, w_mod, b_mod, g_mix, w_in, w_pool, s_pool, w_gate, b_gate, g_gla, g_q,
        g_k, w_out, g_mlp, w_up, w_down, g_final,
    )
    return second_block(
        x, c_2, w_ada_2, b_ada_2, norm_mix_pre_2, norm_mix_post_2, w_in_2, ssm_conv_w_2,
        ssm_conv_b_2, ssm_dt_bias_2, ssm_A_log_2, ssm_D_2, ssm_norm_w_2, gdn_conv_w_2,
        gdn_dt_bias_2, gdn_A_log_2, gdn_norm_w_2, w_ssm_up_2, w_gdn_up_2, w_out_2,
        norm_mlp_pre_2, norm_mlp_post_2, w_mlp_up_2, w_mlp_down_2,
    )


_drawn_inputs = setup_inputs


def setup_inputs(seed=0):
    import zlib

    import numpy as np

    out = dict(_drawn_inputs(seed))
    spreads = {}
    factors = {'b_gate': 3.379,
     'g_gla': 3.49,
     'g_q': 8.0,
     'g_k': 8.0,
     'norm_mix_post_2': 2.725,
     'ssm_D_2': 7.011}
    for name, (base, spread) in spreads.items():
        noise = np.random.default_rng([zlib.crc32(name.encode()), seed]).standard_normal(out[name].shape)
        drawn = base * np.exp(spread * noise) if base else spread * noise
        out[name] = __import__('jax').numpy.asarray(drawn.astype(out[name].dtype))
    for name, factor in factors.items():
        out[name] = (out[name] * factor).astype(out[name].dtype)
    return out
```

```python
from contextlib import ExitStack

import numpy as np

import concourse.bass as bass
from concourse import mybir

P = 128
D = 1024
KT = D // P
HALF = 512
CTX_TILES, LAT_TILES = 2, 4
TILES = CTX_TILES + LAT_TILES
CTX = CTX_TILES * P
LAT = LAT_TILES * P
TOK = TILES * P
HEADS_Q, HEADS_KV, HD = 8, 2, 64
GLA_H = 4
LEVELS = 7
PASSES = 4
GROUPS = 8
EPS = 1e-6

F32 = mybir.dt.float32
U32 = mybir.dt.uint32
ALU = mybir.AluOpType
ACT = mybir.ActivationFunctionType
AX = mybir.AxisListType.X

C_POOL, C_GV, C_GG, C_AQ, C_AK, C_AV = 0, 256, 512, 768, 1280, 1408


class Stage:

    def __init__(self, core, name):
        self.core, self.nc, self.name = core, core.nc, name
        self.held = ExitStack()
        self.sems = []

    def __enter__(self):
        return self

    def sem(self, what):
        s = self.nc.alloc_semaphore(f"{self.name}_{what}")
        self.sems.append(s)
        return s

    def sb(self, what, shape, dt=F32):
        return self.held.enter_context(self.nc.sbuf_tensor(f"{self.name}_{what}", shape, dt))

    def block(self):
        return self.nc.Block(no_gpsimd_drain=True)

    def __exit__(self, kind, value, trace):
        if kind is None:
            for s in self.sems:
                self.nc.gpsimd.sem_clear(s)
            self.nc.all_engine_barrier(sem_only=True)
            for s in self.sems:
                self.nc.release_semaphore(s)
            self.held.close()


class Chain:

    def __init__(self, eng, sem):
        self.eng, self.sem, self.n, self.base = eng, sem, 0, 0

    def __call__(self, ins):
        self.n += 1
        ins.then_inc(self.sem, 1)
        self.eng.wait_ge(self.sem, self.base + self.n)

    def iteration(self, i, per):
        self.base = self.start + i * per
        self.n = 0

    def enter_loop(self):
        self.start = self.base + self.n

    def leave_loop(self, count, per):
        assert self.n == per, (self.n, per)
        self.base, self.n = self.start + count * per, 0


class Ring:

    SLOTS = 8

    def __init__(self, nc, ctx, streams):
        self.w = [ctx.enter_context(nc.sbuf_tensor(f"slab{s}", [P, D], F32)) for s in range(self.SLOTS)]
        self.loaded = [ctx.enter_context(nc.semaphore(f"slab{s}_loaded")) for s in range(self.SLOTS)]
        self.freed = [ctx.enter_context(nc.semaphore(f"slab{s}_freed")) for s in range(self.SLOTS)]
        self.used = [0] * self.SLOTS
        self.streams = streams
        self.at = 0

    def shape(self, n):
        _, _, per, count = self.streams[n]
        ahead = min(per, self.SLOTS)
        return per, count, ahead, per // ahead

    def load(self, sp, slot, n, index):
        _, src, _, _ = self.streams[n]
        ap = src[bass.ds(index, 1)].rearrange("a p n -> p (a n)")
        sp.dma_start(self.w[slot][:], ap).then_inc(self.loaded[slot], 16)

    def first(self, sp, n):
        if n < len(self.streams):
            for s in range(self.shape(n)[2]):
                if self.used[s]:
                    sp.wait_ge(self.freed[s], self.used[s])
                self.load(sp, s, n, s)

    def stream(self, sp, name):
        n = self.at
        assert self.streams[n][0] == name
        per, count, ahead, turns = self.shape(n)

        def follow(i, slabs):
            for u in slabs:
                s = u % ahead
                sp.wait_ge(self.freed[s], self.used[s] + i * turns + u // ahead + 1)
                self.load(sp, s, n, i * per + u + ahead)

        if count > 1:
            with sp.Fori(0, count - 1) as i:
                follow(i, range(per))
        follow(count - 1, range(per - ahead))
        before = list(self.used)
        for s in range(ahead):
            self.used[s] += count * turns
        self.first(sp, n + 1)
        self.used = before

    def slab(self, pe, i, u):
        _, _, ahead, turns = self.shape(self.at)
        s = u % ahead
        pe.wait_ge(self.loaded[s], 16 * (self.used[s] + i * turns + u // ahead + 1))
        return self.w[s], self.freed[s]

    def wait_used(self, eng, i, u):
        _, _, ahead, turns = self.shape(self.at)
        s = u % ahead
        eng.wait_ge(self.freed[s], self.used[s] + i * turns + u // ahead + 1)

    def close(self):
        _, count, ahead, turns = self.shape(self.at)
        for s in range(ahead):
            self.used[s] += count * turns
        self.at += 1


class Core:
    pass


def setup(c, a, ctx):
    nc = c.nc

    def sb(name, shape, dt=F32):
        return ctx.enter_context(nc.sbuf_tensor(name, shape, dt))

    c.ps = ctx.enter_context(nc.psum_tensor("banks", [P, 8, HALF], F32))
    c.const = sb("const", [P, a["const"].shape[1]])
    c.ident = c.const[:, 0:P]
    c.upto = c.const[:, P:2 * P]
    c.since = c.const[:, 2 * P:3 * P]
    c.after = c.const[:, 3 * P:4 * P]
    c.ones = c.const[:, 4 * P:5 * P]
    c.blocks = c.const[:, 5 * P:6 * P]
    c.mask_f = c.const[:, 6 * P:13 * P].rearrange("p (m f) -> p m f", m=LEVELS)
    c.mask_b = c.const[:, 13 * P:20 * P].rearrange("p (m f) -> p m f", m=LEVELS)
    c.eps = c.const[:, 20 * P:20 * P + 1]
    c.eps_k = c.const[:, 20 * P + 1:20 * P + 2]
    c.x = sb("x", [P, TILES, D])
    c.hT = sb("hT", [P, KT, TOK])
    c.cols = sb("cols", [P, a["cols"].shape[1]])
    c.c_act = sb("c_act", [P, 2, KT, 2])
    c.mod = sb("mod", [P, 6, KT, 2])
    c.gain = sb("gain", [P, 2, KT, 2])
    with Stage(c, "setup") as st:
        loads = st.sem("loads")
        act_done = st.sem("act_done")
        with st.block() as block:
            @block.sync
            def _(sp):
                c.ring.first(sp, 0)

            @block.scalar
            def _(act):
                act.dma_start(c.cols[:], a["cols"]).then_inc(loads, 16)
                act.dma_start(c.const[:], a["const"]).then_inc(loads, 16)
                act.dma_start(c.x[:, 0:CTX_TILES, :], a["ctx"].rearrange("a (t p) d -> p (a t) d", p=P)).then_inc(loads, 16)
                act.dma_start(c.x[:, CTX_TILES:, :], a["x"].rearrange("a (t p) d -> p (a t) d", p=P)).then_inc(loads, 16)
                act.wait_ge(loads, 64)
                nc.scalar.activation(c.c_act[:], c.cols[:, 0:32].rearrange("p (b k v) -> p b k v", b=2, v=2), ACT.Silu).then_inc(act_done, 1)
                act.wait_ge(act_done, 1)


def modulation(c, name, which, bias, gains, gate_vectors):
    nc, ring = c.nc, c.ring
    with Stage(c, name) as st:
        cols_ready = st.sem("cols_ready")
        ps = c.ps[:, 0, 0:96]
        with st.block() as block:
            @block.sync
            def _(sp):
                ring.stream(sp, name)

            @block.tensor
            def _(pe):
                with pe.Fori(0, 6) as i:
                    for u in range(8):
                        w, freed = ring.slab(pe, i, u)
                        for k in range(KT):
                            last = nc.tensor.matmul(c.ps[:, 0, bass.ds(i * 16 + 2 * u, 2)], w[:, k * P:(k + 1) * P],
                                                    c.c_act[:, which, k, :], start=k == 0, stop=k == KT - 1)
                        last.then_inc(freed, 1)

            @block.vector
            def _(dve):
                ring.wait_used(dve, 5, 7)
                nc.vector.tensor_tensor(c.mod[:].rearrange("p m k v -> p (m k) v"), ps.rearrange("p (m v) -> p m v", v=2),
                                        bias.unsqueeze(2).to_broadcast([P, 48, 2]), ALU.add).then_inc(cols_ready, 1)
                dve.wait_ge(cols_ready, 1)
                for n, g in enumerate(gains):
                    nc.vector.scalar_tensor_tensor(out=c.gain[:, n], in0=c.mod[:, 3 * n + 1], scalar=1.0,
                                                   in1=g.unsqueeze(2).to_broadcast([P, KT, 2]),
                                                   op0=ALU.add, op1=ALU.mult).then_inc(cols_ready, 1)
                dve.wait_ge(cols_ready, 3)
    ring.close()


def norm_transpose(c, name, n, first):
    nc = c.nc
    tiles = list(range(first, TILES))
    parts = [(t0, t1, v) for t0, t1, v in ((CTX_TILES, TILES, 0), (0, CTX_TILES, 1)) if t0 >= first]
    with Stage(c, name) as st:
        xn = st.sb("xn", [P, TILES, D])
        stat = st.sb("stat", [P, 3, TILES])
        squared, root, scaled = st.sem("squared"), st.sem("root"), st.sem("scaled")
        recip, turned, placed = st.sem("recip"), st.sem("turned"), st.sem("placed")
        with st.block() as block:
            @block.scalar
            def _(act):
                for t in tiles:
                    nc.scalar.activation(xn[:, t, :], c.x[:, t, :], ACT.Square, accum_out=stat[:, 0, t:t + 1]).then_inc(squared, 1)
                act.wait_ge(squared, len(tiles))
                nc.scalar.activation(stat[:, 1, first:], stat[:, 0, first:], ACT.Sqrt, bias=c.eps, scale=1.0 / D).then_inc(root, 1)
                q = 0
                for k in range(KT):
                    for t0, t1, v in parts:
                        act.wait_ge(turned, q + 1)
                        nc.scalar.activation(c.hT[:, k, t0 * P:t1 * P], c.ps[:, q % 8, 0:(t1 - t0) * P], ACT.Identity,
                                             scale=c.gain[:, n, k, v:v + 1], bias=c.mod[:, 3 * n, k, v:v + 1]).then_inc(placed, 1)
                        q += 1
                act.wait_ge(placed, q)

            @block.vector
            def _(dve):
                dve.wait_ge(root, 1)
                nc.vector.reciprocal(stat[:, 2, first:], stat[:, 1, first:]).then_inc(recip, 1)
                dve.wait_ge(recip, 1)
                for t in tiles:
                    nc.vector.tensor_scalar(xn[:, t, :], c.x[:, t, :], stat[:, 2, t:t + 1], None, ALU.mult).then_inc(scaled, 1)

            @block.tensor
            def _(pe):
                pe.wait_ge(scaled, len(tiles))
                q = 0
                for k in range(KT):
                    for t0, t1, v in parts:
                        if q >= 8:
                            pe.wait_ge(placed, q - 7)
                        for t in range(t0, t1):
                            last = nc.tensor.transpose(c.ps[:, q % 8, (t - t0) * P:(t - t0 + 1) * P],
                                                       xn[:, t, k * P:(k + 1) * P], c.ident)
                        last.then_inc(turned, 1)
                        q += 1



def rows_product(c, pe, lhs, tiles, i, u0, kslabs, full, read, reads_before):
    nc, ring = c.nc, c.ring
    for j in range(kslabs):
        w, freed = ring.slab(pe, i, u0 + j)
        for n, t in enumerate(tiles):
            if j == 0 and reads_before is not None:
                pe.wait_ge(read, reads_before + n + 1)
            for kk in range(2):
                last = nc.tensor.matmul(c.ps[:, n, :], lhs(2 * j + kk, t), w[:, kk * HALF:(kk + 1) * HALF],
                                        start=j == 0 and kk == 0, stop=j == kslabs - 1 and kk == 1)
            if n == len(tiles) - 1:
                last.then_inc(freed, 1)
            elif j == kslabs - 1:
                last.then_inc(full, 1)


def wait_bank(c, eng, n, tiles, full, groups_before, i, u_last):
    if n < len(tiles) - 1:
        eng.wait_ge(full, groups_before * (len(tiles) - 1) + n + 1)
    else:
        c.ring.wait_used(eng, i, u_last)


def projection(c, name, l, a, st_out):
    nc, ring = c.nc, c.ring
    tiles = list(range(TILES))
    with Stage(c, name) as st:
        wr = st.sb("wr", [P, KT, 32])
        wr_loaded, full, read, qk_read, r_done = (st.sem(x) for x in ("wr_loaded", "full", "read", "qk_read", "r_done"))
        qk_read_dve, row_set = st.sem("qk_read_dve"), st.sem("row_set")
        with st.block() as block:
            @block.sync
            def _(sp):
                sp.dma_start(wr[:], a["w_r"][l]).then_inc(wr_loaded, 16)
                ring.stream(sp, name)

            @block.tensor
            def _(pe):
                for u in range(4):
                    w, freed = ring.slab(pe, 0, u)
                    if u >= 3:
                        pe.wait_ge(qk_read, u - 2)
                        pe.wait_ge(qk_read_dve, u - 2)
                    b = 2 * (u % 3)
                    for k in range(KT):
                        nc.tensor.matmul(c.ps[:, b, :], w[:, k * P:(k + 1) * P], c.hT[:, k, CTX:], start=k == 0, stop=k == KT - 1)
                    for k in range(KT):
                        last = nc.tensor.matmul(c.ps[:, b + 1, 0:CTX], w[:, k * P:(k + 1) * P], c.hT[:, k, 0:CTX],
                                                start=k == 0, stop=k == KT - 1)
                    last.then_inc(freed, 1)
                pe.wait_ge(wr_loaded, 16)
                for k in range(KT):
                    nc.tensor.matmul(c.ps[0:32, 6, :], wr[:, k, :], c.hT[:, k, CTX:], start=k == 0, stop=k == KT - 1)
                for k in range(KT):
                    last = nc.tensor.matmul(c.ps[0:32, 7, 0:CTX], wr[:, k, :], c.hT[:, k, 0:CTX], start=k == 0, stop=k == KT - 1)
                last.then_inc(r_done, 1)
                pe.wait_ge(qk_read, 4)
                pe.wait_ge(qk_read_dve, 4)
                for g in range(3):
                    rows_product(c, pe, lambda k, t: c.hT[:, k, t * P:(t + 1) * P], tiles, 0, 4 + 4 * g, 4, full, read,
                                 6 * (g - 1) if g else None)

            @block.scalar
            def _(act):
                for u in range(4):
                    ring.wait_used(act, 0, u)
                    nc.scalar.activation(c.gqk[:, u, CTX:], c.ps[:, 2 * (u % 3), :], ACT.Copy,
                                         scale=HD ** -0.5 if u < 2 else 1.0).then_inc(qk_read, 1)
                act.wait_ge(r_done, 1)
                nc.scalar.activation(c.rT[0:32, CTX:], c.ps[0:32, 6, :], ACT.Copy).then_inc(qk_read, 1)
                nc.scalar.activation(c.rT[0:32, 0:CTX], c.ps[0:32, 7, 0:CTX], ACT.Copy).then_inc(qk_read, 1)
                for g in range(3):
                    for n, t in enumerate(tiles):
                        wait_bank(c, act, n, tiles, full, g, 0, 4 + 4 * g + 3)
                        nc.scalar.activation(c.tok[:, t, g * HALF:(g + 1) * HALF], c.ps[:, n, :], ACT.Copy).then_inc(read, 1)
                act.wait_ge(read, 18)
                act.wait_ge(qk_read, 6)

            @block.vector
            def _(dve):
                nc.vector.memset(c.rT[32:33, :], 1.0).then_inc(row_set, 1)
                for u in range(4):
                    ring.wait_used(dve, 0, u)
                    nc.vector.tensor_scalar(c.gqk[:, u, 0:CTX], c.ps[:, 2 * (u % 3) + 1, 0:CTX],
                                            HD ** -0.5 if u < 2 else 1.0, None, ALU.mult).then_inc(qk_read_dve, 1)
                dve.wait_ge(qk_read_dve, 4)
                dve.wait_ge(row_set, 1)
    ring.close()


def pooling(c, name, l, a):
    nc = c.nc
    with Stage(c, name) as st:
        band = st.sb("band", [P, 5, 4, P])
        wp = st.sb("wp", [P, 2, P])
        m = st.sb("m", [P, 2, TOK])
        loads, cleared, means, moved, mixed, scaled = (st.sem(x) for x in ("loads", "cleared", "means", "moved", "mixed", "scaled"))
        with st.block() as block:
            @block.sync
            def _(sp):
                sp.dma_start(band[:], a["band"].rearrange("p (r g f) -> p r g f", r=5, g=4)).then_inc(loads, 16)
                sp.wait_ge(cleared, 1)
                for g in range(4):
                    o = 64 * (g % 2)
                    sp.dma_start(wp[o:o + 64, g // 2, o:o + 64], a["w_pool"][l, g]).then_inc(loads, 16)

            @block.vector
            def _(dve):
                nc.vector.memset(wp[:], 0.0).then_inc(cleared, 1)
                for pair in range(2):
                    for n, (s0, s1) in enumerate(((0, CTX), (CTX, TOK))):
                        dve.wait_ge(mixed, 2 * pair + n + 1)
                        nc.vector.tensor_scalar(c.hT[:, pair, s0:s1], c.ps[:, 4 + 2 * pair + n, 0:s1 - s0],
                                                c.small(l, "s_pool")[:, pair:pair + 1], None, ALU.mult).then_inc(scaled, 1)
                dve.wait_ge(scaled, 4)

            @block.tensor
            def _(pe):
                pe.wait_ge(loads, 80)
                for pair in range(2):
                    for n, (t0, t1) in enumerate(((0, CTX_TILES), (CTX_TILES, TILES))):
                        for gg in range(2):
                            g = 2 * pair + gg
                            for t in range(t0, t1):
                                same = 0 if t == t0 else 2 if t == t1 - 1 else 1
                                terms = [(t, same)] + [(t - 1, 3)] * (t > t0) + [(t + 1, 4)] * (t < t1 - 1)
                                for e, (src, kind) in enumerate(terms):
                                    last = nc.tensor.matmul(c.ps[64 * gg:64 * gg + 64, 2 * pair + n, (t - t0) * P:(t - t0 + 1) * P],
                                                            c.tok[:, src, C_POOL + 64 * g:C_POOL + 64 * g + 64],
                                                            band[:, kind, g, :], start=e == 0, stop=e == len(terms) - 1)
                        last.then_inc(means, 1)
                for pair in range(2):
                    for n, (s0, s1) in enumerate(((0, CTX), (CTX, TOK))):
                        pe.wait_ge(moved, 2 * pair + n + 1)
                        nc.tensor.matmul(c.ps[:, 4 + 2 * pair + n, 0:s1 - s0], wp[:, pair, :], m[:, pair, s0:s1],
                                         start=True, stop=True).then_inc(mixed, 1)

            @block.scalar
            def _(act):
                for pair in range(2):
                    for n, (s0, s1) in enumerate(((0, CTX), (CTX, TOK))):
                        act.wait_ge(means, 2 * pair + n + 1)
                        nc.scalar.activation(m[:, pair, s0:s1], c.ps[:, 2 * pair + n, 0:s1 - s0], ACT.Copy).then_inc(moved, 1)


def gla(c, name, l, a):
    nc = c.nc
    C = TILES
    with Stage(c, name) as st:
        sb, sem = st.sb, st.sem
        wg = sb("wg", [33, 512])
        bT = sb("bT", [P, 4, TOK])
        A = sb("A", [P, C, 4, P])
        qd = sb("qd", [P, 4, TOK])
        r1, r2, r3 = (sb(x, [P, C * 512]) for x in ("r1", "r2", "r3"))
        t0_ = r1[:].rearrange("p (t n) -> p t n", t=C)
        F = r1[:].rearrange("p (b a n) -> p b a n", b=2, a=2)
        kdt = r1[:].rearrange("p (t d f) -> p t d f", t=C, d=4)
        la = r2[:].rearrange("p (t n) -> p t n", t=C)
        E = r2[:, 0:2 * TOK].rearrange("p (a n) -> p a n", a=2)
        Pm = r2[:].rearrange("p (t d f) -> p t d f", t=C, d=4)
        kd = r3[:].rearrange("p (d n) -> p d n", d=4)
        S = r3[:, 0:5 * 512].rearrange("p (c d f) -> p c d f", c=5, d=4)
        o = r2[:, 0:C * 256].rearrange("p (t h e) -> p t h e", t=C, h=4)
        gg = r2[:, C * 256:].rearrange("p (t h e) -> p t h e", t=C, h=4)
        sq = r1[:, 0:C * 256]
        ebl = sb("ebl", [P, 4, C])
        st_ = sb("st", [P, 3, C * GLA_H])
        grow = sb("grow", [P, 64])
        loads, cleared, logits, exps, la_ready, b_full, b_ready = (sem(x) for x in
            ("loads", "cleared", "logits", "exps", "la_ready", "b_full", "b_ready"))
        diff, ee, level_ready, a_full, a_read = (sem(x) for x in ("diff", "ee", "level_ready", "a_full", "a_read"))
        step, decays, kd_ready, kdt_full, kdt_read, s_full, s_ready = (sem(x) for x in
            ("step", "decays", "kd_ready", "kdt_full", "kdt_read", "s_full", "s_ready"))
        o_full, o_read, o_sq, o_root, gated = (sem(x) for x in ("o_full", "o_read", "o_sq", "o_root", "gated"))
        last_col = [P - 1, 0]

        def order(d):
            return [0, 1, 2, 3, 4, 5] if d == 0 else [1, 0, 5, 4, 3, 2]

        with st.block() as block:
            @block.sync
            def _(sp):
                sp.wait_ge(cleared, 1)
                sp.dma_start(wg[0:16, 0:256], a["w_gate"][l, 0]).then_inc(loads, 16)
                sp.dma_start(wg[16:32, 256:512], a["w_gate"][l, 1]).then_inc(loads, 16)
                sp.dma_start(wg[32:33, :], a["b_gate"][l:l + 1].rearrange("a d n -> a (d n)")).then_inc(loads, 16)
                sp.dma_start(grow[:], a["g_gla"][l:l + 1, :].to_broadcast([P, 64])).then_inc(loads, 16)

            @block.tensor
            def _(pe):
                pe.wait_ge(loads, 64)
                for t in range(C):
                    nc.tensor.matmul(c.ps[:, t, :], c.rT[0:33, t * P:(t + 1) * P], wg[:], start=True, stop=True).then_inc(logits, 1)
                for t in range(C):
                    pe.wait_ge(la_ready, t + 1)
                    for dp in range(4):
                        last = nc.tensor.matmul(c.ps[:, t, dp * P:(dp + 1) * P], la[:, t, dp * P:(dp + 1) * P],
                                                c.upto if dp < 2 else c.since, start=True, stop=True)
                    last.then_inc(b_full, 1)
                n = 0
                for lev in range(2 * LEVELS + 1):
                    if lev:
                        pe.wait_ge(level_ready, lev)
                    else:
                        pe.wait_ge(b_ready, C)
                    for t in range(C):
                        if lev:
                            pe.wait_ge(a_read, n - C + 1)
                        for e in range(4):
                            ch, pr = 2 * (t // 2) + e // 2, e % 2
                            r, s = slice(64 * (t % 2), 64 * (t % 2) + 64), slice(ch * P, (ch + 1) * P)
                            if lev:
                                x = F[r, (lev - 1) % 2, pr, s]
                                k_, q_ = x, x
                            else:
                                k_, q_ = c.gqk[r, 2 + pr, s], c.gqk[r, pr, s]
                            last = nc.tensor.matmul(c.ps[:, t, e * P:(e + 1) * P], k_, q_, start=True, stop=True)
                        last.then_inc(a_full, 1)
                        n += 1
                for t in range(C):
                    pe.wait_ge(a_read, n - C + t + 1)
                    pe.wait_ge(kd_ready, t + 1)
                    for dp in range(4):
                        last = nc.tensor.transpose(c.ps[:, t, dp * P:(dp + 1) * P], kd[:, dp, t * P:(t + 1) * P], c.ident)
                    last.then_inc(kdt_full, 1)
                for t in range(C):
                    pe.wait_ge(kdt_read, t + 1)
                    for dp in range(4):
                        last = nc.tensor.matmul(c.ps[:, t, dp * P:(dp + 1) * P], kdt[:, t, dp, :],
                                                c.tok[:, t, C_GV + (dp % 2) * P:C_GV + (dp % 2) * P + P], start=True, stop=True)
                    last.then_inc(s_full, 1)
                pe.wait_ge(s_ready, 1)
                for t in range(C):
                    for p_ in range(2):
                        reg = c.ps[:, t, p_ * P:(p_ + 1) * P]
                        terms = []
                        for d in range(2):
                            at = order(d).index(t)
                            if at:
                                terms.append((qd[:, 2 * d + p_, t * P:(t + 1) * P], S[:, at - 1, 2 * d + p_, :]))
                        for e, (x, y) in enumerate(terms):
                            nc.tensor.matmul(reg, x, y, start=e == 0, stop=e == len(terms) - 1)
                        for hh in range(2):
                            h = 2 * p_ + hh
                            last = nc.tensor.matmul(c.ps[:, t, h * 64:h * 64 + 64], A[:, 2 * (t // 2) + hh, 2 * (t % 2) + p_, :],
                                                    c.tok[:, t, C_GV + 64 * h:C_GV + 64 * h + 64], start=False, stop=True,
                                                    skip_group_check=True)
                    last.then_inc(o_full, 1)

            @block.scalar
            def _(act):
                for t in range(C):
                    act.wait_ge(logits, t + 1)
                    nc.scalar.activation(t0_[:, t, :], c.ps[:, t, :], ACT.Abs).then_inc(exps, 1)
                act.wait_ge(exps, C)
                nc.scalar.activation(t0_, t0_, ACT.Exp, scale=-1.0).then_inc(exps, 1)
                act.wait_ge(exps, C + 1)
                nc.scalar.activation(t0_, t0_, ACT.Ln, bias=1.0).then_inc(exps, 1)
                for t in range(C):
                    act.wait_ge(b_full, t + 1)
                    nc.scalar.activation(bT[:, :, t * P:(t + 1) * P], c.ps[:, t, :].rearrange("p (d f) -> p d f", d=4), ACT.Copy).then_inc(b_ready, 1)
                act.wait_ge(b_ready, C)
                for lev in range(1, 2 * LEVELS + 1):
                    act.wait_ge(diff, lev)
                    nc.scalar.activation(E, E, ACT.Exp).then_inc(ee, 1)
                nc.scalar.activation(qd[:], bT[:], ACT.Exp).then_inc(decays, 1)
                for t in range(C):
                    for dp in range(4):
                        col = t * P + last_col[dp // 2]
                        last = nc.scalar.activation(kd[:, dp, t * P:(t + 1) * P], bT[:, dp, t * P:(t + 1) * P], ACT.Exp,
                                                    scale=-1.0, bias=bT[:, dp, col:col + 1])
                    last.then_inc(decays, 1)
                for d in range(2):
                    bl = bT[:, 2 * d:2 * d + 2, :].rearrange("p d (t f) -> p d t f", f=P)[:, :, :, last_col[d]]
                    nc.scalar.activation(ebl[:, 2 * d:2 * d + 2, :], bl, ACT.Exp).then_inc(decays, 1)
                for t in range(C):
                    act.wait_ge(kdt_full, t + 1)
                    nc.scalar.activation(kdt[:, t], c.ps[:, t, :].rearrange("p (d f) -> p d f", d=4), ACT.Copy).then_inc(kdt_read, 1)
                for t in range(C):
                    act.wait_ge(o_full, t + 1)
                    nc.scalar.activation(o[:, t].rearrange("p h e -> p (h e)"), c.ps[:, t, 0:256], ACT.Copy).then_inc(o_read, 1)
                act.wait_ge(o_read, C)
                nc.scalar.activation(sq, r2[:, 0:C * 256], ACT.Square).then_inc(o_sq, 1)
                nc.scalar.activation(gg, c.tok[:, :, C_GG:C_GG + 256].rearrange("p t (h e) -> p t h e", h=4), ACT.Silu).then_inc(o_sq, 1)
                act.wait_ge(gated, 1)
                nc.scalar.activation(st_[:, 1, :], st_[:, 0, :], ACT.Sqrt, bias=c.eps, scale=1.0 / 64).then_inc(o_root, 1)

            @block.vector
            def _(dve):
                link = Chain(dve, step)
                nc.vector.memset(wg[:], 0.0).then_inc(cleared, 1)
                dve.wait_ge(exps, C + 2)
                for t in range(C):
                    link(nc.vector.scalar_tensor_tensor(out=la[:, t, :], in0=c.ps[:, t, :], scalar=0.0, in1=t0_[:, t, :],
                                                        op0=ALU.min, op1=ALU.subtract))
                    nc.vector.tensor_scalar(la[:, t, :], la[:, t, :], 1.0 / 16, None, ALU.mult).then_inc(la_ready, 1)
                n = 0
                for t in range(C):
                    dve.wait_ge(a_full, t + 1)
                    nc.vector.tensor_tensor(A[:, t], c.ps[:, t, :].rearrange("p (h f) -> p h f", h=4),
                                            c.ident.unsqueeze(1).to_broadcast([P, 4, P]), ALU.mult).then_inc(a_read, 1)
                    n += 1
                dve.wait_ge(b_ready, C)
                for lev in range(1, 2 * LEVELS + 1):
                    d, m = (lev - 1) // LEVELS, 1 << ((lev - 1) % LEVELS)
                    blk = lambda x: x.rearrange("p a (b f) -> p a b f", f=2 * m)
                    b_, E_ = blk(bT[:, 2 * d:2 * d + 2, :]), blk(E)
                    Fl = F[:, (lev - 1) % 2]
                    F_ = blk(Fl)
                    nb = TOK // (2 * m)
                    if lev > 1:
                        dve.wait_ge(level_ready, lev - 1)
                    edge = m - 1 if d == 0 else m
                    for pr in range(2):
                        ref = b_[:, pr, :, edge:edge + 1].to_broadcast([P, nb, m])
                        lo, hi = b_[:, pr, :, 0:m], b_[:, pr, :, m:2 * m]
                        if d == 0:
                            nc.vector.tensor_tensor(E_[:, pr, :, 0:m], ref, lo, ALU.subtract)
                            last = nc.vector.tensor_tensor(E_[:, pr, :, m:2 * m], hi, ref, ALU.subtract)
                        else:
                            nc.vector.tensor_tensor(E_[:, pr, :, 0:m], lo, ref, ALU.subtract)
                            last = nc.vector.tensor_tensor(E_[:, pr, :, m:2 * m], ref, hi, ALU.subtract)
                    last.then_inc(diff, 1)
                    dve.wait_ge(ee, lev)
                    if lev > 2:
                        dve.wait_ge(a_full, C * (lev - 1))
                    q_, k_ = blk(c.gqk[:, 0:2, :]), blk(c.gqk[:, 2:4, :])
                    lo_src, hi_src = (k_, q_) if d == 0 else (q_, k_)
                    for pr in range(2):
                        nc.vector.tensor_tensor(F_[:, pr, :, 0:m], lo_src[:, pr, :, 0:m], E_[:, pr, :, 0:m], ALU.mult)
                        last = nc.vector.tensor_tensor(F_[:, pr, :, m:2 * m], hi_src[:, pr, :, m:2 * m], E_[:, pr, :, m:2 * m], ALU.mult)
                    last.then_inc(level_ready, 1)
                    mask = (c.mask_f if d == 0 else c.mask_b)[:, (lev - 1) % LEVELS, :]
                    for t in range(C):
                        dve.wait_ge(a_full, C * lev + t + 1)
                        nc.vector.copy_predicated(A[:, t], mask.bitcast(U32).unsqueeze(1).to_broadcast([P, 4, P]),
                                                  c.ps[:, t, :].rearrange("p (h f) -> p h f", h=4)).then_inc(a_read, 1)
                        n += 1
                dve.wait_ge(a_read, n)
                dve.wait_ge(decays, 1)
                for d in range(2):
                    last = nc.vector.tensor_tensor(qd[:, 2 * d:2 * d + 2, :], qd[:, 2 * d:2 * d + 2, :], c.gqk[:, 0:2, :], ALU.mult)
                link(last)
                for t in range(C):
                    dve.wait_ge(decays, t + 2)
                    s = slice(t * P, (t + 1) * P)
                    for d in range(2):
                        last = nc.vector.tensor_tensor(kd[:, 2 * d:2 * d + 2, s], kd[:, 2 * d:2 * d + 2, s], c.gqk[:, 2:4, s], ALU.mult)
                    last.then_inc(kd_ready, 1)
                for t in range(C):
                    dve.wait_ge(s_full, t + 1)
                    last = nc.vector.tensor_tensor(Pm[:, t], c.ps[:, t, :].rearrange("p (d f) -> p d f", d=4),
                                                   c.blocks.unsqueeze(1).to_broadcast([P, 4, P]), ALU.mult)
                link(last)
                dve.wait_ge(decays, C + 3)
                for at in range(5):
                    for d in range(2):
                        ch = order(d)[at]
                        for pr in range(2):
                            dp = 2 * d + pr
                            if at == 0:
                                last = nc.vector.tensor_copy(S[:, 0, dp, :], Pm[:, ch, dp, :])
                            else:
                                last = nc.vector.scalar_tensor_tensor(out=S[:, at, dp, :], in0=S[:, at - 1, dp, :],
                                                                      scalar=ebl[:, dp, ch:ch + 1], in1=Pm[:, ch, dp, :],
                                                                      op0=ALU.mult, op1=ALU.add)
                    if at < 4:
                        link(last)
                    else:
                        last.then_inc(s_ready, 1)
                dve.wait_ge(o_sq, 1)
                nc.vector.tensor_reduce(st_[:, 0, :], sq.rearrange("p (n e) -> p n e", e=64), AX, ALU.add).then_inc(gated, 1)
                dve.wait_ge(o_root, 1)
                link(nc.vector.reciprocal(st_[:, 2, :], st_[:, 1, :]))
                dve.wait_ge(o_sq, 2)
                link(nc.vector.tensor_tensor(o.rearrange("p t h e -> p (t h) e"), o.rearrange("p t h e -> p (t h) e"),
                                             st_[:, 2, :].unsqueeze(2).to_broadcast([P, C * 4, 64]), ALU.mult))
                link(nc.vector.tensor_tensor(o.rearrange("p t h e -> p (t h) e"), o.rearrange("p t h e -> p (t h) e"),
                                             gg.rearrange("p t h e -> p (t h) e"), ALU.mult))
                link(nc.vector.tensor_tensor(c.tok[:, :, 0:256].rearrange("p t (h e) -> p t h e", h=4), o,
                                             grow[:].unsqueeze(1).unsqueeze(1).to_broadcast([P, C, 4, 64]), ALU.mult))


def attention(c, name, l, a, update_ctx):
    nc = c.nc
    first = 0 if update_ctx else CTX_TILES
    nqk = 10
    C = TILES
    units = [(h, t) for t in range(first, C) for h in range(HEADS_Q)]
    with Stage(c, name) as st:
        sb, sem = st.sb, st.sem
        sq = sb("sq", [P, C, nqk * HD])
        stat = sb("stat", [P, 3, C * nqk])
        grow = sb("grow", [P, nqk, HD])
        rope = sb("rope", [P, 2, LAT_TILES, 32])
        rot = sb("rot", [P, 2, nqk, 2, 16])
        kdup = sb("kdup", [P, C, 4, HD])
        qkT = sb("qkT", [P, 6, TOK])
        p_ = sb("p", [P, 2, TOK])
        pT = sb("pT", [P, 2, TOK])
        sm = sb("sm", [P, 4, len(units)])
        loads, squared, root, step, qk_ready, turned, placed = (sem(x) for x in
            ("loads", "squared", "root", "step", "qk_ready", "turned", "placed"))
        scored, maxed, exped, p_turned, pT_ready, o_full, o_read, summed = (sem(x) for x in
            ("scored", "maxed", "exped", "p_turned", "pT_ready", "o_full", "o_read", "summed"))
        x = c.tok[:, :, C_AQ:C_AQ + nqk * HD]

        def keys(t):
            return CTX_TILES if t < CTX_TILES else TILES

        def unit_out(dve, n, link):
            h, t = units[n]
            link(nc.vector.reciprocal(sm[:, 3, n:n + 1], sm[:, 2, n:n + 1]))
            dve.wait_ge(o_full, n + 1)
            nc.vector.tensor_scalar(c.tok[:, t, C_AQ + h * HD:C_AQ + (h + 1) * HD], c.ps[:, 5 + 2 * (n % 2), 256:256 + HD],
                                    sm[:, 3, n:n + 1], None, ALU.mult).then_inc(o_read, 1)

        with st.block() as block:
            @block.sync
            def _(sp):
                sp.dma_start(grow[:, 0:8, :], a["g_q"][l:l + 1, :].unsqueeze(1).to_broadcast([P, 8, HD])).then_inc(loads, 16)
                sp.dma_start(grow[:, 8:10, :], a["g_k"][l:l + 1, :].unsqueeze(1).to_broadcast([P, 2, HD])).then_inc(loads, 16)
                sp.dma_start(rope[:], a["rope"].rearrange("p (s t f) -> p s t f", s=2, t=LAT_TILES)).then_inc(loads, 16)

            @block.scalar
            def _(act):
                nc.scalar.activation(sq[:], x, ACT.Square).then_inc(squared, 1)
                act.wait_ge(summed, 1)
                nc.scalar.activation(stat[:, 1, :], stat[:, 0, :], ACT.Sqrt, bias=c.eps, scale=1.0 / HD).then_inc(root, 1)
                n = 0
                for t in range(C):
                    for half in range(2):
                        act.wait_ge(turned, n + 1)
                        nc.scalar.activation(qkT[:, 3 * half:3 * half + 3, t * P:(t + 1) * P],
                                             c.ps[:, n % 8, 0:3 * P].rearrange("p (d f) -> p d f", d=3), ACT.Copy).then_inc(placed, 1)
                        n += 1
                for n, (h, t) in enumerate(units):
                    nk = keys(t)
                    act.wait_ge(maxed, 2 * n + 2)
                    if n >= 2:
                        act.wait_ge(p_turned, n - 1)
                    nc.scalar.activation(p_[:, n % 2, 0:nk * P], c.ps[:, 2 * (n % 2):2 * (n % 2) + 2, :].rearrange("p b f -> p (b f)")[:, 0:nk * P],
                                         ACT.Exp, bias=sm[:, 1, n:n + 1], scale=HD ** -0.5, accum_out=sm[:, 2, n:n + 1]).then_inc(exped, 1)

            @block.vector
            def _(dve):
                link = Chain(dve, step)
                dve.wait_ge(squared, 1)
                nc.vector.tensor_reduce(stat[:, 0, :], sq[:].rearrange("p t (h e) -> p (t h) e", e=HD), AX, ALU.add).then_inc(summed, 1)
                dve.wait_ge(root, 1)
                link(nc.vector.reciprocal(stat[:, 2, :], stat[:, 1, :]))
                dve.wait_ge(loads, 48)
                for t in range(C):
                    last = nc.vector.tensor_tensor(x[:, t].rearrange("p (h e) -> p h e", e=HD), x[:, t].rearrange("p (h e) -> p h e", e=HD),
                                                   stat[:, 2, t * nqk:(t + 1) * nqk].unsqueeze(2).to_broadcast([P, nqk, HD]), ALU.mult)
                link(last)
                for t in range(C):
                    last = nc.vector.tensor_tensor(x[:, t].rearrange("p (h e) -> p h e", e=HD), x[:, t].rearrange("p (h e) -> p h e", e=HD),
                                                   grow[:], ALU.mult)
                link(last)
                for t in range(CTX_TILES, C):
                    xv = x[:, t].rearrange("p (h r s f) -> p h r s f", h=nqk, r=2, s=2)
                    x1, x2 = xv[:, :, :, 0, :], xv[:, :, :, 1, :]
                    cs, sn = (rope[:, j, t - CTX_TILES, :].rearrange("p (r f) -> p r f", r=2).unsqueeze(1).to_broadcast([P, nqk, 2, 16])
                              for j in range(2))
                    nc.vector.tensor_tensor(rot[:, 0], x1, sn, ALU.mult)
                    link(nc.vector.tensor_tensor(rot[:, 1], x2, sn, ALU.mult))
                    nc.vector.tensor_tensor(x1, x1, cs, ALU.mult)
                    link(nc.vector.tensor_tensor(x2, x2, cs, ALU.mult))
                    nc.vector.tensor_tensor(x1, x1, rot[:, 1], ALU.subtract)
                    link(nc.vector.tensor_tensor(x2, x2, rot[:, 0], ALU.add))
                for j in range(4):
                    last = nc.vector.tensor_copy(kdup[:, :, j, :], c.tok[:, :, C_AK + HD * (j // 2):C_AK + HD * (j // 2) + HD])
                last.then_inc(qk_ready, 1)
                for n, (h, t) in enumerate(units):
                    nk = keys(t)
                    dve.wait_ge(scored, n + 1)
                    nc.vector.reduce_max(sm[:, 0, n:n + 1], c.ps[:, 2 * (n % 2):2 * (n % 2) + 2, :].rearrange("p b f -> p (b f)")[:, 0:nk * P], AX).then_inc(maxed, 1)
                    dve.wait_ge(maxed, 2 * n + 1)
                    nc.vector.tensor_scalar(sm[:, 1, n:n + 1], sm[:, 0, n:n + 1], -(HD ** -0.5), None, ALU.mult).then_inc(maxed, 1)
                    if n >= 1:
                        unit_out(dve, n - 1, link)
                    dve.wait_ge(p_turned, n + 1)
                    if n >= 2:
                        dve.wait_ge(o_full, n - 1)
                    nc.vector.tensor_copy(pT[:, n % 2, 0:nk * P], c.ps[:, 4 + 2 * (n % 2):6 + 2 * (n % 2), :].rearrange("p b f -> p (b f)")[:, 0:nk * P]).then_inc(pT_ready, 1)
                unit_out(dve, len(units) - 1, link)

            @block.tensor
            def _(pe):
                pe.wait_ge(qk_ready, 1)
                n = 0
                for t in range(C):
                    src = [c.tok[:, t, C_AQ + P * j:C_AQ + P * j + P] for j in range(4)] + \
                          [kdup[:, t, 2 * j:2 * j + 2, :].rearrange("p d e -> p (d e)") for j in range(2)]
                    for half in range(2):
                        if n >= 8:
                            pe.wait_ge(placed, n - 7)
                        for j in range(3):
                            last = nc.tensor.transpose(c.ps[:, n % 8, j * P:(j + 1) * P], src[3 * half + j], c.ident)
                        last.then_inc(turned, 1)
                        n += 1
                pe.wait_ge(placed, 2 * C)

                def scores(n):
                    h, t = units[n]
                    r = slice(64 * (h % 2), 64 * (h % 2) + 64)
                    if n >= 2:
                        pe.wait_ge(exped, n - 1)
                    q = qkT[r, h // 2, t * P:(t + 1) * P]
                    for b, (s0, s1) in enumerate(((0, HALF), (HALF, TOK)) if keys(t) == TILES else ((0, CTX),)):
                        last = nc.tensor.matmul(c.ps[:, 2 * (n % 2) + b, 0:s1 - s0], q, qkT[r, 4 + h // 4, s0:s1], start=True, stop=True)
                    last.then_inc(scored, 1)

                scores(0)
                for n, (h, t) in enumerate(units):
                    if n + 1 < len(units):
                        scores(n + 1)
                    pe.wait_ge(exped, n + 1)
                    if n >= 2:
                        pe.wait_ge(o_read, n - 1)
                    b = 4 + 2 * (n % 2)
                    for s in range(keys(t)):
                        last = nc.tensor.transpose(c.ps[:, b + s // 4, (s % 4) * P:(s % 4 + 1) * P], p_[:, n % 2, s * P:(s + 1) * P], c.ident)
                    last.then_inc(p_turned, 1)
                    pe.wait_ge(pT_ready, n + 1)
                    v = C_AV + HD * (h // 4)
                    for s in range(keys(t)):
                        last = nc.tensor.matmul(c.ps[:, b + 1, 256:256 + HD], pT[:, n % 2, s * P:(s + 1) * P],
                                                c.tok[:, s, v:v + HD], start=s == 0, stop=s == keys(t) - 1)
                    last.then_inc(o_full, 1)


def turn_heads(c, name, first):
    nc = c.nc
    with Stage(c, name) as st:
        turned, placed = st.sem("turned"), st.sem("placed")
        cols = [0, P] + [C_AQ + P * j for j in range(4)]
        units = [(k, t0, t1) for k in range(6) for t0, t1 in ((CTX_TILES, TILES), (0, CTX_TILES)) if t0 >= first]
        with st.block() as block:
            @block.tensor
            def _(pe):
                for n, (k, t0, t1) in enumerate(units):
                    if n >= 8:
                        pe.wait_ge(placed, n - 7)
                    for t in range(t0, t1):
                        last = nc.tensor.transpose(c.ps[:, n % 8, (t - t0) * P:(t - t0 + 1) * P], c.tok[:, t, cols[k]:cols[k] + P], c.ident)
                    last.then_inc(turned, 1)

            @block.scalar
            def _(act):
                for n, (k, t0, t1) in enumerate(units):
                    act.wait_ge(turned, n + 1)
                    nc.scalar.activation(c.hT[:, 2 + k, t0 * P:t1 * P], c.ps[:, n % 8, 0:(t1 - t0) * P], ACT.Copy).then_inc(placed, 1)
                act.wait_ge(placed, len(units))


def out_product(c, name, first, y, lhs=None):
    nc, ring = c.nc, c.ring
    tiles = list(range(first, TILES))
    with Stage(c, name) as st:
        full, read = st.sem("full"), st.sem("read")
        with st.block() as block:
            @block.sync
            def _(sp):
                ring.stream(sp, name)

            @block.tensor
            def _(pe):
                for h in range(2):
                    rows_product(c, pe, lhs or (lambda k, t: c.hT[:, k, t * P:(t + 1) * P]), tiles, 0, 4 * h, 4, full, read, 0 if h else None)

            @block.scalar
            def _(act):
                for h in range(2):
                    for n, t in enumerate(tiles):
                        wait_bank(c, act, n, tiles, full, h, 0, 4 * h + 3)
                        nc.scalar.activation(y[:, t, h * HALF:(h + 1) * HALF], c.ps[:, n, :], ACT.Copy).then_inc(read, 1)
                act.wait_ge(read, 2 * len(tiles))
    ring.close()


def residual(c, name, m, first, y, post=None):
    nc = c.nc
    tiles = list(range(first, TILES))
    vectors = 2 if first == 0 else 1
    with Stage(c, name) as st:
        diag = st.sb("diag", [P, vectors, KT, P])
        gate = st.sb("gate", [P, vectors, D])
        stat = st.sb("stat", [P, 3, TILES])
        sq = st.sb("sq", [P, D])
        diag_ready, rows_ready, copied, step = (st.sem(s) for s in ("diag_ready", "rows_ready", "copied", "step"))
        squared, root, loads = st.sem("squared"), st.sem("root"), st.sem("loads")
        if post is not None:
            row = st.sb("row", [P, D])
        with st.block() as block:
            if post is not None:
                @block.sync
                def _(sp):
                    sp.dma_start(row[:], post.to_broadcast([P, D])).then_inc(loads, 16)

            @block.vector
            def _(dve):
                link = Chain(dve, step)
                for v in range(vectors):
                    nc.vector.tensor_tensor(diag[:, v], c.ident.unsqueeze(1).to_broadcast([P, KT, P]),
                                            c.mod[:, m, :, v:v + 1].to_broadcast([P, KT, P]), ALU.mult).then_inc(diag_ready, 1)
                if post is not None:
                    dve.wait_ge(root, 1)
                    link(nc.vector.reciprocal(stat[:, 2, first:], stat[:, 1, first:]))
                    for t in tiles:
                        last = nc.vector.tensor_scalar(y[:, t, :], y[:, t, :], stat[:, 2, t:t + 1], None, ALU.mult)
                    link(last)
                    dve.wait_ge(loads, 16)
                    for t in tiles:
                        last = nc.vector.tensor_tensor(y[:, t, :], y[:, t, :], row[:], ALU.mult)
                    link(last)
                dve.wait_ge(copied, vectors)
                for t in tiles:
                    last = nc.vector.tensor_tensor(y[:, t, :], y[:, t, :], gate[:, 1 if t < CTX_TILES else 0, :], ALU.mult)
                link(last)
                for t in tiles:
                    last = nc.vector.tensor_tensor(c.x[:, t, :], c.x[:, t, :], y[:, t, :], ALU.add)
                link(last)

            @block.tensor
            def _(pe):
                for v in range(vectors):
                    pe.wait_ge(diag_ready, v + 1)
                    for h in range(2):
                        nc.tensor.matmul(c.ps[:, 2 * v + h, :], c.ones, diag[:, v, 4 * h:4 * h + 4, :].rearrange("p k f -> p (k f)"),
                                         start=True, stop=True).then_inc(rows_ready, 1)

            @block.scalar
            def _(act):
                if post is not None:
                    for n, t in enumerate(tiles):
                        if n:
                            act.wait_ge(squared, n)
                        nc.scalar.activation(sq[:], y[:, t, :], ACT.Square, accum_out=stat[:, 0, t:t + 1]).then_inc(squared, 1)
                    act.wait_ge(squared, len(tiles))
                    nc.scalar.activation(stat[:, 1, first:], stat[:, 0, first:], ACT.Sqrt, bias=c.eps, scale=1.0 / D).then_inc(root, 1)
                for v in range(vectors):
                    act.wait_ge(rows_ready, 2 * v + 2)
                    nc.scalar.activation(gate[:, v, :], c.ps[:, 2 * v:2 * v + 2, :].rearrange("p b f -> p (b f)"), ACT.Copy).then_inc(copied, 1)


def mlp(c, name, first, y):
    nc, ring = c.nc, c.ring
    tiles = list(range(first, TILES))
    nt = len(tiles)
    s0 = first * P
    with Stage(c, name) as st:
        hid = st.sb("hid", [P, 8, TOK])
        tmp = st.sb("tmp", [P, 2, TOK])
        rel, hid_ready, full, read, cleared = (st.sem(s) for s in ("rel", "hid_ready", "full", "read", "cleared"))
        pairs = [6, 4]
        with st.block() as block:
            @block.sync
            def _(sp):
                ring.stream(sp, name)

            @block.tensor
            def _(pe):
                with pe.Fori(0, PASSES) as i:
                    for u in range(8):
                        w, freed = ring.slab(pe, i, u)
                        b = pairs[u % 2]
                        if u == 1:
                            pe.wait_ge(read, i * 2 * nt)
                        if u >= 2:
                            pe.wait_ge(rel, i * 8 + u - 1)
                        elif u == 0:
                            pe.wait_ge(rel, i * 8)
                        for k in range(KT):
                            last = nc.tensor.matmul(c.ps[:, b, :], w[:, k * P:(k + 1) * P], c.hT[:, k, CTX:], start=k == 0, stop=k == KT - 1)
                        if first == 0:
                            for k in range(KT):
                                last = nc.tensor.matmul(c.ps[:, b + 1, 0:CTX], w[:, k * P:(k + 1) * P], c.hT[:, k, 0:CTX],
                                                        start=k == 0, stop=k == KT - 1)
                        last.then_inc(freed, 1)
                    pe.wait_ge(rel, i * 8 + 8)
                    pe.wait_ge(hid_ready, i * 8 + 8)
                    for h in range(2):
                        for j in range(4):
                            u = 8 + 4 * h + j
                            w, freed = ring.slab(pe, i, u)
                            for n, t in enumerate(tiles):
                                if j == 0:
                                    pe.wait_ge(read, i * 2 * nt + (n + 1 if h else 0))
                                for kk in range(2):
                                    last = nc.tensor.matmul(c.ps[:, n, :], hid[:, 2 * j + kk, t * P:(t + 1) * P],
                                                            w[:, kk * HALF:(kk + 1) * HALF], start=j == 0 and kk == 0, stop=j == 3 and kk == 1)
                                if n == nt - 1:
                                    last.then_inc(freed, 1)
                                elif j == 3:
                                    last.then_inc(full, 1)

            @block.scalar
            def _(act):
                with act.Fori(0, PASSES) as i:
                    for u in range(8):
                        b = pairs[u % 2]
                        ring.wait_used(act, i, u)
                        if u >= 2:
                            act.wait_ge(hid_ready, i * 8 + u - 1)
                        else:
                            act.wait_ge(hid_ready, i * 8)
                        if first == 0:
                            nc.scalar.activation(tmp[:, u % 2, :], c.ps[:, b:b + 2, :].rearrange("p b f -> p (b f)")[:, 0:TOK], ACT.Relu).then_inc(rel, 1)
                        else:
                            nc.scalar.activation(tmp[:, u % 2, 0:LAT], c.ps[:, b, :], ACT.Relu).then_inc(rel, 1)

            @block.gpsimd
            def _(pool):
                with pool.Fori(0, PASSES) as i:
                    for u in range(8):
                        pool.wait_ge(rel, i * 8 + u + 1)
                        if u == 0:
                            ring.wait_used(pool, i - 1, 15)
                        if first == 0:
                            nc.gpsimd.tensor_tensor(hid[:, u, 0:CTX], tmp[:, u % 2, LAT:], tmp[:, u % 2, LAT:], ALU.mult)
                        nc.gpsimd.tensor_tensor(hid[:, u, CTX:], tmp[:, u % 2, 0:LAT], tmp[:, u % 2, 0:LAT], ALU.mult).then_inc(hid_ready, 1)

            @block.vector
            def _(dve):
                nc.vector.memset(y[:, first:, :], 0.0).then_inc(cleared, 1)
                dve.wait_ge(cleared, 1)
                with dve.Fori(0, PASSES) as i:
                    dve.wait_ge(read, i * 2 * nt)
                    for h in range(2):
                        for n, t in enumerate(tiles):
                            if n < nt - 1:
                                dve.wait_ge(full, i * 2 * (nt - 1) + h * (nt - 1) + n + 1)
                            else:
                                ring.wait_used(dve, i, 8 + 4 * h + 3)
                            nc.vector.tensor_tensor(y[:, t, h * HALF:(h + 1) * HALF], y[:, t, h * HALF:(h + 1) * HALF],
                                                    c.ps[:, n, :], ALU.add).then_inc(read, 1)
                dve.wait_ge(read, PASSES * 2 * nt)
    ring.close()


def first_layer(c, a, l, update_ctx):
    first = 0 if update_ctx else CTX_TILES
    nc = c.nc
    with ExitStack() as held:
        c.tok = held.enter_context(nc.sbuf_tensor(f"tok{l}", [P, TILES, 1536], F32))
        c.gqk = held.enter_context(nc.sbuf_tensor(f"gqk{l}", [P, 4, TOK], F32))
        c.rT = held.enter_context(nc.sbuf_tensor(f"rT{l}", [33, TOK], F32))
        modulation(c, f"mod{l}", 0, c.small(l, "b_mod"), [c.small(l, "g_mix"), c.small(l, "g_mlp")], 2)
        norm_transpose(c, f"norm{l}", 0, 0)
        projection(c, f"proj{l}", l, a, None)
        pooling(c, f"pool{l}", l, a)
        gla(c, f"gla{l}", l, a)
        attention(c, f"attn{l}", l, a, update_ctx)
        turn_heads(c, f"turn{l}", first)
    with ExitStack() as held:
        y = held.enter_context(nc.sbuf_tensor(f"y{l}", [P, TILES, D], F32))
        out_product(c, f"out{l}", first, y)
        residual(c, f"res{l}", 2, first, y)
        norm_transpose(c, f"norm_mlp{l}", 1, first)
        mlp(c, f"mlp{l}", first, y)
        residual(c, f"res_mlp{l}", 5, first, y)


def final_norm(c, name, a):
    nc = c.nc
    first = CTX_TILES
    with Stage(c, name) as st:
        g = st.sb("g", [P, D])
        sq = st.sb("sq", [P, D])
        stat = st.sb("stat", [P, 3, TILES])
        loads, squared, root, step = (st.sem(x) for x in ("loads", "squared", "root", "step"))
        with st.block() as block:
            @block.sync
            def _(sp):
                sp.dma_start(g[:], a["g_final"].unsqueeze(0).to_broadcast([P, D])).then_inc(loads, 16)

            @block.scalar
            def _(act):
                for n, t in enumerate(range(first, TILES)):
                    if n:
                        act.wait_ge(squared, n)
                    nc.scalar.activation(sq[:], c.x[:, t, :], ACT.Square, accum_out=stat[:, 0, t:t + 1]).then_inc(squared, 1)
                act.wait_ge(squared, TILES - first)
                nc.scalar.activation(stat[:, 1, first:], stat[:, 0, first:], ACT.Sqrt, bias=c.eps, scale=1.0 / D).then_inc(root, 1)

            @block.vector
            def _(dve):
                link = Chain(dve, step)
                dve.wait_ge(root, 1)
                link(nc.vector.reciprocal(stat[:, 2, first:], stat[:, 1, first:]))
                dve.wait_ge(loads, 16)
                for t in range(first, TILES):
                    last = nc.vector.scalar_tensor_tensor(out=c.x[:, t, :], in0=c.x[:, t, :], scalar=stat[:, 2, t:t + 1],
                                                          in1=g[:], op0=ALU.mult, op1=ALU.mult)
                link(last)


R_LOG, R_IN, R_OUT, R_LAST, R_STEP, R_STEP_OUT, R_SKIP = range(7)
SSM_H, GDN_H = 32, 16
NH = SSM_H + GDN_H


def rates(c, name, a):
    nc = c.nc
    T4 = LAT_TILES
    with Stage(c, name) as st:
        sb, sem = st.sb, st.sem
        ws = sb("ws", [P, KT, 64])
        bias = sb("bias", [P, NH])
        alog = sb("alog", [P, NH])
        raw = sb("raw", [P, T4, 64])
        u = sb("u", [P, T4, NH])
        v = sb("v", [P, T4, NH])
        w = sb("w", [P, T4, NH])
        e = sb("e", [P, T4, 16])
        loads, full, taken, summed, soft, ready, cums, step = (sem(x) for x in
            ("loads", "full", "taken", "summed", "soft", "ready", "cums", "step"))
        R = c.rates
        with st.block() as block:
            @block.sync
            def _(sp):
                sp.dma_start(ws[:], a["w_rates"]).then_inc(loads, 16)
                sp.dma_start(bias[:, 0:SSM_H], a["ssm_dt_bias_2"].to_broadcast([P, SSM_H])).then_inc(loads, 16)
                sp.dma_start(bias[:, SSM_H:], a["gdn_dt_bias_2"].to_broadcast([P, GDN_H])).then_inc(loads, 16)
                sp.dma_start(alog[:, 0:SSM_H], a["ssm_A_log_2"].to_broadcast([P, SSM_H])).then_inc(loads, 16)
                sp.dma_start(alog[:, SSM_H:], a["gdn_A_log_2"].to_broadcast([P, GDN_H])).then_inc(loads, 16)
                sp.dma_start(R[:, R_SKIP, :, 0:SSM_H], a["ssm_D_2"].unsqueeze(1).to_broadcast([P, T4, SSM_H])).then_inc(loads, 16)

            @block.tensor
            def _(pe):
                pe.wait_ge(loads, 96)
                for t in range(T4):
                    for k in range(KT):
                        last = nc.tensor.matmul(c.ps[:, 0, t * 64:(t + 1) * 64], c.hT[:, k, CTX + t * P:CTX + (t + 1) * P], ws[:, k, :],
                                                start=k == 0, stop=k == KT - 1)
                last.then_inc(full, 1)
                pe.wait_ge(ready, 1)
                for n, m in enumerate((c.upto, c.after, c.ones)):
                    for t in range(T4):
                        last = nc.tensor.matmul(c.ps[:, 1 + n, t * NH:(t + 1) * NH], m, R[:, R_LOG, t, :], start=True, stop=True)
                    last.then_inc(cums, 1)

            @block.scalar
            def _(act):
                act.wait_ge(full, 1)
                nc.scalar.activation(raw[:], c.ps[:, 0, 0:T4 * 64].rearrange("p (t n) -> p t n", t=T4), ACT.Copy).then_inc(taken, 1)
                act.wait_ge(loads, 96)
                nc.scalar.activation(alog[:], alog[:], ACT.Exp).then_inc(taken, 1)
                act.wait_ge(taken, 1)
                nc.scalar.activation(e[:], raw[:, :, 32:48], ACT.Exp, scale=-1.0).then_inc(taken, 1)
                act.wait_ge(summed, 1)
                nc.scalar.activation(v[:], u[:], ACT.Abs).then_inc(soft, 1)
                act.wait_ge(soft, 1)
                nc.scalar.activation(v[:], v[:], ACT.Exp, scale=-1.0).then_inc(soft, 1)
                act.wait_ge(soft, 2)
                nc.scalar.activation(v[:], v[:], ACT.Ln, bias=1.0).then_inc(soft, 1)
                for n, k in enumerate((R_IN, R_OUT, R_LAST)):
                    act.wait_ge(cums, n + 1)
                    nc.scalar.activation(R[:, k], c.ps[:, 1 + n, 0:T4 * NH].rearrange("p (t n) -> p t n", t=T4), ACT.Exp).then_inc(soft, 1)

            @block.vector
            def _(dve):
                link = Chain(dve, step)
                dve.wait_ge(taken, 1)
                nc.vector.tensor_tensor(u[:, :, 0:SSM_H], raw[:, :, 0:SSM_H], bias[:, 0:SSM_H].unsqueeze(1).to_broadcast([P, T4, SSM_H]), ALU.add)
                nc.vector.tensor_tensor(u[:, :, SSM_H:], raw[:, :, 48:64], bias[:, SSM_H:].unsqueeze(1).to_broadcast([P, T4, GDN_H]), ALU.add).then_inc(summed, 1)
                dve.wait_ge(soft, 3)
                link(nc.vector.scalar_tensor_tensor(out=w[:], in0=u[:], scalar=0.0, in1=v[:], op0=ALU.max, op1=ALU.add))
                dve.wait_ge(taken, 3)
                nc.vector.tensor_copy(R[:, R_STEP, :, 0:SSM_H], w[:, :, 0:SSM_H])
                nc.vector.scalar_tensor_tensor(out=R[:, R_LOG], in0=w[:], scalar=-1.0, in1=alog[:].unsqueeze(1).to_broadcast([P, T4, NH]),
                                               op0=ALU.mult, op1=ALU.mult).then_inc(ready, 1)
                link(nc.vector.tensor_scalar(e[:], e[:], 1.0, None, ALU.add))
                link(nc.vector.reciprocal(R[:, R_STEP, :, SSM_H:], e[:]))
                dve.wait_ge(soft, 5)
                link(nc.vector.tensor_tensor(R[:, R_STEP_OUT], R[:, R_STEP], R[:, R_OUT], ALU.mult))
                nc.vector.memset(R[:, R_SKIP, :, SSM_H:], 0.0)


def scan_products(c, pe, i, u, took, z_full):
    nc, ring = c.nc, c.ring
    bank = 6 + u % 2
    if not (isinstance(i, int) and i == 0 and u < 2):
        pe.wait_ge(took, i * 6 + u - 1)
    if u < 4:
        w, freed = ring.slab(pe, i, u)
        for k in range(KT):
            last = nc.tensor.matmul(c.ps[:, bank, :], w[:, k * P:(k + 1) * P], c.hT[:, k, CTX:], start=k == 0, stop=k == KT - 1)
        last.then_inc(freed, 1)
        return
    w = [ring.slab(pe, i, s) for s in (4, 5)]
    for tt in range(2):
        t = 2 * (u - 4) + tt
        for k in range(KT):
            last = nc.tensor.matmul(c.ps[:, bank, tt * 256:(tt + 1) * 256], c.hT[:, k, CTX + t * P:CTX + (t + 1) * P],
                                    w[k // 4][0][:, (k % 4) * 256:(k % 4 + 1) * 256], start=k == 0, stop=k == KT - 1)
            if t == 3 and k == 3:
                last.then_inc(w[0][1], 1)
    last.then_inc(z_full if u == 4 else w[1][1], 1)


def scan_takes(c, act, i, u, took, z_full, conv_done, gated, xin, zs):
    nc, ring = c.nc, c.ring
    later = not (isinstance(i, int) and i == 0)
    if u < 4:
        ring.wait_used(act, i, u)
        if later:
            act.wait_ge(conv_done, i * 4 + u - 3)
        nc.scalar.activation(xin[:, u, 3:], c.ps[:, 6 + u % 2, :], ACT.Copy).then_inc(took, 1)
        return
    if u == 4:
        act.wait_ge(z_full, i + 1)
        if later:
            act.wait_ge(gated, i)
    else:
        ring.wait_used(act, i, 5)
    nc.scalar.activation(zs[:, 2 * (u - 4):2 * (u - 4) + 2, :], c.ps[:, 2 + u, :].rearrange("p (t f) -> p t f", t=2), ACT.Silu).then_inc(took, 1)


def convolve(c, dve, link, g, xin, acc, par, took, sil_ready, conv_done):
    nc = c.nc
    for j in range(4):
        dve.wait_ge(took, g * 6 + j + 1)
        if j >= 2 or not (isinstance(g, int) and g == 0):
            dve.wait_ge(sil_ready, g * 4 + max(j - 1, 0) if j >= 1 else g * 4)
        link(nc.vector.tensor_scalar(acc[:, j % 2, :], xin[:, j, 0:LAT], par[:, 4 * j:4 * j + 1], None, ALU.mult))
        for tap in range(1, 4):
            ins = nc.vector.scalar_tensor_tensor(out=acc[:, j % 2, :], in0=xin[:, j, tap:tap + LAT], scalar=par[:, 4 * j + tap:4 * j + tap + 1],
                                                 in1=acc[:, j % 2, :], op0=ALU.mult, op1=ALU.add)
            if tap < 3:
                link(ins)
            else:
                ins.then_inc(conv_done, 1)


def run_groups(eng, products, scan, first_part=False):
    for u in range(6):
        products(0, u)
    with eng.Fori(1, GROUPS) as i:
        for part in range(6):
            if first_part:
                scan(i - 1, part)
                products(i, part)
            else:
                products(i, part)
                scan(i - 1, part)
    for part in range(6):
        scan(GROUPS - 1, part)


def ssm(c, name, a, ysT):
    nc = c.nc
    T4, PER = LAT_TILES, 26
    with Stage(c, name) as st:
        sb, sem = st.sb, st.sem
        xin = sb("xin", [P, 4, LAT + 3])
        acc = sb("acc", [P, 2, LAT])
        par = sb("par", [P, 20])
        tab = sb("tab", [P, 7, T4, 4])
        sil = sb("sil", [P, 4, LAT])
        zs = sb("zs", [P, T4, 256])
        am = sb("am", [P, T4, 4, P])
        dec = sb("dec", [P, T4, 4, P])
        cbm = sb("cbm", [P, T4, P])
        btok = sb("btok", [P, T4, P])
        xdt, xw, xd, y = (sb(x, [P, T4, 256]) for x in ("xdt", "xw", "xd", "y"))
        S = sb("S", [P, 4, 256])
        sq = sb("sq", [P, 256])
        stat = sb("stat", [P, 3, T4])
        names = ("took", "z_full", "conv_done", "gated", "sil_ready", "am_ready", "dec_full", "dec_ready", "xs_turned", "xs_read",
                 "b_turned", "btok_ready", "cb_full", "m_ready", "p_full", "y_full", "s_ready", "yo_full", "y_sq", "root",
                 "yn_ready", "yt_full", "placed", "step", "y_ready", "zeroed")
        (took, z_full, conv_done, gated, sil_ready, am_ready, dec_full, dec_ready, xs_turned, xs_read, b_turned, btok_ready,
         cb_full, m_ready, p_full, y_full, s_ready, yo_full, y_sq, root, yn_ready, yt_full, placed, step, y_ready,
         zeroed) = (sem(x) for x in names)

        def half(bank, ch):
            return c.ps[:, bank + ch // 2, (ch % 2) * 256:(ch % 2) * 256 + 256]

        with st.block() as block:
            @block.sync
            def _(sp):
                c.ring.stream(sp, name)

            @block.tensor
            def _(pe):
                def products(i, u):
                    scan_products(c, pe, i, u, took, z_full)

                def scan(g, part):
                    later = not isinstance(g, int) or g > 0
                    if part == 1:
                        pe.wait_ge(am_ready, g + 1)
                        pe.wait_ge(placed, g * 2)
                        for ch in range(T4):
                            nc.tensor.matmul(c.ps[:, ch, :], c.after, am[:, ch].rearrange("p h f -> p (h f)"), start=True, stop=True).then_inc(dec_full, 1)
                        pe.wait_ge(sil_ready, g * 4 + 2)
                        for b in range(2):
                            for ch in (2 * b, 2 * b + 1):
                                for j in range(2):
                                    last = nc.tensor.transpose(half(4, ch)[:, j * P:(j + 1) * P], sil[:, j, ch * P:(ch + 1) * P], c.ident)
                            last.then_inc(xs_turned, 1)
                    if part == 2:
                        pe.wait_ge(sil_ready, g * 4 + 4)
                        pe.wait_ge(dec_ready, g * 4 + 2)
                        for ch in range(T4):
                            last = nc.tensor.transpose(c.ps[:, 0, ch * P:(ch + 1) * P], sil[:, 2, ch * P:(ch + 1) * P], c.ident)
                        last.then_inc(b_turned, 1)
                        for ch in range(T4):
                            last = nc.tensor.matmul(c.ps[:, 1, ch * P:(ch + 1) * P], sil[:, 2, ch * P:(ch + 1) * P],
                                                    sil[:, 3, ch * P:(ch + 1) * P], start=True, stop=True)
                        last.then_inc(cb_full, 1)
                    if part == 3:
                        pe.wait_ge(btok_ready, g + 1)
                        pe.wait_ge(xs_read, g * 2 + 2)
                        pe.wait_ge(m_ready, g * 4 + 1)
                        for ch in range(3):
                            last = nc.tensor.matmul(half(0, ch), btok[:, ch, :], xw[:, ch, :], start=True, stop=True)
                        last.then_inc(p_full, 1)
                        pe.wait_ge(dec_ready, g * 4 + 4)
                        for ch in range(T4):
                            pe.wait_ge(m_ready, g * 4 + ch + 1)
                            for h in range(4):
                                last = nc.tensor.matmul(half(2, ch)[:, h * 64:(h + 1) * 64], dec[:, ch, h, :], xdt[:, ch, h * 64:(h + 1) * 64],
                                                        start=True, stop=True)
                            if ch % 2:
                                last.then_inc(y_full, 1)
                    if part == 4:
                        for ch in range(1, T4):
                            pe.wait_ge(s_ready, g * 3 + ch)
                            nc.tensor.matmul(half(4, ch), sil[:, 3, ch * P:(ch + 1) * P], S[:, ch, :], start=True, stop=True).then_inc(yo_full, 1)
                    if part == 5:
                        pe.wait_ge(yn_ready, g + 1)
                        for j in range(2):
                            for ch in range(T4):
                                last = nc.tensor.transpose(c.ps[:, j, ch * P:(ch + 1) * P], y[:, ch, j * P:(j + 1) * P], c.ident)
                            last.then_inc(yt_full, 1)

                run_groups(pe, products, scan)

            @block.scalar
            def _(act):
                def products(i, u):
                    scan_takes(c, act, i, u, took, z_full, conv_done, gated, xin, zs)

                def scan(g, part):
                    if part == 0:
                        act.wait_ge(yt_full, g * 2)
                        for j in range(4):
                            act.wait_ge(conv_done, g * 4 + j + 1)
                            nc.scalar.activation(sil[:, j, :], acc[:, j % 2, :], ACT.Silu, bias=par[:, 16 + j:17 + j]).then_inc(sil_ready, 1)
                    if part == 1:
                        for ch in range(T4):
                            act.wait_ge(dec_full, g * 4 + ch + 1)
                            nc.scalar.activation(dec[:, ch].rearrange("p h f -> p (h f)"), c.ps[:, ch, :], ACT.Exp).then_inc(dec_ready, 1)
                    if part == 2:
                        act.wait_ge(b_turned, g + 1)
                        nc.scalar.activation(btok[:].rearrange("p t f -> p (t f)"), c.ps[:, 0, :], ACT.Copy).then_inc(btok_ready, 1)
                    if part == 4:
                        for ch in range(T4):
                            act.wait_ge(y_ready, g * 4 + ch + 1)
                            if ch:
                                act.wait_ge(y_sq, g * 4 + ch)
                            nc.scalar.activation(sq[:], y[:, ch, :], ACT.Square, accum_out=stat[:, 0, ch:ch + 1]).then_inc(y_sq, 1)
                        act.wait_ge(y_sq, g * 4 + 4)
                        nc.scalar.activation(stat[:, 1, :], stat[:, 0, :], ACT.Sqrt, bias=c.eps, scale=1.0 / 256).then_inc(root, 1)
                    if part == 5:
                        for j in range(2):
                            act.wait_ge(yt_full, g * 2 + j + 1)
                            nc.scalar.activation(ysT[:, bass.ds(g * 2 + j, 1), :].rearrange("p a f -> p (a f)"), c.ps[:, j, :], ACT.Copy,
                                                 scale=c.small(0, "ssm_norm_w_2")[:, bass.ds(g * 2 + j, 1)]).then_inc(placed, 1)

                act.wait_ge(zeroed, 1)
                run_groups(act, products, scan, True)

            @block.vector
            def _(dve):
                link = Chain(dve, step)
                nc.vector.memset(xin[:, :, 0:3], 0.0).then_inc(zeroed, 1)
                link.enter_loop()
                with dve.Fori(0, GROUPS) as g:
                    link.iteration(g, PER)
                    dve.wait_ge(sil_ready, g * 4)
                    nc.vector.tensor_copy(par[:], c.small(0, "ssm_par")[:, bass.ds(g * 20, 20)])
                    link(nc.vector.tensor_copy(tab[:].rearrange("p a t h -> p (a t) h"),
                                               c.rates[:].rearrange("p a t h -> p (a t) h")[:, :, bass.ds(g * 4, 4)]))
                    convolve(c, dve, link, g, xin, acc, par, took, sil_ready, conv_done)
                    for ch in range(T4):
                        last = nc.vector.tensor_tensor(am[:, ch], c.upto.unsqueeze(1).to_broadcast([P, 4, P]),
                                                       tab[:, R_LOG, ch, :].unsqueeze(2).to_broadcast([P, 4, P]), ALU.mult)
                    last.then_inc(am_ready, 1)
                    for b in range(2):
                        dve.wait_ge(xs_turned, g * 2 + b + 1)
                        src = c.ps[:, 4 + b, :].rearrange("p (n e) -> p n e", e=64)
                        for out, k in ((xdt, R_STEP), (xw, R_STEP_OUT), (xd, R_SKIP)):
                            f = tab[:, k].rearrange("p t h -> p (t h)")[:, 8 * b:8 * b + 8].unsqueeze(2).to_broadcast([P, 8, 64])
                            last = nc.vector.tensor_tensor(out[:, 2 * b:2 * b + 2, :].rearrange("p t (h e) -> p (t h) e", e=64), src, f, ALU.mult)
                        last.then_inc(xs_read, 1)
                    dve.wait_ge(cb_full, g + 1)
                    link(nc.vector.tensor_tensor(cbm[:], c.ps[:, 1, :].rearrange("p (t f) -> p t f", t=T4),
                                                 c.upto.unsqueeze(1).to_broadcast([P, T4, P]), ALU.mult))
                    for ch in range(T4):
                        dve.wait_ge(dec_ready, g * 4 + ch + 1)
                        nc.vector.tensor_tensor(dec[:, ch], dec[:, ch], cbm[:, ch].unsqueeze(1).to_broadcast([P, 4, P]), ALU.mult).then_inc(m_ready, 1)
                    dve.wait_ge(p_full, g + 1)
                    nc.vector.tensor_copy(S[:, 1, :], half(0, 0)).then_inc(s_ready, 1)
                    for ch in (1, 2):
                        dve.wait_ge(s_ready, g * 3 + ch)
                        link(nc.vector.tensor_tensor(S[:, ch + 1, :].rearrange("p (h e) -> p h e", h=4), S[:, ch, :].rearrange("p (h e) -> p h e", h=4),
                                                     tab[:, R_LAST, ch, :].unsqueeze(2).to_broadcast([P, 4, 64]), ALU.mult))
                        nc.vector.tensor_tensor(S[:, ch + 1, :], S[:, ch + 1, :], half(0, ch), ALU.add).then_inc(s_ready, 1)
                    for ch in range(T4):
                        dve.wait_ge(y_full, g * 2 + ch // 2 + 1)
                        link(nc.vector.tensor_tensor(y[:, ch, :], half(2, ch), xd[:, ch, :], ALU.add))
                        if ch:
                            dve.wait_ge(yo_full, g * 3 + (1 if ch == 1 else 3))
                            link(nc.vector.tensor_tensor(xd[:, ch, :].rearrange("p (h e) -> p h e", h=4), half(4, ch).rearrange("p (h e) -> p h e", h=4),
                                                         tab[:, R_IN, ch, :].unsqueeze(2).to_broadcast([P, 4, 64]), ALU.mult))
                            link(nc.vector.tensor_tensor(y[:, ch, :], y[:, ch, :], xd[:, ch, :], ALU.add))
                        if ch == 0:
                            dve.wait_ge(took, g * 6 + 6)
                        nc.vector.tensor_tensor(y[:, ch, :], y[:, ch, :], zs[:, ch, :], ALU.mult).then_inc(y_ready, 1)
                    dve.wait_ge(y_ready, g * 4 + 4)
                    dve.wait_ge(root, g + 1)
                    nc.vector.reciprocal(stat[:, 2, :], stat[:, 1, :]).then_inc(gated, 1)
                    dve.wait_ge(gated, g + 1)
                    for ch in range(T4):
                        last = nc.vector.tensor_scalar(y[:, ch, :], y[:, ch, :], stat[:, 2, ch:ch + 1], None, ALU.mult)
                    last.then_inc(yn_ready, 1)
                link.leave_loop(GROUPS, PER)
    c.ring.close()


def gdn(c, name, a, ogT):
    nc = c.nc
    T4, PER = LAT_TILES, 29
    with Stage(c, name) as st:
        sb, sem = st.sb, st.sem
        xin = sb("xin", [P, 4, LAT + 3])
        acc = sb("acc", [P, 2, LAT])
        par = sb("par", [P, 16])
        tab = sb("tab", [P, 7, T4, 2])
        sil = c.x[:, 0:CTX_TILES, :].rearrange("p t d -> p (t d)").rearrange("p (j f) -> p j f", j=4)
        vtok, zs = c.hT[:, 0:4, 0:CTX], c.hT[:, 4:8, 0:CTX]
        dec = sb("dec", [P, T4, 2, P])
        ktok = sb("ktok", [P, T4, P])
        U, Um, X, Y, W, att = (sb(x, [P, T4, 2, P]) for x in ("U", "Um", "X", "Y", "W", "att"))
        sq = Um[:].rearrange("p t h f -> p (t h f)").rearrange("p (a f) -> p a f", a=2)
        rn = W[:].rearrange("p t h f -> p (t h f)").rearrange("p (a f) -> p a f", a=2)
        am = X[:]
        S = sb("S", [P, 2, 256])
        R_, vn, vw = (sb(x, [P, 256]) for x in ("R", "vn", "vw"))
        o = U[:].rearrange("p t h f -> p t (h f)")
        stat = sb("stat", [P, 3, T4 * 2])
        names = ("took", "z_full", "conv_done", "gated", "sil_ready", "am_ready", "dec_full", "dec_ready", "qk_sq", "sums", "qk_root",
                 "qk_ready", "k_turned", "v_turned", "kk_full", "kq_full", "ktok_ready", "vtok_ready", "um_ready", "w_full", "w_ready",
                 "xy_full", "xy_ready", "ks_full", "r_ready", "vn_full", "vn_ready", "p_full", "s_ready", "o_full", "o_ready",
                 "o_sq", "root", "yn_ready", "yt_full", "placed", "step", "zeroed")
        sems = {x: sem(x) for x in names}
        (took, z_full, conv_done, gated, sil_ready, am_ready, dec_full, dec_ready, qk_sq, sums, qk_root, qk_ready, k_turned, v_turned,
         kk_full, kq_full, ktok_ready, vtok_ready, um_ready, w_full, w_ready, xy_full, xy_ready, ks_full, r_ready, vn_full, vn_ready,
         p_full, s_ready, o_full, o_ready, o_sq, root, yn_ready, yt_full, placed, step, zeroed) = (sems[x] for x in names)

        def split(x):
            return x.rearrange("p (h f) -> p h f", h=2)

        def chunk(ch):
            return slice(ch * P, (ch + 1) * P)

        def prob(hf):
            return [(2 * hf + e // 2, e % 2) for e in range(4)]

        with st.block() as block:
            @block.sync
            def _(sp):
                c.ring.stream(sp, name)

            @block.tensor
            def _(pe):
                def products(i, u):
                    scan_products(c, pe, i, u, took, z_full)

                def level(g, lev):
                    for hf in range(2):
                        pe.wait_ge(um_ready, g * 7 + lev + 1)
                        if lev:
                            pe.wait_ge(xy_ready, (g * 7 + lev - 1) * 2 + hf + 1)
                        for e, (ch, h) in enumerate(prob(hf)):
                            last = nc.tensor.matmul(c.ps[:, 3 * hf, e * P:(e + 1) * P], Um[:, ch, h, :], X[:, ch, h, :] if lev else c.ident,
                                                    start=True, stop=True)
                        last.then_inc(w_full, 1)
                    if lev:
                        for hf in range(2):
                            pe.wait_ge(w_ready, (g * 6 + lev - 1) * 2 + hf + 1)
                            if lev < LEVELS - 1:
                                for e, (ch, h) in enumerate(prob(hf)):
                                    nc.tensor.matmul(c.ps[:, 3 * hf + 1, e * P:(e + 1) * P], Y[:, ch, h, :], W[:, ch, h, :], start=True, stop=True)
                            for e, (ch, h) in enumerate(prob(hf)):
                                last = nc.tensor.matmul(c.ps[:, 3 * hf + 2, e * P:(e + 1) * P], W[:, ch, h, :], Y[:, ch, h, :], start=True, stop=True)
                            last.then_inc(xy_full, 1)

                def scan(g, part):
                    if part == 0:
                        pe.wait_ge(placed, g * 2)
                        for j in range(2):
                            pe.wait_ge(qk_sq, g * 2 + j + 1)
                            nc.tensor.matmul(c.ps[:, j, :], c.ones, sq[:, j, :], start=True, stop=True).then_inc(sums, 1)
                        pe.wait_ge(am_ready, g + 1)
                        for b in range(2):
                            nc.tensor.matmul(c.ps[:, 2 + b, :], c.after, am[:, 2 * b:2 * b + 2].rearrange("p t h f -> p (t h f)"),
                                             start=True, stop=True).then_inc(dec_full, 1)
                    if part == 1:
                        pe.wait_ge(sil_ready, g * 4 + 4)
                        pe.wait_ge(qk_root, g * 2 + 2)
                        for b in range(2):
                            for ch in (2 * b, 2 * b + 1):
                                for j in range(2):
                                    last = nc.tensor.transpose(c.ps[:, b, (ch % 2) * 256 + j * P:(ch % 2) * 256 + (j + 1) * P], sil[:, 2 + j, chunk(ch)], c.ident)
                            last.then_inc(v_turned, 1)
                        pe.wait_ge(qk_ready, g + 1)
                        for ch in range(T4):
                            last = nc.tensor.transpose(c.ps[:, 4, chunk(ch)], sil[:, 1, chunk(ch)], c.ident)
                        last.then_inc(k_turned, 1)
                        for ch in range(T4):
                            last = nc.tensor.matmul(c.ps[:, 5, chunk(ch)], sil[:, 1, chunk(ch)], sil[:, 1, chunk(ch)], start=True, stop=True)
                        last.then_inc(kk_full, 1)
                        pe.wait_ge(dec_ready, g * 2 + 1)
                        for ch in range(T4):
                            last = nc.tensor.matmul(c.ps[:, 2, chunk(ch)], sil[:, 1, chunk(ch)], sil[:, 0, chunk(ch)], start=True, stop=True)
                        last.then_inc(kq_full, 1)
                    if part == 2:
                        pe.wait_ge(vtok_ready, g * 2 + 2)
                        pe.wait_ge(ktok_ready, g + 1)
                        pe.wait_ge(dec_ready, g * 2 + 2)
                        level(g, 0)
                        level(g, 1)
                        level(g, 2)
                    if part == 3:
                        for lev in range(3, LEVELS):
                            level(g, lev)
                    if part == 4:
                        for ch in range(T4):
                            if ch:
                                pe.wait_ge(s_ready, g * 3 + ch)
                                nc.tensor.matmul(c.ps[:, 0, 0:256], sil[:, 1, chunk(ch)], S[:, ch % 2, :], start=True, stop=True).then_inc(ks_full, 1)
                                if ch > 1:
                                    pe.wait_ge(o_ready, g * 4 + ch)
                                nc.tensor.matmul(c.ps[:, 3, 0:256], sil[:, 0, chunk(ch)], S[:, ch % 2, :], start=True, stop=True)
                            pe.wait_ge(r_ready, g * 4 + ch + 1)
                            if ch == 0:
                                pe.wait_ge(xy_ready, (g * 7 + 6) * 2 + 2)
                            for h in range(2):
                                last = nc.tensor.matmul(c.ps[:, 1, h * P:(h + 1) * P], Y[:, ch, h, :], R_[:, h * P:(h + 1) * P], start=True, stop=True)
                            last.then_inc(vn_full, 1)
                            pe.wait_ge(vn_ready, g * 4 + ch + 1)
                            if ch < 3:
                                nc.tensor.matmul(c.ps[:, 2, 0:256], ktok[:, ch, :], vw[:], start=True, stop=True).then_inc(p_full, 1)
                            if ch:
                                pe.wait_ge(o_ready, g * 4 + ch)
                            for h in range(2):
                                last = nc.tensor.matmul(c.ps[:, 4, h * P:(h + 1) * P], att[:, ch, h, :], vn[:, h * P:(h + 1) * P], start=True, stop=True)
                            last.then_inc(o_full, 1)
                    if part == 5:
                        pe.wait_ge(yn_ready, g + 1)
                        for j in range(2):
                            for ch in range(T4):
                                last = nc.tensor.transpose(c.ps[:, j, chunk(ch)], o[:, ch, j * P:(j + 1) * P], c.ident)
                            last.then_inc(yt_full, 1)

                run_groups(pe, products, scan)

            @block.scalar
            def _(act):
                def products(i, u):
                    scan_takes(c, act, i, u, took, z_full, conv_done, gated, xin, zs)

                def level(g, lev):
                    if lev:
                        for hf in range(2):
                            act.wait_ge(w_full, (g * 7 + lev) * 2 + hf + 1)
                            nc.scalar.activation(W[:, 2 * hf:2 * hf + 2].rearrange("p t h f -> p (t h f)"), c.ps[:, 3 * hf, :], ACT.Copy).then_inc(w_ready, 1)

                def scan(g, part):
                    if part == 0:
                        act.wait_ge(yt_full, g * 2)
                        for j in range(4):
                            act.wait_ge(conv_done, g * 4 + j + 1)
                            nc.scalar.activation(sil[:, j, :], acc[:, j % 2, :], ACT.Silu).then_inc(sil_ready, 1)
                            if j < 2:
                                act.wait_ge(sil_ready, g * 4 + j + 1)
                                nc.scalar.activation(sq[:, j, :], sil[:, j, :], ACT.Square).then_inc(qk_sq, 1)
                        for j in range(2):
                            act.wait_ge(sums, g * 2 + j + 1)
                            nc.scalar.activation(rn[:, j, :], c.ps[:, j, :], ACT.Sqrt, bias=c.eps if j else c.eps_k,
                                                 scale=1.0 if j else float(P)).then_inc(qk_root, 1)
                        for b in range(2):
                            act.wait_ge(dec_full, g * 2 + b + 1)
                            nc.scalar.activation(dec[:, 2 * b:2 * b + 2].rearrange("p t h f -> p (t h f)"), c.ps[:, 2 + b, :], ACT.Exp).then_inc(dec_ready, 1)
                    if part == 1:
                        for b in range(2):
                            act.wait_ge(v_turned, g * 2 + b + 1)
                            nc.scalar.activation(vtok[:, 2 * b:2 * b + 2, :], c.ps[:, b, :].rearrange("p (t f) -> p t f", t=2), ACT.Copy).then_inc(vtok_ready, 1)
                        act.wait_ge(k_turned, g + 1)
                        nc.scalar.activation(ktok[:].rearrange("p t f -> p (t f)"), c.ps[:, 4, :], ACT.Copy).then_inc(ktok_ready, 1)
                    if part == 2:
                        for lev in range(3):
                            level(g, lev)
                    if part == 3:
                        for lev in range(3, LEVELS):
                            level(g, lev)
                    if part == 4:
                        act.wait_ge(o_ready, g * 4 + 4)
                        act.wait_ge(w_ready, g * 12 + 12)
                        nc.scalar.activation(W[:].rearrange("p t h f -> p (t h f)"), U[:].rearrange("p t h f -> p (t h f)"), ACT.Square).then_inc(o_sq, 1)
                        act.wait_ge(gated, g + 1)
                        nc.scalar.activation(stat[:, 1, :], stat[:, 0, :], ACT.Sqrt, bias=c.eps, scale=1.0 / P).then_inc(root, 1)
                    if part == 5:
                        for j in range(2):
                            act.wait_ge(yt_full, g * 2 + j + 1)
                            nc.scalar.activation(ogT[:, bass.ds(g * 2 + j, 1), :].rearrange("p a f -> p (a f)"), c.ps[:, j, :], ACT.Copy,
                                                 scale=c.small(0, "gdn_norm_w_2")).then_inc(placed, 1)

                act.wait_ge(zeroed, 1)
                run_groups(act, products, scan, True)

            @block.gpsimd
            def _(pool):
                with pool.Fori(0, GROUPS) as g:
                    for lev in range(1, LEVELS):
                        if lev == 1:
                            pool.wait_ge(um_ready, g * 7 + 1)
                        pool.wait_ge(w_full, (g * 7 + lev) * 2)
                        for ch in range(T4):
                            last = nc.gpsimd.tensor_tensor(Um[:, ch], U[:, ch], c.mask_f[:, lev, :].unsqueeze(1).to_broadcast([P, 2, P]), ALU.mult)
                        last.then_inc(um_ready, 1)

            @block.vector
            def _(dve):
                link = Chain(dve, step)
                nc.vector.memset(xin[:, :, 0:3], 0.0).then_inc(zeroed, 1)
                link.enter_loop()
                with dve.Fori(0, GROUPS) as g:
                    link.iteration(g, PER)
                    nc.vector.tensor_copy(par[:], c.small(0, "gdn_par")[:, bass.ds(g * 16, 16)])
                    link(nc.vector.tensor_copy(tab[:].rearrange("p a t h -> p (a t) h"),
                                               c.rates[:].rearrange("p a t h -> p (a t) h")[:, :, bass.ds(g * 2 + SSM_H, 2)]))
                    convolve(c, dve, link, g, xin, acc, par, took, sil_ready, conv_done)
                    for ch in range(T4):
                        last = nc.vector.tensor_tensor(am[:, ch], c.upto.unsqueeze(1).to_broadcast([P, 2, P]),
                                                       tab[:, R_LOG, ch, :].unsqueeze(2).to_broadcast([P, 2, P]), ALU.mult)
                    last.then_inc(am_ready, 1)
                    for j in range(2):
                        dve.wait_ge(qk_root, g * 2 + j + 1)
                        link(nc.vector.reciprocal(rn[:, j, :], rn[:, j, :]))
                        last = nc.vector.tensor_tensor(sil[:, j, :], sil[:, j, :], rn[:, j, :], ALU.mult)
                    last.then_inc(qk_ready, 1)
                    for ch in range(T4):
                        if ch % 2 == 0:
                            dve.wait_ge(dec_ready, g * 2 + ch // 2 + 1)
                        last = nc.vector.tensor_tensor(dec[:, ch], dec[:, ch], c.upto.unsqueeze(1).to_broadcast([P, 2, P]), ALU.mult)
                    link(last)
                    dve.wait_ge(kk_full, g + 1)
                    for ch in range(T4):
                        last = nc.vector.tensor_tensor(U[:, ch], dec[:, ch], c.ps[:, 5, chunk(ch)].unsqueeze(1).to_broadcast([P, 2, P]), ALU.mult)
                    link(last)
                    link(nc.vector.tensor_tensor(U[:].rearrange("p t h f -> p (t h) f"), U[:].rearrange("p t h f -> p (t h) f"),
                                                 tab[:, R_STEP].rearrange("p t h -> p (t h)").unsqueeze(2).to_broadcast([P, 8, P]), ALU.mult))
                    link(nc.vector.tensor_tensor(Um[:].rearrange("p t h f -> p (t h) f"), U[:].rearrange("p t h f -> p (t h) f"),
                                                 c.mask_f[:, 0, :].unsqueeze(1).to_broadcast([P, 8, P]), ALU.mult))
                    nc.vector.tensor_tensor(Y[:].rearrange("p t h f -> p (t h) f"), c.ident.unsqueeze(1).to_broadcast([P, 8, P]),
                                            Um[:].rearrange("p t h f -> p (t h) f"), ALU.subtract).then_inc(um_ready, 1)
                    dve.wait_ge(kq_full, g + 1)
                    for ch in range(T4):
                        last = nc.vector.tensor_tensor(att[:, ch], dec[:, ch], c.ps[:, 2, chunk(ch)].unsqueeze(1).to_broadcast([P, 2, P]), ALU.mult)
                    link(last)
                    for lev in range(LEVELS):
                        for hf in range(2):
                            part = lambda M: M[:, 2 * hf:2 * hf + 2].rearrange("p t h f -> p (t h f)")
                            if lev == 0:
                                dve.wait_ge(w_full, g * 14 + hf + 1)
                                nc.vector.tensor_tensor(X[:, 2 * hf:2 * hf + 2].rearrange("p t h f -> p (t h) f"), c.ident.unsqueeze(1).to_broadcast([P, 4, P]),
                                                        c.ps[:, 3 * hf, :].rearrange("p (e f) -> p e f", e=4), ALU.subtract).then_inc(xy_ready, 1)
                                continue
                            dve.wait_ge(xy_full, (g * 6 + lev - 1) * 2 + hf + 1)
                            if lev < LEVELS - 1:
                                nc.vector.tensor_tensor(part(X), part(X), c.ps[:, 3 * hf + 1, :], ALU.subtract)
                            nc.vector.tensor_tensor(part(Y), part(Y), c.ps[:, 3 * hf + 2, :], ALU.subtract).then_inc(xy_ready, 1)
                    tb = lambda k, ch: tab[:, k, ch, :].unsqueeze(2).to_broadcast([P, 2, P])
                    for ch in range(T4):
                        if ch:
                            dve.wait_ge(ks_full, g * 3 + ch)
                            link(nc.vector.tensor_tensor(split(R_[:]), split(c.ps[:, 0, 0:256]), tb(R_IN, ch), ALU.mult))
                            nc.vector.tensor_tensor(R_[:], vtok[:, ch, :], R_[:], ALU.subtract).then_inc(r_ready, 1)
                        else:
                            nc.vector.tensor_copy(R_[:], vtok[:, 0, :]).then_inc(r_ready, 1)
                        dve.wait_ge(vn_full, g * 4 + ch + 1)
                        nc.vector.tensor_tensor(split(vn[:]), split(c.ps[:, 1, 0:256]), tb(R_STEP, ch), ALU.mult)
                        nc.vector.tensor_tensor(split(vw[:]), split(c.ps[:, 1, 0:256]), tb(R_STEP_OUT, ch), ALU.mult).then_inc(vn_ready, 1)
                        if ch == 0:
                            dve.wait_ge(p_full, g * 3 + 1)
                            nc.vector.tensor_copy(S[:, 1, :], c.ps[:, 2, 0:256]).then_inc(s_ready, 1)
                        elif ch < 3:
                            link(nc.vector.tensor_tensor(split(S[:, (ch + 1) % 2, :]), split(S[:, ch % 2, :]), tb(R_LAST, ch), ALU.mult))
                            dve.wait_ge(p_full, g * 3 + ch + 1)
                            nc.vector.tensor_tensor(S[:, (ch + 1) % 2, :], S[:, (ch + 1) % 2, :], c.ps[:, 2, 0:256], ALU.add).then_inc(s_ready, 1)
                        dve.wait_ge(o_full, g * 4 + ch + 1)
                        if ch:
                            link(nc.vector.tensor_tensor(split(o[:, ch, :]), split(c.ps[:, 3, 0:256]), tb(R_IN, ch), ALU.mult))
                            nc.vector.tensor_tensor(o[:, ch, :], o[:, ch, :], c.ps[:, 4, 0:256], ALU.add).then_inc(o_ready, 1)
                        else:
                            nc.vector.tensor_copy(o[:, 0, :], c.ps[:, 4, 0:256]).then_inc(o_ready, 1)
                    dve.wait_ge(o_sq, g + 1)
                    nc.vector.tensor_reduce(stat[:, 0, :], W[:].rearrange("p t h f -> p (t h) f"), AX, ALU.add)
                    dve.wait_ge(took, g * 6 + 6)
                    nc.vector.tensor_tensor(o, o, zs, ALU.mult).then_inc(gated, 1)
                    dve.wait_ge(gated, g + 1)
                    dve.wait_ge(root, g + 1)
                    link(nc.vector.reciprocal(stat[:, 2, :], stat[:, 1, :]))
                    nc.vector.tensor_tensor(U[:].rearrange("p t h f -> p (t h) f"), U[:].rearrange("p t h f -> p (t h) f"),
                                            stat[:, 2, :].unsqueeze(2).to_broadcast([P, 8, P]), ALU.mult).then_inc(yn_ready, 1)
                link.leave_loop(GROUPS, PER)
    c.ring.close()


def merge(c, name, ysT, ogT, mT):
    nc, ring = c.nc, c.ring
    with Stage(c, name) as st:
        sg = st.sb("sg", [P, 2, LAT])
        m = st.sb("m", [P, 2, LAT])
        gate_full, gate_read, sig_ready, up_full, up_read, done = (st.sem(x) for x in ("gate_full", "gate_read", "sig_ready", "up_full", "up_read", "done"))
        with st.block() as block:
            @block.sync
            def _(sp):
                ring.stream(sp, name)

            @block.tensor
            def _(pe):
                with pe.Fori(0, GROUPS) as j:
                    for b in range(2):
                        w, freed = ring.slab(pe, j, b)
                        pe.wait_ge(sig_ready, j * 2)
                        for k in range(KT):
                            last = nc.tensor.matmul(c.ps[:, b, :], w[:, k * P:(k + 1) * P], c.hT[:, k, CTX:], start=k == 0, stop=k == KT - 1)
                        last.then_inc(freed, 1)
                    for b, src in enumerate((ysT, ogT)):
                        pe.wait_ge(up_read, j * 2)
                        for half in range(2):
                            w, freed = ring.slab(pe, j, 2 + 2 * b + half)
                            for k in range(KT):
                                last = nc.tensor.matmul(c.ps[:, 2 + b, :], w[:, k * P:(k + 1) * P], src[:, 8 * half + k, :],
                                                        start=half == 0 and k == 0, stop=half == 1 and k == KT - 1)
                            last.then_inc(freed, 1)

            @block.scalar
            def _(act):
                with act.Fori(0, GROUPS) as j:
                    for b in range(2):
                        ring.wait_used(act, j, b)
                        act.wait_ge(up_read, j * 2)
                        nc.scalar.activation(sg[:, b, :], c.ps[:, b, :], ACT.Sigmoid).then_inc(sig_ready, 1)

            @block.vector
            def _(dve):
                with dve.Fori(0, GROUPS) as j:
                    for b in range(2):
                        dve.wait_ge(sig_ready, j * 2 + b + 1)
                        ring.wait_used(dve, j, 3 + 2 * b)
                        nc.vector.tensor_tensor(m[:, b, :], c.ps[:, 2 + b, :], sg[:, b, :], ALU.mult).then_inc(up_read, 1)
                    dve.wait_ge(up_read, j * 2 + 2)
                    nc.vector.tensor_tensor(mT[:, bass.ds(j, 1), :].rearrange("p a f -> p (a f)"), m[:, 0, :], m[:, 1, :], ALU.add).then_inc(done, 1)
                    dve.wait_ge(done, j + 1)
    ring.close()





def second_block(c, a, stop):
    nc = c.nc
    first = CTX_TILES
    final_norm(c, "final", a)
    modulation(c, "ada", 1, c.small(0, "b_ada_2"), [c.small(0, "norm_mix_pre_2"), c.small(0, "norm_mlp_pre_2")], 1)
    norm_transpose(c, "norm2", 0, first)
    with ExitStack() as held:
        ysT = held.enter_context(nc.sbuf_tensor("ysT", [P, 2 * GROUPS, LAT], F32))
        y = ysT[:].rearrange("p n f -> p (n f)")[:, 0:TILES * D].rearrange("p (t d) -> p t d", d=D)
        with ExitStack() as inner:
            sb = lambda n, s: inner.enter_context(nc.sbuf_tensor(n, s, F32))
            c.rates = sb("rates", [P, 7, LAT_TILES, NH])
            rates(c, "rate", a)
            ssm(c, "ssm", a, ysT)
            ogT = sb("ogT", [P, 2 * GROUPS, LAT])
            gdn(c, "gdn", a, ogT)
            mT = sb("mT", [P, KT, LAT])
            merge(c, "merge", ysT, ogT, mT)
            out_product(c, "out2", first, y, lambda k, t: mT[:, k, (t - first) * P:(t - first + 1) * P])
        residual(c, "res2", 2, first, y, a["norm_mix_post_2"])
        norm_transpose(c, "norm_mlp2", 1, first)
        mlp(c, "mlp2", first, y)
        residual(c, "res_mlp2", 5, first, y, a["norm_mlp_post_2"])


COLS = {}


def build(nc, a, out, stop=None):
    with ExitStack() as ctx:
        c = Core()
        c.nc = nc
        streams = []
        for l in range(2):
            streams += [(f"mod{l}", a[f"s_mod{l}"], 8, 6), (f"proj{l}", a[f"s_in{l}"], 16, 1),
                        (f"out{l}", a[f"s_out{l}"], 8, 1), (f"mlp{l}", a[f"s_mlp{l}"], 16, PASSES)]
        if stop == "b2":
            streams = []
        streams += [("ada", a["s_ada"], 8, 6), ("ssm", a["s_ssm"], 6, GROUPS), ("gdn", a["s_gdn"], 6, GROUPS),
                    ("merge", a["s_merge"], 6, GROUPS), ("out2", a["s_out2"], 8, 1), ("mlp2", a["s_mlp2"], 16, PASSES)]
        c.ring = Ring(nc, ctx, streams)
        c.small = lambda l, name: c.cols[:, COLS[name][0] + l * COLS[name][1]:COLS[name][0] + (l + 1) * COLS[name][1]]
        setup(c, a, ctx)
        if stop != "b2":
            first_layer(c, a, 0, True)
        if stop not in ("l0", "b2"):
            first_layer(c, a, 1, False)
        if stop in (None, "b2"):
            second_block(c, a, stop)
        with Stage(c, "store") as st:
            stored = st.sem("stored")
            with st.block() as block:
                @block.sync
                def _(sp):
                    if stop is None:
                        sp.dma_start(out.rearrange("a (t p) d -> p (a t) d", p=P), c.x[:, CTX_TILES:, :]).then_inc(stored, 16)
                    else:
                        sp.dma_start(out, c.x[:]).then_inc(stored, 16)
                    sp.wait_ge(stored, 16)


def _column_slabs(w):
    K, N = w.shape
    return w.reshape(K // D, KT, P, N // P, P).transpose(3, 0, 2, 1, 4).reshape(-1, P, D)


def _row_slabs(w):
    K, N = w.shape
    return w.reshape(K // 256, 2, P, N // HALF, HALF).transpose(3, 0, 2, 1, 4).reshape(-1, P, D)


def _z_slabs(w):
    return w.reshape(2, 4, P, 256).transpose(0, 2, 1, 3).reshape(2, P, D)


def _mlp_slabs(up, down):
    u = _column_slabs(up).reshape(PASSES, 8, P, D)
    d = np.stack([_row_slabs(down[q * D:(q + 1) * D]) for q in range(PASSES)])
    return np.concatenate([u, d], 1).reshape(-1, P, D)


def _columns(v):
    return v.reshape(-1, P).T


def _constants():
    s, f = np.arange(P)[:, None], np.arange(P)[None, :]
    parts = [s == f, s <= f, s >= f, s > f, (s >= 0) & (f >= 0), s // 64 == f // 64]
    joins = [(s // (2 * m) == f // (2 * m)) & (s % (2 * m) < m) & (f % (2 * m) >= m) for m in (1 << n for n in range(LEVELS))]
    parts += joins + [x.T for x in joins]
    eps = np.zeros((P, 2), np.float32)
    eps[:, 0], eps[:, 1] = EPS, P * EPS
    return np.concatenate([x.astype(np.float32) for x in parts] + [eps], 1)


def _bands():
    out = np.zeros((P, 5, 4, P), np.float32)
    for g, w in enumerate((2, 4, 8, 16)):
        M = np.zeros((LAT, LAT))
        for t in range(LAT):
            lo, hi = max(t - w // 2, 0), min(t + w // 2 - 1, LAT - 1)
            M[lo:hi + 1, t] = 1.0 / (hi - lo + 1)
            M[t, t] -= 1
        out[:, 0, g], out[:, 1, g], out[:, 2, g] = M[:P, :P], M[P:2 * P, P:2 * P], M[3 * P:, 3 * P:]
        out[:, 3, g], out[:, 4, g] = M[:P, P:2 * P], M[2 * P:3 * P, P:2 * P]
    return out.reshape(P, -1)


def _rope():
    half = HD // 2
    inv = (10000.0 ** (-np.arange(0, half, 2, dtype=np.float32) / half)).astype(np.float32)
    n = np.arange(LAT)
    ang = np.stack([(n // 64)[:, None].astype(np.float32) * inv, (n % 64)[:, None].astype(np.float32) * inv], 1)
    out = np.stack([np.cos(ang), np.sin(ang)], 0).reshape(2, LAT_TILES, P, 32).transpose(2, 0, 1, 3)
    return out.reshape(P, -1).astype(np.float32)


def _layout(i):
    r = {}
    vec = [np.stack([_columns(i["c"][0]), _columns(i["c_ctx"])], -1).reshape(P, 16),
           np.stack([_columns(i["c_2"][0])] * 2, -1).reshape(P, 16)]
    at = 32

    def add(name, x, width):
        nonlocal at
        COLS[name] = (at, width)
        vec.append(x)
        at += x.shape[1]

    for n in ("b_mod", "g_mix", "g_mlp", "s_pool"):
        x = _columns(i[n])
        add(n, x, x.shape[1] // 2)
    for n in ("b_ada_2", "norm_mix_pre_2", "norm_mlp_pre_2", "ssm_norm_w_2", "gdn_norm_w_2"):
        x = _columns(i[n])
        add(n, x, x.shape[1])
    taps = i["ssm_conv_w_2"][0].reshape(4, 32, P).transpose(2, 1, 0)
    bias = _columns(i["ssm_conv_b_2"])
    of = [[2 * q, 2 * q + 1, 16 + q, 24 + q] for q in range(GROUPS)]
    add("ssm_par", np.concatenate([y for t in of for y in (taps[:, t].reshape(P, 16), bias[:, t])], 1), 20 * GROUPS)
    taps = i["gdn_conv_w_2"][0].reshape(4, 32, P).transpose(2, 1, 0)
    of = [[q, 8 + q, 16 + 2 * q, 17 + 2 * q] for q in range(GROUPS)]
    add("gdn_par", np.concatenate([taps[:, t].reshape(P, 16) for t in of], 1), 16 * GROUPS)
    r["cols"] = np.concatenate(vec, 1)
    r["const"], r["band"], r["rope"] = _constants(), _bands(), _rope()
    for l in range(2):
        w = i["w_in"][l]
        r[f"s_mod{l}"] = _column_slabs(i["w_mod"][l])
        r[f"s_in{l}"] = np.concatenate([_column_slabs(w[:, 256:768]),
                                        _row_slabs(np.concatenate([w[:, :256], w[:, 768:1280], w[:, 1312:2080]], 1))])
        r[f"s_out{l}"] = _row_slabs(i["w_out"][l])
        r[f"s_mlp{l}"] = _mlp_slabs(i["w_up"][l], i["w_down"][l])
    r["w_r"] = i["w_in"][:, :, 1280:1312].reshape(2, KT, P, 32).transpose(0, 2, 1, 3)
    w = i["w_in_2"][0]
    z_ssm, xs, B, C, dt, q, k, v, z_gdn, ba, g_ssm, g_gdn = np.split(
        w, np.cumsum([2048, 2048, 1024, 1024, 32, 1024, 1024, 2048, 2048, 32, 1024]), axis=1)
    r["s_ssm"] = np.concatenate([y for n in range(GROUPS) for y in (
        _column_slabs(xs[:, 256 * n:256 * n + 256]), _column_slabs(B[:, P * n:P * n + P]), _column_slabs(C[:, P * n:P * n + P]),
        _z_slabs(z_ssm[:, 256 * n:256 * n + 256]))])
    r["s_gdn"] = np.concatenate([y for n in range(GROUPS) for y in (
        _column_slabs(q[:, P * n:P * n + P]), _column_slabs(k[:, P * n:P * n + P]), _column_slabs(v[:, 256 * n:256 * n + 256]),
        _z_slabs(z_gdn[:, 256 * n:256 * n + 256]))])
    r["s_merge"] = np.concatenate([
        _column_slabs(g_ssm)[:, None], _column_slabs(g_gdn)[:, None], _column_slabs(i["w_ssm_up_2"][0]).reshape(8, 2, P, D),
        _column_slabs(i["w_gdn_up_2"][0]).reshape(8, 2, P, D)], 1).reshape(48, P, D)
    r["w_rates"] = np.concatenate([dt, ba], 1).reshape(KT, P, 64).transpose(1, 0, 2)
    r["s_ada"] = _column_slabs(i["w_ada_2"][0])
    r["s_out2"] = _row_slabs(i["w_out_2"][0])
    r["s_mlp2"] = _mlp_slabs(i["w_mlp_up_2"][0], i["w_mlp_down_2"][0])
    for n in ("g_final", "ssm_dt_bias_2", "gdn_dt_bias_2", "ssm_A_log_2", "gdn_A_log_2", "ssm_D_2", "norm_mix_post_2",
              "norm_mlp_post_2", "x", "ctx", "w_pool", "w_gate", "b_gate", "g_gla", "g_q", "g_k"):
        r[n] = i[n]
    return r


def kernel(**inputs):
    import concourse.bacc as _bacc
    from concourse.bass_utils import run_bass_kernel_spmd as _run

    laid = _layout({k: np.asarray(v) for k, v in inputs.items()})
    nc = _bacc.Bacc("TRN2", target_bir_lowering=False, num_devices=1, dynamic_dma_scratch_size=1024)
    arrays, a = {}, {}
    for name, x in laid.items():
        arrays[f"in_{name}_dram"] = np.ascontiguousarray(x)
        a[name] = nc.dram_tensor(f"in_{name}_dram", x.shape, F32, kind="ExternalInput").ap()
    out = nc.dram_tensor("out_0_dram", (1, LAT, D), F32, kind="ExternalOutput").ap()
    build(nc, a, out)
    return _run(nc, [arrays], core_ids=[0]).results[0]["out_0_dram"]
```

```python
from contextlib import ExitStack

import numpy as np

import concourse.bass as bass
from concourse import mybir

P = 128
D = 1024
KT = D // P
HALF = 512
CTX_TILES, LAT_TILES = 2, 4
TILES = CTX_TILES + LAT_TILES
CTX = CTX_TILES * P
LAT = LAT_TILES * P
TOK = TILES * P
HEADS_Q, HEADS_KV, HD = 8, 2, 64
GLA_H = 4
LEVELS = 7
PASSES = 4
GROUPS = 8
EPS = 1e-6

F32 = mybir.dt.float32
F32R = mybir.dt.float32r
U32 = mybir.dt.uint32
ALU = mybir.AluOpType
ACT = mybir.ActivationFunctionType
AX = mybir.AxisListType.X

C_POOL, C_GV, C_GG, C_AQ, C_AK, C_AV = 0, 256, 512, 768, 1280, 1408


class Stage:

    def __init__(self, core, name):
        self.core, self.nc, self.name = core, core.nc, name
        self.held = ExitStack()
        self.sems = []

    def __enter__(self):
        return self

    def sem(self, what):
        s = self.nc.alloc_semaphore(f"{self.name}_{what}")
        self.sems.append(s)
        return s

    def sb(self, what, shape, dt=F32):
        return self.held.enter_context(self.nc.sbuf_tensor(f"{self.name}_{what}", shape, dt))

    def block(self):
        for s in self.core.spent:
            self.nc.gpsimd.sem_clear(s)
        for s in self.sems:
            self.nc.gpsimd.sem_inc(s, 1)
        self.nc.all_engine_barrier(sem_only=True)
        for s in self.core.spent:
            self.nc.release_semaphore(s)
        self.core.spent = self.sems
        return self.nc.Block(no_gpsimd_drain=True)

    def __exit__(self, kind, value, trace):
        self.held.close()


class Chain:

    def __init__(self, eng, sem):
        self.eng, self.sem, self.n, self.base = eng, sem, 0, 0

    def __call__(self, ins):
        self.n += 1
        ins.then_inc(self.sem, 1)
        self.eng.wait_ge(self.sem, self.base + self.n + 1)

    def iteration(self, i, per):
        self.base = self.start + i * per
        self.n = 0

    def enter_loop(self):
        self.start = self.base + self.n

    def leave_loop(self, count, per):
        assert self.n == per, (self.n, per)
        self.base, self.n = self.start + count * per, 0


class Pair:

    def __init__(self, hi, lo):
        self.hi, self.lo = hi, lo

    def __getitem__(self, at):
        return Pair(self.hi[at], self.lo[at])

    def rows(self, first, count, at):
        return Pair(*(x[:, bass.ds(first, count), at].rearrange("p a n -> p (a n)") for x in (self.hi, self.lo)))


def sbuf_pair(enter, nc, name, shape):
    return Pair(*(enter(nc.sbuf_tensor(f"{name}_{x}", shape, F32R)) for x in ("hi", "lo")))


def product3(nc, out, lhs, rhs, start, stop):
    nc.tensor.matmul(out, lhs.hi, rhs.hi, start=start, stop=False)
    nc.tensor.matmul(out, lhs.hi, rhs.lo, start=False, stop=False)
    return nc.tensor.matmul(out, lhs.lo, rhs.hi, start=False, stop=stop)


class Ring:

    SLOTS, PAIRS = 4, 3

    def __init__(self, nc, ctx, streams):
        self.nc = nc
        self.raw = [ctx.enter_context(nc.sbuf_tensor(f"slab{s}", [P, D], F32)) for s in range(self.SLOTS)]
        self.pairs = [sbuf_pair(ctx.enter_context, nc, f"slab{s}", [P, D]) for s in range(self.PAIRS)]
        self.loaded = [ctx.enter_context(nc.semaphore(f"slab{s}_loaded")) for s in range(self.SLOTS)]
        self.rounded, self.split, self.freed = (ctx.enter_context(nc.semaphore(f"slabs_{x}")) for x in ("rounded", "split", "freed"))
        self.used = [0] * self.SLOTS
        self.before = 0
        self.streams = streams
        self.at = 0

    def shape(self, n):
        _, _, per, count = self.streams[n]
        n = 4 if per % 4 == 0 else 3
        return per, count, n, n

    def fourth_pair(self, stage):
        self.pairs[3:] = [sbuf_pair(stage.held.enter_context, self.nc, f"{stage.name}_slab3", [P, D])]

    def load(self, sp, slot, n, index):
        _, src, _, _ = self.streams[n]
        ap = src[bass.ds(index, 1)].rearrange("a p n -> p (a n)")
        sp.dma_start(self.raw[slot][:], ap).then_inc(self.loaded[slot], 16)

    def first(self, sp, n, before=0):
        if n < len(self.streams):
            slots = self.shape(n)[2]
            held = self.shape(n - 1)[2] if n else 0
            for s in range(slots):
                if n:
                    sp.wait_ge(self.split, min(before, before - held + s + 1))
                self.load(sp, s, n, s)

    def stream(self, sp, name):
        n = self.at
        assert self.streams[n][0] == name
        per, count, slots, _ = self.shape(n)

        def follow(i, slabs):
            for u in slabs:
                sp.wait_ge(self.split, self.number(i, u))
                self.load(sp, u % slots, n, i * per + u + slots)

        if count > 1:
            with sp.Fori(0, count - 1) as i:
                follow(i, range(per))
        follow(count - 1, range(per - slots))
        self.first(sp, n + 1, self.before + count * per)

    def number(self, i, u):
        return self.before + i * self.shape(self.at)[0] + u + 1

    def round_slab(self, eng, i, u):
        per, _, slots, pairs = self.shape(self.at)
        s = u % slots
        eng.wait_ge(self.loaded[s], 16 * (self.used[s] + i * (per // slots) + u // slots + 1))
        if not (isinstance(i, int) and i == 0 and u < pairs):
            eng.wait_ge(self.freed, self.number(i, u) - pairs)
        hi = self.pairs[u % pairs].hi[:]
        if eng is self.nc.gpsimd:
            one = self.ones.unsqueeze(1).to_broadcast([P, KT, P])
            self.nc.gpsimd.tensor_tensor(*(x.rearrange("p (k f) -> p k f", k=KT) for x in (hi, self.raw[s][:])), one,
                                         ALU.mult).then_inc(self.rounded, 1)
        else:
            self.nc.scalar.activation(hi, self.raw[s][:], ACT.Copy).then_inc(self.rounded, 1)

    def round_first(self, act, i):
        for u in range(self.shape(self.at)[3]):
            self.round_slab(act, i, u)

    def round_next(self, act, i, u):
        per, _, _, pairs = self.shape(self.at)
        if u + pairs < per:
            self.round_slab(act, i, u + pairs)

    def split_slab(self, pool, i, u):
        _, _, slots, pairs = self.shape(self.at)
        pair = self.pairs[u % pairs]
        pool.wait_ge(self.rounded, self.number(i, u))
        self.nc.gpsimd.tensor_tensor(pair.lo[:], self.raw[u % slots][:], pair.hi[:].bitcast(F32), ALU.subtract).then_inc(self.split, 1)

    def split_all(self, pool):
        per, count, _, _ = self.shape(self.at)
        if count == 1:
            for u in range(per):
                self.split_slab(pool, 0, u)
        else:
            with pool.Fori(0, count) as i:
                for u in range(per):
                    self.split_slab(pool, i, u)

    def pair(self, u):
        return self.pairs[u % self.shape(self.at)[3]]

    def slab(self, pe, i, u):
        pe.wait_ge(self.split, self.number(i, u))
        return self.pair(u), self.freed

    def wait_used(self, eng, i, u):
        eng.wait_ge(self.freed, self.number(i, u))

    def close(self):
        per, count, slots, _ = self.shape(self.at)
        for s in range(slots):
            self.used[s] += count * per // slots
        self.before += count * per
        self.at += 1


class Core:

    spent = []


def setup(c, a, ctx):
    nc = c.nc

    def sb(name, shape, dt=F32):
        return ctx.enter_context(nc.sbuf_tensor(name, shape, dt))

    c.ps = ctx.enter_context(nc.psum_tensor("banks", [P, 8, HALF], F32))
    c.const = sb("const", [P, a["const"].shape[1]])
    c.ident = c.const[:, 0:P]
    c.upto = c.const[:, P:2 * P]
    c.since = c.const[:, 2 * P:3 * P]
    c.after = c.const[:, 3 * P:4 * P]
    c.ones = c.const[:, 4 * P:5 * P]
    c.ring.ones = c.ones
    c.blocks = c.const[:, 5 * P:6 * P]
    c.mask_f = c.const[:, 6 * P:13 * P].rearrange("p (m f) -> p m f", m=LEVELS)
    c.mask_b = c.const[:, 13 * P:20 * P].rearrange("p (m f) -> p m f", m=LEVELS)
    c.eps = c.const[:, 20 * P:20 * P + 1]
    c.eps_k = c.const[:, 20 * P + 1:20 * P + 2]
    c.x = sb("x", [P, TILES, D])
    c.cols = sb("cols", [P, a["cols"].shape[1]])
    c.c_act = sb("c_act", [P, 2, KT, 2])
    c.c_pair = sb("c_pair", [P, 2, KT, 2, 2], F32R)
    c.mod = sb("mod", [P, 6, KT, 2])
    c.raw = sb("raw", [P, 96])
    c.join = sb("join", [P, 2])
    c.gain = sb("gain", [P, 2, KT, 2])
    with Stage(c, "setup") as st:
        loads = st.sem("loads")
        act_done = st.sem("act_done")
        with st.block() as block:
            @block.sync
            def _(sp):
                c.ring.first(sp, 0)

            @block.scalar
            def _(act):
                act.dma_start(c.cols[:], a["cols"]).then_inc(loads, 16)
                act.dma_start(c.const[:], a["const"]).then_inc(loads, 16)
                act.dma_start(c.x[:, 0:CTX_TILES, :], a["ctx"].rearrange("a (t p) d -> p (a t) d", p=P)).then_inc(loads, 16)
                act.dma_start(c.x[:, CTX_TILES:, :], a["x"].rearrange("a (t p) d -> p (a t) d", p=P)).then_inc(loads, 16)
                act.wait_ge(loads, 65)
                nc.scalar.activation(c.c_act[:], c.cols[:, 0:32].rearrange("p (b k v) -> p b k v", b=2, v=2), ACT.Silu).then_inc(act_done, 1)
                act.wait_ge(act_done, 2)
                nc.scalar.activation(c.c_pair[:, :, :, 0, :], c.c_act[:], ACT.Copy).then_inc(act_done, 1)

            @block.vector
            def _(dve):
                dve.wait_ge(act_done, 3)
                nc.vector.tensor_tensor(c.c_pair[:, :, :, 1, :], c.c_act[:], c.c_pair[:, :, :, 0, :].bitcast(F32), ALU.subtract).then_inc(act_done, 1)
                nc.vector.tensor_tensor(c.join[:], c.ident[:, 0:2], c.ident[:, 2:4], ALU.add).then_inc(act_done, 1)
                dve.wait_ge(act_done, 5)


class Modulation:

    def __init__(self, c, st):
        self.c, self.rows = c, st.sb("mod_rows", [4, 2, HALF])
        self.rows_ready, self.cols_full, self.cols_read = (st.sem(x) for x in ("mod_rows_ready", "mod_cols_full", "mod_cols_read"))

    def slab(self, pe, i, u, m, before=0):
        c, g, j = self.c, m // 4, m % 4
        w, freed = c.ring.slab(pe, i, u)
        if g >= 2 and j == 0:
            pe.wait_ge(self.cols_read, g)
        for kk in range(2):
            for half in (w.hi, w.lo):
                last = c.nc.tensor.matmul(c.ps[0:4, 6 + g % 2, :], c.c_pair[:, c.cond, 2 * j + kk].rearrange("p s v -> p (s v)"),
                                          half[:, kk * HALF:(kk + 1) * HALF], start=j == 0 and kk == 0 and half is w.hi,
                                          stop=j == 3 and kk == 1 and half is w.lo)
        last.then_inc(freed, 1)
        if j == 1 and g:
            self.columns(pe, g - 1, before)

    def columns(self, pe, g, before=0):
        c = self.c
        pe.wait_ge(self.rows_ready, before + g + 2)
        for q in range(4):
            last = c.nc.tensor.matmul(c.ps[:, 6 + g % 2, 2 * q:2 * q + 2], self.rows[0:4, g % 2, q * P:(q + 1) * P], c.join[0:4, :],
                                      start=True, stop=True)
        last.then_inc(self.cols_full, 1)

    def rows_out(self, dve, i, u, g):
        c = self.c
        c.ring.wait_used(dve, i, u)
        c.nc.vector.tensor_copy(self.rows[0:4, g % 2, :], c.ps[0:4, 6 + g % 2, :]).then_inc(self.rows_ready, 1)

    def cols_out(self, dve, g, at, before=0):
        c = self.c
        dve.wait_ge(self.cols_full, before + g + 2)
        c.nc.vector.tensor_copy(c.raw[:, bass.ds(at, 8)], c.ps[:, 6 + g % 2, 0:8]).then_inc(self.cols_read, 1)

    def all_out(self, dve, groups, last_slab, at, begun=False):
        for g in range(groups):
            if g:
                self.cols_out(dve, g - 1, at + 8 * (g - 1))
            if g or not begun:
                self.rows_out(dve, 0, last_slab(g), g)
        self.cols_out(dve, groups - 1, at + 8 * (groups - 1))
        dve.wait_ge(self.cols_read, groups + 1)


def modulation_start(c, name):
    nc, ring = c.nc, c.ring
    with Stage(c, name) as st:
        ring.fourth_pair(st)
        mods = Modulation(c, st)
        with st.block() as block:
            @block.sync
            def _(sp):
                ring.stream(sp, name)

            @block.tensor
            def _(pe):
                for u in range(16):
                    mods.slab(pe, 0, u, u)
                mods.columns(pe, 3)

            @block.scalar
            def _(act):
                ring.round_first(act, 0)
                for u in range(16):
                    ring.round_next(act, 0, u)

            @block.gpsimd
            def _(pool):
                ring.split_all(pool)

            @block.vector
            def _(dve):
                mods.all_out(dve, 4, lambda g: 4 * g + 3, 0)
    ring.close()


def modulation_end(c, name, parts, bias, gains):
    nc = c.nc
    m0, m1 = parts
    with Stage(c, name) as st:
        made = st.sem("made")
        with st.block() as block:
            @block.vector
            def _(dve):
                n = KT * (m1 - m0)
                nc.vector.tensor_tensor(c.mod[:, m0:m1].rearrange("p m k v -> p (m k) v"),
                                        c.raw[:, 16 * m0:16 * m1].rearrange("p (m v) -> p m v", v=2),
                                        bias[:, KT * m0:KT * m1].unsqueeze(2).to_broadcast([P, n, 2]), ALU.add).then_inc(made, 1)
                dve.wait_ge(made, 2)
                for n, g in gains:
                    nc.vector.scalar_tensor_tensor(out=c.gain[:, n], in0=c.mod[:, 3 * n + 1], scalar=1.0,
                                                   in1=g.unsqueeze(2).to_broadcast([P, KT, 2]),
                                                   op0=ALU.add, op1=ALU.mult).then_inc(made, 1)
                dve.wait_ge(made, 1 + len(gains) + 1)


def norm_transpose(c, name, n, first):
    nc = c.nc
    tiles = list(range(first, TILES))
    parts = [(t0, t1, v) for t0, t1, v in ((CTX_TILES, TILES, 0), (0, CTX_TILES, 1)) if t0 >= first]
    with Stage(c, name) as st:
        xn = st.sb("xn", [P, TILES, D])
        h = st.sb("h", [P, 2, HALF])
        stat = st.sb("stat", [P, 3, TILES])
        squared, root, scaled = st.sem("squared"), st.sem("root"), st.sem("scaled")
        recip, turned, placed = st.sem("recip"), st.sem("turned"), st.sem("placed")
        h_rounded, h_split = st.sem("h_rounded"), st.sem("h_split")
        units = [(k, t0, t1, v) for k in range(KT) for t0, t1, v in parts]
        with st.block() as block:
            @block.scalar
            def _(act):
                for t in tiles:
                    nc.scalar.activation(xn[:, t, :], c.x[:, t, :], ACT.Square, accum_out=stat[:, 0, t:t + 1]).then_inc(squared, 1)
                act.wait_ge(squared, len(tiles) + 1)
                nc.scalar.activation(stat[:, 1, first:], stat[:, 0, first:], ACT.Sqrt, bias=c.eps, scale=1.0 / D).then_inc(root, 1)
                for q, (k, t0, t1, v) in enumerate(units):
                    act.wait_ge(turned, q + 2)
                    if q >= 2:
                        act.wait_ge(h_split, q)
                    nc.scalar.activation(h[:, q % 2, 0:(t1 - t0) * P], c.ps[:, q % 8, 0:(t1 - t0) * P], ACT.Identity,
                                         scale=c.gain[:, n, k, v:v + 1], bias=c.mod[:, 3 * n, k, v:v + 1]).then_inc(placed, 1)

            @block.vector
            def _(dve):
                dve.wait_ge(root, 2)
                nc.vector.reciprocal(stat[:, 2, first:], stat[:, 1, first:]).then_inc(recip, 1)
                dve.wait_ge(recip, 2)
                for t in tiles:
                    nc.vector.tensor_scalar(xn[:, t, :], c.x[:, t, :], stat[:, 2, t:t + 1], None, ALU.mult).then_inc(scaled, 1)
                for q, (k, t0, t1, v) in enumerate(units):
                    s = slice(t0 * P - c.hT_at, t1 * P - c.hT_at)
                    dve.wait_ge(placed, q + 2)
                    nc.vector.tensor_copy(c.hT.hi[:, k, s], h[:, q % 2, 0:(t1 - t0) * P]).then_inc(h_rounded, 1)
                    dve.wait_ge(h_rounded, q + 2)
                    nc.vector.tensor_tensor(c.hT.lo[:, k, s], h[:, q % 2, 0:(t1 - t0) * P], c.hT.hi[:, k, s].bitcast(F32),
                                            ALU.subtract).then_inc(h_split, 1)
                dve.wait_ge(h_split, len(units) + 1)

            @block.tensor
            def _(pe):
                pe.wait_ge(scaled, len(tiles) + 1)
                q = 0
                for k in range(KT):
                    for t0, t1, v in parts:
                        if q >= 8:
                            pe.wait_ge(placed, q - 6)
                        for t in range(t0, t1):
                            last = nc.tensor.transpose(c.ps[:, q % 8, (t - t0) * P:(t - t0 + 1) * P],
                                                       xn[:, t, k * P:(k + 1) * P], c.ident)
                        last.then_inc(turned, 1)
                        q += 1


def rows_product(c, pe, lhs, tiles, i, u0, kslabs, full, read, reads_before, step=1, mods=None, m0=0):
    nc, ring = c.nc, c.ring
    for j in range(kslabs):
        w, freed = ring.slab(pe, i, u0 + step * j)
        for n, t in enumerate(tiles):
            if j == 0 and reads_before is not None:
                pe.wait_ge(read, reads_before + n + 2)
            for kk in range(2):
                last = product3(nc, c.ps[:, n, :], lhs(2 * j + kk, t), w[:, kk * HALF:(kk + 1) * HALF],
                                j == 0 and kk == 0, j == kslabs - 1 and kk == 1)
            if n == len(tiles) - 1:
                last.then_inc(freed, 1)
            elif j == kslabs - 1:
                last.then_inc(full, 1)
        for m in range(step - 1):
            mods.slab(pe, i, u0 + step * j + 1 + m, m0 + (step - 1) * j + m)


def wait_bank(c, eng, n, tiles, full, groups_before, i, u_last):
    if n < len(tiles) - 1:
        eng.wait_ge(full, groups_before * (len(tiles) - 1) + n + 2)
    else:
        c.ring.wait_used(eng, i, u_last)


def projection(c, name, l, a, step):
    nc, ring = c.nc, c.ring
    tiles = list(range(TILES))
    with Stage(c, name) as st:
        ring.fourth_pair(st)
        wr = st.sb("wr", [P, KT, 32])
        wr_pair = sbuf_pair(st.held.enter_context, nc, f"{name}_wr_pair", [P, KT, 32])
        wr_loaded, full, read, qk_read, r_done = (st.sem(x) for x in ("wr_loaded", "full", "read", "qk_read", "r_done"))
        qk_read_dve, row_set, wr_split = st.sem("qk_read_dve"), st.sem("row_set"), st.sem("wr_split")
        mods = Modulation(c, st) if step > 1 else None
        with st.block() as block:
            @block.sync
            def _(sp):
                sp.dma_start(wr[:], a["w_r"][l]).then_inc(wr_loaded, 16)
                ring.stream(sp, name)

            @block.tensor
            def _(pe):
                for u in range(4):
                    w, freed = ring.slab(pe, 0, step * u)
                    if u >= 3:
                        pe.wait_ge(qk_read, u - 1)
                        pe.wait_ge(qk_read_dve, u - 1)
                    b = 2 * (u % 3)
                    for k in range(KT):
                        product3(nc, c.ps[:, b, :], w[:, k * P:(k + 1) * P], c.hT[:, k, CTX:], k == 0, k == KT - 1)
                    for k in range(KT):
                        last = product3(nc, c.ps[:, b + 1, 0:CTX], w[:, k * P:(k + 1) * P], c.hT[:, k, 0:CTX], k == 0, k == KT - 1)
                    last.then_inc(freed, 1)
                    for m in range(step - 1):
                        mods.slab(pe, 0, step * u + 1 + m, (step - 1) * u + m)
                pe.wait_ge(wr_split, 3)
                pe.wait_ge(qk_read, 3)
                pe.wait_ge(qk_read_dve, 3)
                for k in range(KT):
                    product3(nc, c.ps[0:32, 2, :], wr_pair[:, k, :], c.hT[:, k, CTX:], k == 0, k == KT - 1)
                for k in range(KT):
                    last = product3(nc, c.ps[0:32, 3, 0:CTX], wr_pair[:, k, :], c.hT[:, k, 0:CTX], k == 0, k == KT - 1)
                last.then_inc(r_done, 1)
                pe.wait_ge(qk_read, 7)
                pe.wait_ge(qk_read_dve, 5)
                for g in range(3):
                    rows_product(c, pe, lambda k, t: c.hT[:, k, t * P:(t + 1) * P], tiles, 0, step * (4 + 4 * g), 4,
                                 full, read, 6 * (g - 1) if g else None, step, mods, 4 * (step - 1) * (g + 1))
                if mods:
                    mods.columns(pe, 7)

            @block.scalar
            def _(act):
                ring.round_first(act, 0)
                for u in range(16 * step):
                    piece = u // step
                    if u % step == 0 and piece < 4:
                        ring.wait_used(act, 0, u)
                        nc.scalar.activation(c.gqk[:, piece, CTX:], c.ps[:, 2 * (piece % 3), :], ACT.Copy,
                                             scale=HD ** -0.5 if piece < 2 else 1.0).then_inc(qk_read, 1)
                    elif u % step == 0 and piece % 4 == 3:
                        g = piece // 4 - 1
                        for n, t in enumerate(tiles):
                            wait_bank(c, act, n, tiles, full, g, 0, u)
                            nc.scalar.activation(c.tok[:, t, g * HALF:(g + 1) * HALF], c.ps[:, n, :], ACT.Copy).then_inc(read, 1)
                    ring.round_next(act, 0, u)
                    if u == 4 * step - 1:
                        act.wait_ge(r_done, 2)
                        nc.scalar.activation(c.rT[0:32, CTX:], c.ps[0:32, 2, :], ACT.Copy).then_inc(qk_read, 1)
                        nc.scalar.activation(c.rT[0:32, 0:CTX], c.ps[0:32, 3, 0:CTX], ACT.Copy).then_inc(qk_read, 1)
                act.wait_ge(read, 19)
                act.wait_ge(qk_read, 7)

            @block.gpsimd
            def _(pool):
                ring.split_all(pool)

            @block.vector
            def _(dve):
                nc.vector.memset(c.rT[32:33, :], 1.0).then_inc(row_set, 1)
                dve.wait_ge(wr_loaded, 17)
                nc.vector.tensor_copy(wr_pair.hi[:], wr[:]).then_inc(wr_split, 1)
                dve.wait_ge(wr_split, 2)
                nc.vector.tensor_tensor(wr_pair.lo[:], wr[:], wr_pair.hi[:].bitcast(F32), ALU.subtract).then_inc(wr_split, 1)
                for u in range(4):
                    ring.wait_used(dve, 0, step * u)
                    nc.vector.tensor_scalar(c.gqk[:, u, 0:CTX], c.ps[:, 2 * (u % 3) + 1, 0:CTX],
                                            HD ** -0.5 if u < 2 else 1.0, None, ALU.mult).then_inc(qk_read_dve, 1)
                    if mods and u == 1:
                        mods.rows_out(dve, 0, 5, 0)
                dve.wait_ge(qk_read_dve, 5)
                dve.wait_ge(row_set, 2)
                if mods:
                    mods.all_out(dve, 8, lambda g: 6 * g + 5, 32, True)
    ring.close()


def pooling(c, name, l, a):
    nc = c.nc
    with Stage(c, name) as st:
        band = st.sb("band", [P, 5, 4, P])
        wp = st.sb("wp", [P, 2, P])
        m = st.sb("m", [P, 2, TOK])
        loads, cleared, means, moved, mixed, scaled = (st.sem(x) for x in ("loads", "cleared", "means", "moved", "mixed", "scaled"))
        with st.block() as block:
            @block.sync
            def _(sp):
                sp.dma_start(band[:], a["band"].rearrange("p (r g f) -> p r g f", r=5, g=4)).then_inc(loads, 16)
                sp.wait_ge(cleared, 2)
                for g in range(4):
                    o = 64 * (g % 2)
                    sp.dma_start(wp[o:o + 64, g // 2, o:o + 64], a["w_pool"][l, g]).then_inc(loads, 16)

            @block.vector
            def _(dve):
                nc.vector.memset(wp[:], 0.0).then_inc(cleared, 1)
                for pair in range(2):
                    for n, (s0, s1) in enumerate(((0, CTX), (CTX, TOK))):
                        dve.wait_ge(mixed, 2 * pair + n + 2)
                        nc.vector.tensor_scalar(c.pooled[:, pair, s0:s1], c.ps[:, 4 + 2 * pair + n, 0:s1 - s0],
                                                c.small(l, "s_pool")[:, pair:pair + 1], None, ALU.mult).then_inc(scaled, 1)
                dve.wait_ge(scaled, 5)

            @block.tensor
            def _(pe):
                pe.wait_ge(loads, 81)
                for pair in range(2):
                    for n, (t0, t1) in enumerate(((0, CTX_TILES), (CTX_TILES, TILES))):
                        for gg in range(2):
                            g = 2 * pair + gg
                            for t in range(t0, t1):
                                same = 0 if t == t0 else 2 if t == t1 - 1 else 1
                                terms = [(t, same)] + [(t - 1, 3)] * (t > t0) + [(t + 1, 4)] * (t < t1 - 1)
                                for e, (src, kind) in enumerate(terms):
                                    last = nc.tensor.matmul(c.ps[64 * gg:64 * gg + 64, 2 * pair + n, (t - t0) * P:(t - t0 + 1) * P],
                                                            c.tok[:, src, C_POOL + 64 * g:C_POOL + 64 * g + 64],
                                                            band[:, kind, g, :], start=e == 0, stop=e == len(terms) - 1)
                        last.then_inc(means, 1)
                for pair in range(2):
                    for n, (s0, s1) in enumerate(((0, CTX), (CTX, TOK))):
                        pe.wait_ge(moved, 2 * pair + n + 2)
                        nc.tensor.matmul(c.ps[:, 4 + 2 * pair + n, 0:s1 - s0], wp[:, pair, :], m[:, pair, s0:s1],
                                         start=True, stop=True).then_inc(mixed, 1)

            @block.scalar
            def _(act):
                for pair in range(2):
                    for n, (s0, s1) in enumerate(((0, CTX), (CTX, TOK))):
                        act.wait_ge(means, 2 * pair + n + 2)
                        nc.scalar.activation(m[:, pair, s0:s1], c.ps[:, 2 * pair + n, 0:s1 - s0], ACT.Copy).then_inc(moved, 1)


def gla(c, name, l, a, first):
    nc = c.nc
    C = TILES
    s0 = first * P
    nb = C - first
    with Stage(c, name) as st:
        sb, sem = st.sb, st.sem
        wg = sb("wg", [33, 512])
        bT = sb("bT", [P, 4, TOK])
        A = sb("A", [P, C, 2, 2, P])
        qd = sb("qd", [P, 4, TOK])
        Q = qd[:].rearrange("p d n -> p (d n)").rearrange("p (b h a t f) -> p b h a t f", b=2, h=2, a=2, f=64)
        r1, r2, r3 = (sb(x, [P, C * 512]) for x in ("r1", "r2", "r3"))
        t0_ = r1[:].rearrange("p (t n) -> p t n", t=C)
        F = r1[:].rearrange("p (b a n) -> p b a n", b=2, a=2)
        kdt = r1[:].rearrange("p (t d f) -> p t d f", t=C, d=4)
        la = r2[:].rearrange("p (t n) -> p t n", t=C)
        E = r2[:].rearrange("p (b a n) -> p b a n", b=2, a=2)
        Pm = r2[:].rearrange("p (t d f) -> p t d f", t=C, d=4)
        kd = r3[:].rearrange("p (d n) -> p d n", d=4)
        S = r3[:, 0:5 * 512].rearrange("p (c d f) -> p c d f", c=5, d=4)
        o = r2[:, 0:C * 256].rearrange("p (t h e) -> p t h e", t=C, h=4)
        gg = r2[:, C * 256:].rearrange("p (t h e) -> p t h e", t=C, h=4)
        sq = r1[:, 0:C * 256]
        ebl = sb("ebl", [P, 4, C])
        st_ = sb("st", [P, 3, C * GLA_H])
        grow = sb("grow", [P, 64])
        loads, cleared, logits, exps, la_ready, b_full, b_ready = (sem(x) for x in
            ("loads", "cleared", "logits", "exps", "la_ready", "b_full", "b_ready"))
        diff, ee, level_ready, a_full, a_read = (sem(x) for x in ("diff", "ee", "level_ready", "a_full", "a_read"))
        own_full, own_read = sem("own_full"), sem("own_read")
        step, decays, kd_ready, kdt_full, kdt_read, s_full, s_ready = (sem(x) for x in
            ("step", "decays", "kd_ready", "kdt_full", "kdt_read", "s_full", "s_ready"))
        o_full, o_read, o_sq, o_root, gated = (sem(x) for x in ("o_full", "o_read", "o_sq", "o_root", "gated"))
        last_col = [P - 1, 0]

        def order(d):
            return [0, 1, 2, 3, 4, 5] if d == 0 else [1, 0, 5, 4, 3, 2]

        with st.block() as block:
            @block.sync
            def _(sp):
                sp.wait_ge(cleared, 2)
                sp.dma_start(wg[0:16, 0:256], a["w_gate"][l, 0]).then_inc(loads, 16)
                sp.dma_start(wg[16:32, 256:512], a["w_gate"][l, 1]).then_inc(loads, 16)
                sp.dma_start(wg[32:33, :], a["b_gate"][l:l + 1].rearrange("a d n -> a (d n)")).then_inc(loads, 16)
                sp.dma_start(grow[:], a["g_gla"][l:l + 1, :].to_broadcast([P, 64])).then_inc(loads, 16)

            @block.tensor
            def _(pe):
                pe.wait_ge(loads, 65)
                for t in range(C):
                    nc.tensor.matmul(c.ps[:, t, :], c.rT[0:33, t * P:(t + 1) * P], wg[:], start=True, stop=True).then_inc(logits, 1)
                for t in range(C):
                    pe.wait_ge(la_ready, t + 2)
                    for dp in range(4):
                        last = nc.tensor.matmul(c.ps[:, t, dp * P:(dp + 1) * P], la[:, t, dp * P:(dp + 1) * P],
                                                c.upto if dp < 2 else c.since, start=True, stop=True)
                    last.then_inc(b_full, 1)
                pe.wait_ge(b_ready, C + 1)
                for n in range(nb):
                    r, ch0 = slice(64 * (n % 2), 64 * (n % 2) + 64), first + 2 * (n // 2)
                    for e in range(4):
                        s = slice((ch0 + e // 2) * P, (ch0 + e // 2 + 1) * P)
                        last = nc.tensor.matmul(c.ps[:, n, e * P:(e + 1) * P], c.gqk[r, 2 + e % 2, s], c.gqk[r, e % 2, s], start=True, stop=True)
                    last.then_inc(own_full, 1)
                for lev in range(1, 2 * LEVELS + 1):
                    pe.wait_ge(level_ready, lev + 1)
                    if lev == 1:
                        pe.wait_ge(own_read, nb + 1)
                    for n in range(nb // 2):
                        done = (lev - 1) * (nb // 2) + n
                        if done >= 8:
                            pe.wait_ge(a_read, done - 6)
                        for e in range(4):
                            ch = first + 2 * n + e // 2
                            last = nc.tensor.matmul(c.ps[:, done % 8, e * P:(e + 1) * P].rearrange("p (h f) -> p h f", h=2),
                                                    F[:, lev % 2, e % 2, ch * P:(ch + 1) * P], Q[:, lev % 2, :, e % 2, ch, :], start=True, stop=True)
                        last.then_inc(a_full, 1)
                pe.wait_ge(a_read, LEVELS * nb + 1)
                for t in range(C):
                    pe.wait_ge(kd_ready, t + 2)
                    for dp in range(4):
                        last = nc.tensor.transpose(c.ps[:, t, dp * P:(dp + 1) * P], kd[:, dp, t * P:(t + 1) * P], c.ident)
                    last.then_inc(kdt_full, 1)
                for t in range(C):
                    pe.wait_ge(kdt_read, t + 2)
                    for dp in range(4):
                        last = nc.tensor.matmul(c.ps[:, t, dp * P:(dp + 1) * P], kdt[:, t, dp, :],
                                                c.tok[:, t, C_GV + (dp % 2) * P:C_GV + (dp % 2) * P + P], start=True, stop=True)
                    last.then_inc(s_full, 1)
                pe.wait_ge(s_ready, 2)
                for t in range(first, C):
                    for p_ in range(2):
                        reg = c.ps[:, t, p_ * P:(p_ + 1) * P]
                        terms = []
                        for d in range(2):
                            at = order(d).index(t)
                            if at:
                                terms.append((qd[:, 2 * d + p_, t * P:(t + 1) * P], S[:, at - 1, 2 * d + p_, :]))
                        for e, (x, y) in enumerate(terms):
                            nc.tensor.matmul(reg, x, y, start=e == 0, stop=e == len(terms) - 1)
                        for hh in range(2):
                            h = 2 * p_ + hh
                            last = nc.tensor.matmul(c.ps[:, t, h * 64:h * 64 + 64], A[:, t, p_, hh, :],
                                                    c.tok[:, t, C_GV + 64 * h:C_GV + 64 * h + 64], start=False, stop=True,
                                                    skip_group_check=True)
                    last.then_inc(o_full, 1)

            @block.scalar
            def _(act):
                for t in range(C):
                    act.wait_ge(logits, t + 2)
                    nc.scalar.activation(t0_[:, t, :], c.ps[:, t, :], ACT.Abs).then_inc(exps, 1)
                act.wait_ge(exps, C + 1)
                nc.scalar.activation(t0_, t0_, ACT.Exp, scale=-1.0).then_inc(exps, 1)
                act.wait_ge(exps, C + 2)
                nc.scalar.activation(t0_, t0_, ACT.Ln, bias=1.0).then_inc(exps, 1)
                for t in range(C):
                    act.wait_ge(b_full, t + 2)
                    nc.scalar.activation(bT[:, :, t * P:(t + 1) * P], c.ps[:, t, :].rearrange("p (d f) -> p d f", d=4), ACT.Copy).then_inc(b_ready, 1)
                act.wait_ge(b_ready, C + 1)
                for lev in range(1, 2 * LEVELS + 1):
                    act.wait_ge(diff, lev + 1)
                    nc.scalar.activation(E[:, lev % 2, :, s0:], E[:, lev % 2, :, s0:], ACT.Exp).then_inc(ee, 1)
                act.wait_ge(a_full, LEVELS * nb + 1)
                nc.scalar.activation(qd[:], bT[:], ACT.Exp).then_inc(decays, 1)
                for t in range(C):
                    for dp in range(4):
                        col = t * P + last_col[dp // 2]
                        last = nc.scalar.activation(kd[:, dp, t * P:(t + 1) * P], bT[:, dp, t * P:(t + 1) * P], ACT.Exp,
                                                    scale=-1.0, bias=bT[:, dp, col:col + 1])
                    last.then_inc(decays, 1)
                for d in range(2):
                    bl = bT[:, 2 * d:2 * d + 2, :].rearrange("p d (t f) -> p d t f", f=P)[:, :, :, last_col[d]]
                    nc.scalar.activation(ebl[:, 2 * d:2 * d + 2, :], bl, ACT.Exp).then_inc(decays, 1)
                for t in range(C):
                    act.wait_ge(kdt_full, t + 2)
                    nc.scalar.activation(kdt[:, t], c.ps[:, t, :].rearrange("p (d f) -> p d f", d=4), ACT.Copy).then_inc(kdt_read, 1)
                for t in range(first, C):
                    act.wait_ge(o_full, t - first + 2)
                    nc.scalar.activation(o[:, t].rearrange("p h e -> p (h e)"), c.ps[:, t, 0:256], ACT.Copy).then_inc(o_read, 1)
                act.wait_ge(o_read, C - first + 1)
                nc.scalar.activation(sq[:, first * 256:], r2[:, first * 256:C * 256], ACT.Square).then_inc(o_sq, 1)
                nc.scalar.activation(gg, c.tok[:, :, C_GG:C_GG + 256].rearrange("p t (h e) -> p t h e", h=4), ACT.Silu).then_inc(o_sq, 1)
                act.wait_ge(gated, 2)
                nc.scalar.activation(st_[:, 1, 4 * first:], st_[:, 0, 4 * first:], ACT.Sqrt, bias=c.eps, scale=1.0 / 64).then_inc(o_root, 1)

            @block.gpsimd
            def _(pool):
                pool.wait_ge(b_ready, C + 1)
                for lev in range(1, 2 * LEVELS + 1):
                    d, m = (lev - 1) // LEVELS, 1 << ((lev - 1) % LEVELS)
                    blk = lambda x: x[:, :, s0:].rearrange("p a (b f) -> p a b f", f=2 * m)
                    b_, E_ = blk(bT[:, 2 * d:2 * d + 2, :]), blk(E[:, lev % 2])
                    edge = m - 1 if d == 0 else m
                    if lev > 2:
                        pool.wait_ge(level_ready, lev - 1)
                    for pr in range(2):
                        lo, hi = b_[:, pr, :, 0:m], b_[:, pr, :, m:2 * m]
                        ref = b_[:, pr, :, edge:edge + 1].to_broadcast(list(lo.shape))
                        if d == 0:
                            nc.gpsimd.tensor_tensor(E_[:, pr, :, 0:m], ref, lo, ALU.subtract)
                            last = nc.gpsimd.tensor_tensor(E_[:, pr, :, m:2 * m], hi, ref, ALU.subtract)
                        else:
                            nc.gpsimd.tensor_tensor(E_[:, pr, :, 0:m], lo, ref, ALU.subtract)
                            last = nc.gpsimd.tensor_tensor(E_[:, pr, :, m:2 * m], ref, hi, ALU.subtract)
                    last.then_inc(diff, 1)

            @block.vector
            def _(dve):
                link = Chain(dve, step)
                nc.vector.memset(wg[:], 0.0).then_inc(cleared, 1)
                nc.vector.memset(qd[:], 0.0).then_inc(cleared, 1)
                dve.wait_ge(exps, C + 3)
                for t in range(C):
                    link(nc.vector.scalar_tensor_tensor(out=la[:, t, :], in0=c.ps[:, t, :], scalar=0.0, in1=t0_[:, t, :],
                                                        op0=ALU.min, op1=ALU.subtract))
                    nc.vector.tensor_scalar(la[:, t, :], la[:, t, :], 1.0 / 16, None, ALU.mult).then_inc(la_ready, 1)
                for n in range(nb):
                    dve.wait_ge(own_full, n + 2)
                    ch0 = first + 2 * (n // 2)
                    nc.vector.tensor_tensor(A[:, ch0:ch0 + 2, :, n % 2].rearrange("p t a f -> p (t a) f"), c.ps[:, n, :].rearrange("p (h f) -> p h f", h=4),
                                            c.ident.unsqueeze(1).to_broadcast([P, 4, P]), ALU.mult).then_inc(own_read, 1)

                def decayed(lev):
                    d, m = (lev - 1) // LEVELS, 1 << ((lev - 1) % LEVELS)
                    blk = lambda x: x[:, :, s0:].rearrange("p a (b f) -> p a b f", f=2 * m)
                    keys, queries = slice(m * d, m * d + m), slice(m - m * d, 2 * m - m * d)
                    F_, E_ = blk(F[:, lev % 2]), blk(E[:, lev % 2])
                    q_, k_ = blk(c.gqk[:, 0:2, :]), blk(c.gqk[:, 2:4, :])
                    dve.wait_ge(ee, lev + 1)
                    if lev > 2:
                        dve.wait_ge(a_full, (lev - 2) * (nb // 2) + 1)
                    nc.vector.tensor_tensor(F_[:, :, :, keys], k_[:, :, :, keys], E_[:, :, :, keys], ALU.mult)
                    for h in range(2):
                        r = slice(64 * h, 64 * h + 64)
                        to = Q[r, lev % 2, h, :, first:, :].rearrange("p a t f -> p a (t f)").rearrange("p a (b m) -> p a b m", m=m)
                        last = nc.vector.tensor_tensor(to, q_[r, :, :, queries], E_[r, :, :, queries], ALU.mult)
                    last.then_inc(level_ready, 1)

                nc.vector.memset(F, 0.0).then_inc(cleared, 1)
                dve.wait_ge(cleared, 4)
                decayed(1)
                dve.wait_ge(own_read, nb + 1)
                for lev in range(1, 2 * LEVELS + 1):
                    if lev < 2 * LEVELS:
                        decayed(lev + 1)
                    d, m = (lev - 1) // LEVELS, 1 << ((lev - 1) % LEVELS)
                    second = lambda x: x.rearrange("p e (b two m) -> p e b two m", two=2, m=m)[:, :, :, 1 - d, :]
                    mask = second((c.mask_f if d == 0 else c.mask_b)[:, (lev - 1) % LEVELS:(lev - 1) % LEVELS + 1, :]).bitcast(U32)
                    for n in range(nb // 2):
                        done = (lev - 1) * (nb // 2) + n
                        dve.wait_ge(a_full, done + 2)
                        if lev > 1:
                            dve.wait_ge(a_read, done - nb // 2 + 2)
                        nc.vector.copy_predicated(second(A[:, first + 2 * n:first + 2 * n + 2].rearrange("p t a h f -> p (t a h) f")),
                                                  mask.to_broadcast([P, 8, 64 // m, m]),
                                                  c.ps[:, done % 8, :].rearrange("p (e b m) -> p e b m", e=8, m=m)).then_inc(a_read, 1)
                dve.wait_ge(a_read, LEVELS * nb + 1)
                dve.wait_ge(decays, 2)
                for d in range(2):
                    last = nc.vector.tensor_tensor(qd[:, 2 * d:2 * d + 2, :], qd[:, 2 * d:2 * d + 2, :], c.gqk[:, 0:2, :], ALU.mult)
                link(last)
                for t in range(C):
                    dve.wait_ge(decays, t + 3)
                    s = slice(t * P, (t + 1) * P)
                    for d in range(2):
                        last = nc.vector.tensor_tensor(kd[:, 2 * d:2 * d + 2, s], kd[:, 2 * d:2 * d + 2, s], c.gqk[:, 2:4, s], ALU.mult)
                    last.then_inc(kd_ready, 1)
                for t in range(C):
                    dve.wait_ge(s_full, t + 2)
                    last = nc.vector.tensor_tensor(Pm[:, t], c.ps[:, t, :].rearrange("p (d f) -> p d f", d=4),
                                                   c.blocks.unsqueeze(1).to_broadcast([P, 4, P]), ALU.mult)
                link(last)
                dve.wait_ge(decays, C + 4)
                for at in range(5):
                    for d in range(2):
                        ch = order(d)[at]
                        for pr in range(2):
                            dp = 2 * d + pr
                            if at == 0:
                                last = nc.vector.tensor_copy(S[:, 0, dp, :], Pm[:, ch, dp, :])
                            else:
                                last = nc.vector.scalar_tensor_tensor(out=S[:, at, dp, :], in0=S[:, at - 1, dp, :],
                                                                      scalar=ebl[:, dp, ch:ch + 1], in1=Pm[:, ch, dp, :],
                                                                      op0=ALU.mult, op1=ALU.add)
                    if at < 4:
                        link(last)
                    else:
                        last.then_inc(s_ready, 1)
                dve.wait_ge(o_sq, 2)
                nc.vector.tensor_reduce(st_[:, 0, 4 * first:], sq[:, first * 256:].rearrange("p (n e) -> p n e", e=64), AX, ALU.add).then_inc(gated, 1)
                dve.wait_ge(o_root, 2)
                link(nc.vector.reciprocal(st_[:, 2, 4 * first:], st_[:, 1, 4 * first:]))
                dve.wait_ge(o_sq, 3)
                link(nc.vector.tensor_tensor(o[:, first:].rearrange("p t h e -> p (t h) e"), o[:, first:].rearrange("p t h e -> p (t h) e"),
                                             st_[:, 2, 4 * first:].unsqueeze(2).to_broadcast([P, (C - first) * 4, 64]), ALU.mult))
                link(nc.vector.tensor_tensor(o[:, first:].rearrange("p t h e -> p (t h) e"), o[:, first:].rearrange("p t h e -> p (t h) e"),
                                             gg[:, first:].rearrange("p t h e -> p (t h) e"), ALU.mult))
                link(nc.vector.tensor_tensor(c.tok[:, first:, 0:256].rearrange("p t (h e) -> p t h e", h=4), o[:, first:],
                                             grow[:].unsqueeze(1).unsqueeze(1).to_broadcast([P, C - first, 4, 64]), ALU.mult))


def attention(c, name, l, a, update_ctx):
    nc = c.nc
    first = 0 if update_ctx else CTX_TILES
    nqk = 10
    C = TILES
    units = [(h, t) for t in range(first, C) for h in range(HEADS_Q)]
    with Stage(c, name) as st:
        sb, sem = st.sb, st.sem
        sq = sb("sq", [P, C, nqk * HD])
        stat = sb("stat", [P, 3, C * nqk])
        grow = sb("grow", [P, nqk, HD])
        rope = sb("rope", [P, 2, LAT_TILES, 32])
        rot = sb("rot", [P, 2, nqk, 2, 16])
        kdup = sb("kdup", [P, C, 4, HD])
        qkT = sb("qkT", [P, 6, TOK])
        p_ = sb("p", [P, 2, TOK])
        pT = sb("pT", [P, 2, TOK])
        sm = sb("sm", [P, 4, len(units)])
        loads, squared, root, step, qk_ready, turned, placed = (sem(x) for x in
            ("loads", "squared", "root", "step", "qk_ready", "turned", "placed"))
        scored, maxed, exped, p_turned, pT_ready, o_full, o_read, summed = (sem(x) for x in
            ("scored", "maxed", "exped", "p_turned", "pT_ready", "o_full", "o_read", "summed"))
        inverted = sem("inverted")
        x = c.tok[:, :, C_AQ:C_AQ + nqk * HD]

        def keys(t):
            return CTX_TILES if t < CTX_TILES else TILES

        def row_max(dve, n):
            dve.wait_ge(scored, n + 2)
            nc.vector.reduce_max(sm[:, 0, n:n + 1], c.ps[:, 2 * (n % 2):2 * (n % 2) + 2, :].rearrange("p b f -> p (b f)")[:, 0:keys(units[n][1]) * P], AX).then_inc(maxed, 1)
            dve.wait_ge(maxed, 2 * n + 2)
            nc.vector.tensor_scalar(sm[:, 1, n:n + 1], sm[:, 0, n:n + 1], -(HD ** -0.5), None, ALU.mult).then_inc(maxed, 1)

        def unit_out(dve, n):
            h, t = units[n]
            col = 256 + HD * (h // 4)
            dve.wait_ge(inverted, n + 2)
            dve.wait_ge(o_full, n + 2)
            nc.vector.tensor_scalar(c.tok[:, t, C_AQ + h * HD:C_AQ + (h + 1) * HD], c.ps[:, 5 + 2 * (n % 2), col:col + HD],
                                    sm[:, 3, n:n + 1], None, ALU.mult).then_inc(o_read, 1)

        with st.block() as block:
            @block.sync
            def _(sp):
                sp.dma_start(grow[:, 0:8, :], a["g_q"][l:l + 1, :].unsqueeze(1).to_broadcast([P, 8, HD])).then_inc(loads, 16)
                sp.dma_start(grow[:, 8:10, :], a["g_k"][l:l + 1, :].unsqueeze(1).to_broadcast([P, 2, HD])).then_inc(loads, 16)
                sp.dma_start(rope[:], a["rope"].rearrange("p (s t f) -> p s t f", s=2, t=LAT_TILES)).then_inc(loads, 16)

            @block.scalar
            def _(act):
                nc.scalar.activation(sq[:], x, ACT.Square).then_inc(squared, 1)
                act.wait_ge(summed, 2)
                nc.scalar.activation(stat[:, 1, :], stat[:, 0, :], ACT.Sqrt, bias=c.eps, scale=1.0 / HD).then_inc(root, 1)
                n = 0
                for t in range(C):
                    for half in range(2):
                        act.wait_ge(turned, n + 2)
                        nc.scalar.activation(qkT[:, 3 * half:3 * half + 3, t * P:(t + 1) * P],
                                             c.ps[:, n % 8, 0:3 * P].rearrange("p (d f) -> p d f", d=3), ACT.Copy).then_inc(placed, 1)
                        n += 1
                for n, (h, t) in enumerate(units):
                    nk = keys(t)
                    act.wait_ge(maxed, 2 * n + 3)
                    if n >= 2:
                        act.wait_ge(p_turned, n)
                    nc.scalar.activation(p_[:, n % 2, 0:nk * P], c.ps[:, 2 * (n % 2):2 * (n % 2) + 2, :].rearrange("p b f -> p (b f)")[:, 0:nk * P],
                                         ACT.Exp, bias=sm[:, 1, n:n + 1], scale=HD ** -0.5, accum_out=sm[:, 2, n:n + 1]).then_inc(exped, 1)

            @block.vector
            def _(dve):
                link = Chain(dve, step)
                dve.wait_ge(squared, 2)
                nc.vector.tensor_reduce(stat[:, 0, :], sq[:].rearrange("p t (h e) -> p (t h) e", e=HD), AX, ALU.add).then_inc(summed, 1)
                dve.wait_ge(root, 2)
                link(nc.vector.reciprocal(stat[:, 2, :], stat[:, 1, :]))
                dve.wait_ge(loads, 49)
                for t in range(C):
                    last = nc.vector.tensor_tensor(x[:, t].rearrange("p (h e) -> p h e", e=HD), x[:, t].rearrange("p (h e) -> p h e", e=HD),
                                                   stat[:, 2, t * nqk:(t + 1) * nqk].unsqueeze(2).to_broadcast([P, nqk, HD]), ALU.mult)
                link(last)
                for t in range(C):
                    last = nc.vector.tensor_tensor(x[:, t].rearrange("p (h e) -> p h e", e=HD), x[:, t].rearrange("p (h e) -> p h e", e=HD),
                                                   grow[:], ALU.mult)
                link(last)
                for t in range(CTX_TILES, C):
                    xv = x[:, t].rearrange("p (h r s f) -> p h r s f", h=nqk, r=2, s=2)
                    x1, x2 = xv[:, :, :, 0, :], xv[:, :, :, 1, :]
                    cs, sn = (rope[:, j, t - CTX_TILES, :].rearrange("p (r f) -> p r f", r=2).unsqueeze(1).to_broadcast([P, nqk, 2, 16])
                              for j in range(2))
                    nc.vector.tensor_tensor(rot[:, 0], x1, sn, ALU.mult)
                    link(nc.vector.tensor_tensor(rot[:, 1], x2, sn, ALU.mult))
                    nc.vector.tensor_tensor(x1, x1, cs, ALU.mult)
                    link(nc.vector.tensor_tensor(x2, x2, cs, ALU.mult))
                    nc.vector.tensor_tensor(x1, x1, rot[:, 1], ALU.subtract)
                    link(nc.vector.tensor_tensor(x2, x2, rot[:, 0], ALU.add))
                for j in range(4):
                    last = nc.vector.tensor_copy(kdup[:, :, j, :], c.tok[:, :, C_AK + HD * (j // 2):C_AK + HD * (j // 2) + HD])
                last.then_inc(qk_ready, 1)
                row_max(dve, 0)
                for n, (h, t) in enumerate(units):
                    nk = keys(t)
                    if n + 1 < len(units):
                        row_max(dve, n + 1)
                    dve.wait_ge(p_turned, n + 2)
                    if n >= 2:
                        dve.wait_ge(o_full, n)
                    nc.vector.tensor_copy(pT[:, n % 2, 0:nk * P], c.ps[:, 4 + 2 * (n % 2):6 + 2 * (n % 2), :].rearrange("p b f -> p (b f)")[:, 0:nk * P]).then_inc(pT_ready, 1)
                    nc.vector.reciprocal(sm[:, 3, n:n + 1], sm[:, 2, n:n + 1]).then_inc(inverted, 1)
                    if n >= 1:
                        unit_out(dve, n - 1)
                unit_out(dve, len(units) - 1)

            @block.tensor
            def _(pe):
                pe.wait_ge(qk_ready, 2)
                n = 0
                for t in range(C):
                    src = [c.tok[:, t, C_AQ + P * j:C_AQ + P * j + P] for j in range(4)] + \
                          [kdup[:, t, 2 * j:2 * j + 2, :].rearrange("p d e -> p (d e)") for j in range(2)]
                    for half in range(2):
                        if n >= 8:
                            pe.wait_ge(placed, n - 6)
                        for j in range(3):
                            last = nc.tensor.transpose(c.ps[:, n % 8, j * P:(j + 1) * P], src[3 * half + j], c.ident)
                        last.then_inc(turned, 1)
                        n += 1
                pe.wait_ge(placed, 2 * C + 1)

                def scores(n):
                    h, t = units[n]
                    r = slice(64 * (h % 2), 64 * (h % 2) + 64)
                    if n >= 2:
                        pe.wait_ge(exped, n)
                    q = qkT[r, h // 2, t * P:(t + 1) * P]
                    for b, (s0, s1) in enumerate(((0, HALF), (HALF, TOK)) if keys(t) == TILES else ((0, CTX),)):
                        last = nc.tensor.matmul(c.ps[:, 2 * (n % 2) + b, 0:s1 - s0], q, qkT[r, 4 + h // 4, s0:s1], start=True, stop=True)
                    last.then_inc(scored, 1)

                def weighted(n):
                    h, t = units[n]
                    pe.wait_ge(pT_ready, n + 2)
                    for s in range(keys(t)):
                        last = nc.tensor.matmul(c.ps[:, 5 + 2 * (n % 2), 256:256 + P], pT[:, n % 2, s * P:(s + 1) * P],
                                                c.tok[:, s, C_AV:C_AV + P], start=s == 0, stop=s == keys(t) - 1)
                    last.then_inc(o_full, 1)

                scores(0)
                for n, (h, t) in enumerate(units):
                    if n + 1 < len(units):
                        scores(n + 1)
                    pe.wait_ge(exped, n + 2)
                    if n >= 2:
                        pe.wait_ge(o_read, n)
                    b = 4 + 2 * (n % 2)
                    for s in range(keys(t)):
                        last = nc.tensor.transpose(c.ps[:, b + s // 4, (s % 4) * P:(s % 4 + 1) * P], p_[:, n % 2, s * P:(s + 1) * P], c.ident)
                    last.then_inc(p_turned, 1)
                    if n >= 1:
                        weighted(n - 1)
                weighted(len(units) - 1)


def turn_heads(c, name, first):
    nc = c.nc
    with Stage(c, name) as st:
        turned, placed, split = st.sem("turned"), st.sem("placed"), st.sem("split")
        cols = [0, P] + [C_AQ + P * j for j in range(4)]
        units = [(k, t0, t1) for k in range(-2, 6) for t0, t1 in ((CTX_TILES, TILES), (0, CTX_TILES)) if t0 >= first]
        pooled = sum(1 for k, _, _ in units if k < 0)

        def source(n):
            k, t0, t1 = units[n]
            return c.pooled[:, 2 + k, t0 * P:t1 * P] if k < 0 else c.ps[:, n % 8, 0:(t1 - t0) * P]

        with st.block() as block:
            @block.tensor
            def _(pe):
                for n, (k, t0, t1) in enumerate(units):
                    if k < 0:
                        continue
                    if n >= 8 + pooled:
                        pe.wait_ge(split, n - 6)
                    for t in range(t0, t1):
                        last = nc.tensor.transpose(c.ps[:, n % 8, (t - t0) * P:(t - t0 + 1) * P], c.tok[:, t, cols[k]:cols[k] + P], c.ident)
                    last.then_inc(turned, 1)

            @block.scalar
            def _(act):
                for n, (k, t0, t1) in enumerate(units):
                    if k >= 0:
                        act.wait_ge(turned, n - pooled + 2)
                    nc.scalar.activation(c.mix.hi[:, 2 + k, t0 * P:t1 * P], source(n), ACT.Copy).then_inc(placed, 1)

            @block.vector
            def _(dve):
                for n, (k, t0, t1) in enumerate(units):
                    dve.wait_ge(placed, n + 2)
                    nc.vector.tensor_tensor(c.mix.lo[:, 2 + k, t0 * P:t1 * P], source(n), c.mix.hi[:, 2 + k, t0 * P:t1 * P].bitcast(F32),
                                            ALU.subtract).then_inc(split, 1)
                dve.wait_ge(split, len(units) + 1)


def out_product(c, name, first, y, step=1):
    nc, ring = c.nc, c.ring
    tiles = list(range(first, TILES))
    with Stage(c, name) as st:
        ring.fourth_pair(st)
        full, read = st.sem("full"), st.sem("read")
        mods = Modulation(c, st) if step > 1 else None
        with st.block() as block:
            @block.sync
            def _(sp):
                ring.stream(sp, name)

            @block.tensor
            def _(pe):
                for h in range(2):
                    rows_product(c, pe, lambda k, t: c.mix[:, k, t * P - c.hT_at:(t + 1) * P - c.hT_at], tiles, 0, step * 4 * h, 4,
                                 full, read, 0 if h else None, step, mods, 4 * (step - 1) * h)
                if mods:
                    mods.columns(pe, 3)

            @block.scalar
            def _(act):
                ring.round_first(act, 0)
                for u in range(8 * step):
                    if u % (4 * step) == 3 * step:
                        h = u // (4 * step)
                        for n, t in enumerate(tiles):
                            wait_bank(c, act, n, tiles, full, h, 0, u)
                            nc.scalar.activation(y[:, t, h * HALF:(h + 1) * HALF], c.ps[:, n, :], ACT.Copy).then_inc(read, 1)
                    ring.round_next(act, 0, u)
                act.wait_ge(read, 2 * len(tiles) + 1)

            @block.gpsimd
            def _(pool):
                ring.split_all(pool)

            if mods:
                @block.vector
                def _(dve):
                    mods.all_out(dve, 4, lambda g: 6 * g + 5, 0)
    ring.close()


def residual(c, name, m, first, y, post=None):
    nc = c.nc
    tiles = list(range(first, TILES))
    vectors = 2 if first == 0 else 1
    shared = len(tiles) // 3 if post is None else 0
    dve_tiles, pool_tiles = tiles[shared:], tiles[:shared]
    with Stage(c, name) as st:
        diag = st.sb("diag", [P, vectors, KT, P])
        gate = st.sb("gate", [P, vectors, D])
        stat = st.sb("stat", [P, 3, TILES])
        diag_ready, rows_ready, copied, step = (st.sem(s) for s in ("diag_ready", "rows_ready", "copied", "step"))
        squared, root, loads, pool_step = (st.sem(s) for s in ("squared", "root", "loads", "pool_step"))
        if post is not None:
            row = st.sb("row", [P, D])
            sq = st.sb("sq", [P, D])
        with st.block() as block:
            if post is not None:
                @block.sync
                def _(sp):
                    sp.dma_start(row[:], post.to_broadcast([P, D])).then_inc(loads, 16)

            @block.vector
            def _(dve):
                link = Chain(dve, step)
                for v in range(vectors):
                    nc.vector.tensor_tensor(diag[:, v], c.ident.unsqueeze(1).to_broadcast([P, KT, P]),
                                            c.mod[:, m, :, v:v + 1].to_broadcast([P, KT, P]), ALU.mult).then_inc(diag_ready, 1)
                if post is not None:
                    dve.wait_ge(root, 2)
                    link(nc.vector.reciprocal(stat[:, 2, first:], stat[:, 1, first:]))
                    dve.wait_ge(loads, 17)
                    dve.wait_ge(copied, vectors + 1)
                    link(nc.vector.tensor_tensor(gate[:, 0, :], gate[:, 0, :], row[:], ALU.mult))
                    for t in dve_tiles:
                        last = nc.vector.scalar_tensor_tensor(out=y[:, t, :], in0=y[:, t, :], scalar=stat[:, 2, t:t + 1], in1=gate[:, 0, :],
                                                              op0=ALU.mult, op1=ALU.mult)
                else:
                    dve.wait_ge(copied, vectors + 1)
                    for t in dve_tiles:
                        last = nc.vector.tensor_tensor(y[:, t, :], y[:, t, :], gate[:, 1 if t < CTX_TILES else 0, :], ALU.mult)
                link(last)
                for t in dve_tiles:
                    last = nc.vector.tensor_tensor(c.x[:, t, :], c.x[:, t, :], y[:, t, :], ALU.add)
                link(last)

            if pool_tiles:
                @block.gpsimd
                def _(pool):
                    pool.wait_ge(copied, vectors + 1)
                    for t in pool_tiles:
                        nc.gpsimd.tensor_tensor(y[:, t, :], y[:, t, :], gate[:, 1 if t < CTX_TILES else 0, :], ALU.mult).then_inc(pool_step, 1)
                    for n, t in enumerate(pool_tiles):
                        pool.wait_ge(pool_step, n + 2)
                        nc.gpsimd.tensor_tensor(c.x[:, t, :], c.x[:, t, :], y[:, t, :], ALU.add).then_inc(pool_step, 1)
                    pool.wait_ge(pool_step, 2 * len(pool_tiles) + 1)

            @block.tensor
            def _(pe):
                for v in range(vectors):
                    pe.wait_ge(diag_ready, v + 2)
                    for h in range(2):
                        nc.tensor.matmul(c.ps[:, 2 * v + h, :], c.ones, diag[:, v, 4 * h:4 * h + 4, :].rearrange("p k f -> p (k f)"),
                                         start=True, stop=True).then_inc(rows_ready, 1)

            @block.scalar
            def _(act):
                if post is not None:
                    for n, t in enumerate(tiles):
                        if n:
                            act.wait_ge(squared, n + 1)
                        nc.scalar.activation(sq[:], y[:, t, :], ACT.Square, accum_out=stat[:, 0, t:t + 1]).then_inc(squared, 1)
                    act.wait_ge(squared, len(tiles) + 1)
                    nc.scalar.activation(stat[:, 1, first:], stat[:, 0, first:], ACT.Sqrt, bias=c.eps, scale=1.0 / D).then_inc(root, 1)
                for v in range(vectors):
                    act.wait_ge(rows_ready, 2 * v + 3)
                    nc.scalar.activation(gate[:, v, :], c.ps[:, 2 * v:2 * v + 2, :].rearrange("p b f -> p (b f)"), ACT.Copy).then_inc(copied, 1)


def mlp(c, name, first, y, with_mods=False):
    nc, ring = c.nc, c.ring
    tiles = list(range(first, TILES))
    nt = len(tiles)
    step = 2 if with_mods else 1
    with Stage(c, name) as st:
        ring.fourth_pair(st)
        held = TOK - first * P
        hid = sbuf_pair(st.held.enter_context, nc, f"{name}_hid", [P, 8, held])
        tmp = st.sb("tmp", [P, 2, held])
        sq = st.sb("sq", [P, 2, held])
        squared, hid_rounded = st.sem("squared"), st.sem("hid_rounded")
        rel, hid_ready, full, read, cleared = (st.sem(s) for s in ("rel", "hid_ready", "full", "read", "cleared"))
        mods = Modulation(c, st) if with_mods else None
        pairs = [6, 4]
        with st.block() as block:
            @block.sync
            def _(sp):
                ring.stream(sp, name)

            @block.tensor
            def _(pe):
                with pe.Fori(0, PASSES) as i:
                    for u in range(8):
                        w, freed = ring.slab(pe, i, u)
                        b = pairs[u % 2]
                        if u == 1:
                            pe.wait_ge(read, i * 2 * nt + 1)
                        if u >= 2:
                            pe.wait_ge(rel, i * 8 + u)
                        elif u == 0:
                            pe.wait_ge(rel, i * 8 + 1)
                            if mods:
                                pe.wait_ge(mods.cols_read, i * 2 + 1)
                        for k in range(KT):
                            last = product3(nc, c.ps[:, b, :], w[:, k * P:(k + 1) * P], c.hT[:, k, CTX - c.hT_at:], k == 0, k == KT - 1)
                        if first == 0:
                            for k in range(KT):
                                last = product3(nc, c.ps[:, b + 1, 0:CTX], w[:, k * P:(k + 1) * P], c.hT[:, k, 0:CTX], k == 0, k == KT - 1)
                        last.then_inc(freed, 1)
                    pe.wait_ge(rel, i * 8 + 9)
                    pe.wait_ge(hid_ready, i * 8 + 9)
                    for h in range(2):
                        for j in range(4):
                            u = 8 + step * (4 * h + j)
                            w, freed = ring.slab(pe, i, u)
                            for n, t in enumerate(tiles):
                                if j == 0:
                                    pe.wait_ge(read, (i * 2 * nt + (n + 1 if h else 0)) + 1)
                                at = (t - CTX_TILES if t >= CTX_TILES else t + LAT_TILES) * P
                                for kk in range(2):
                                    last = product3(nc, c.ps[:, n, :], hid[:, 2 * j + kk, at:at + P],
                                                    w[:, kk * HALF:(kk + 1) * HALF], j == 0 and kk == 0, j == 3 and kk == 1)
                                if n == nt - 1:
                                    last.then_inc(freed, 1)
                                elif j == 3:
                                    last.then_inc(full, 1)
                            if mods:
                                mods.slab(pe, i, u + 1, 4 * h + j, i * 2)
                    if mods:
                        mods.columns(pe, 1, i * 2)

            @block.scalar
            def _(act):
                with act.Fori(0, PASSES) as i:
                    ring.round_first(act, i)
                    for u in range(8):
                        b = pairs[u % 2]
                        ring.wait_used(act, i, u)
                        if u >= 2:
                            act.wait_ge(squared, i * 8 + u)
                        else:
                            act.wait_ge(squared, i * 8 + 1)
                        src = c.ps[:, b:b + 2, :].rearrange("p b f -> p (b f)")[:, 0:held]
                        nc.scalar.activation(tmp[:, u % 2, :], src, ACT.Relu).then_inc(rel, 1)
                        ring.round_next(act, i, u)
                        act.wait_ge(rel, i * 8 + u + 2)
                        if u == 0:
                            ring.wait_used(act, i - 1, 7 + 8 * step)
                        nc.scalar.activation(hid.hi[:, u, :], tmp[:, u % 2, :], ACT.Square).then_inc(hid_rounded, 1)
                    for u in range(8, 8 + 8 * step):
                        ring.round_next(act, i, u)

            @block.gpsimd
            def _(pool):
                ring.split_all(pool)

            @block.vector
            def _(dve):
                nc.vector.memset(y[:, first:, :], 0.0).then_inc(cleared, 1)
                dve.wait_ge(cleared, 2)
                with dve.Fori(0, PASSES) as i:
                    for u in range(8):
                        dve.wait_ge(rel, i * 8 + u + 2)
                        nc.vector.tensor_tensor(sq[:, u % 2, :], tmp[:, u % 2, :], tmp[:, u % 2, :], ALU.mult).then_inc(squared, 1)
                        dve.wait_ge(squared, i * 8 + u + 2)
                        dve.wait_ge(hid_rounded, i * 8 + u + 2)
                        nc.vector.tensor_tensor(hid.lo[:, u, :], sq[:, u % 2, :], hid.hi[:, u, :].bitcast(F32), ALU.subtract).then_inc(hid_ready, 1)
                    dve.wait_ge(read, i * 2 * nt + 1)
                    for h in range(2):
                        if mods and h:
                            mods.cols_out(dve, 0, i * 16 + 32, i * 2)
                        for n, t in enumerate(tiles):
                            if n < nt - 1:
                                dve.wait_ge(full, i * 2 * (nt - 1) + h * (nt - 1) + n + 2)
                            else:
                                ring.wait_used(dve, i, 8 + step * (4 * h + 3))
                            nc.vector.tensor_tensor(y[:, t, h * HALF:(h + 1) * HALF], y[:, t, h * HALF:(h + 1) * HALF],
                                                    c.ps[:, n, :], ALU.add).then_inc(read, 1)
                        if mods:
                            mods.rows_out(dve, i, 15 + 8 * h, h)
                    if mods:
                        mods.cols_out(dve, 1, i * 16 + 40, i * 2)
                dve.wait_ge(read, PASSES * 2 * nt + 1)
                if mods:
                    dve.wait_ge(mods.cols_read, 2 * PASSES + 1)
    ring.close()


def first_layer(c, a, l, update_ctx):
    first = 0 if update_ctx else CTX_TILES
    nc = c.nc
    bias = c.small(l, "b_mod")
    gains = [(0, c.small(l, "g_mix")), (1, c.small(l, "g_mlp"))]
    c.cond, c.hT_at = 0, 0
    pair = lambda held, what: sbuf_pair(held.enter_context, nc, f"{what}{l}", [P, KT, TOK])
    with ExitStack() as held:
        c.tok = held.enter_context(nc.sbuf_tensor(f"tok{l}", [P, TILES, 1536], F32))
        c.gqk = held.enter_context(nc.sbuf_tensor(f"gqk{l}", [P, 4, TOK], F32))
        c.rT = held.enter_context(nc.sbuf_tensor(f"rT{l}", [33, TOK], F32))
        c.pooled = held.enter_context(nc.sbuf_tensor(f"pooled{l}", [P, 2, TOK], F32))
        if l == 0:
            modulation_start(c, "mod0")
            modulation_end(c, "mod0a", (0, 2), bias, gains[:1])
        else:
            modulation_end(c, "mod1", (0, 6), bias, gains)
        with ExitStack() as inner:
            c.hT = pair(inner, "hT")
            norm_transpose(c, f"norm{l}", 0, 0)
            projection(c, f"proj{l}", l, a, 3 if l == 0 else 1)
        if l == 0:
            modulation_end(c, "mod0b", (2, 6), bias, gains[1:])
        pooling(c, f"pool{l}", l, a)
        gla(c, f"gla{l}", l, a, first)
        attention(c, f"attn{l}", l, a, update_ctx)
        c.cond = l
        with ExitStack() as inner:
            c.mix = pair(inner, "mix")
            turn_heads(c, f"turn{l}", first)
            y = c.tok[:, :, 0:D]
            out_product(c, f"out{l}", first, y, 3)
        residual(c, f"res{l}", 2, first, y)
    with ExitStack() as held:
        y = held.enter_context(nc.sbuf_tensor(f"y{l}", [P, TILES, D], F32))
        c.hT = pair(held, "hT_mlp")
        norm_transpose(c, f"norm_mlp{l}", 1, first)
        mlp(c, f"mlp{l}", first, y, True)
        residual(c, f"res_mlp{l}", 5, first, y)


def final_norm(c, name, a):
    nc = c.nc
    first = CTX_TILES
    with Stage(c, name) as st:
        g = st.sb("g", [P, D])
        sq = st.sb("sq", [P, D])
        stat = st.sb("stat", [P, 3, TILES])
        loads, squared, root, step = (st.sem(x) for x in ("loads", "squared", "root", "step"))
        with st.block() as block:
            @block.sync
            def _(sp):
                sp.dma_start(g[:], a["g_final"].unsqueeze(0).to_broadcast([P, D])).then_inc(loads, 16)

            @block.scalar
            def _(act):
                for n, t in enumerate(range(first, TILES)):
                    if n:
                        act.wait_ge(squared, n + 1)
                    nc.scalar.activation(sq[:], c.x[:, t, :], ACT.Square, accum_out=stat[:, 0, t:t + 1]).then_inc(squared, 1)
                act.wait_ge(squared, TILES - first + 1)
                nc.scalar.activation(stat[:, 1, first:], stat[:, 0, first:], ACT.Sqrt, bias=c.eps, scale=1.0 / D).then_inc(root, 1)

            @block.vector
            def _(dve):
                link = Chain(dve, step)
                dve.wait_ge(root, 2)
                link(nc.vector.reciprocal(stat[:, 2, first:], stat[:, 1, first:]))
                dve.wait_ge(loads, 17)
                for t in range(first, TILES):
                    last = nc.vector.scalar_tensor_tensor(out=c.x[:, t, :], in0=c.x[:, t, :], scalar=stat[:, 2, t:t + 1],
                                                          in1=g[:], op0=ALU.mult, op1=ALU.mult)
                link(last)


R_LOG, R_IN, R_OUT, R_LAST, R_STEP, R_STEP_OUT, R_SKIP = range(7)
SSM_H, GDN_H = 32, 16
NH = SSM_H + GDN_H


def rates(c, name, a):
    nc = c.nc
    T4 = LAT_TILES
    with Stage(c, name) as st:
        sb, sem = st.sb, st.sem
        ws = sb("ws", [P, KT, 64])
        bias = sb("bias", [P, NH])
        alog = sb("alog", [P, NH])
        raw = sb("raw", [P, T4, 64])
        u = sb("u", [P, T4, NH])
        v = sb("v", [P, T4, NH])
        w = sb("w", [P, T4, NH])
        e = sb("e", [P, T4, 16])
        loads, full, taken, summed, soft, ready, cums, step = (sem(x) for x in
            ("loads", "full", "taken", "summed", "soft", "ready", "cums", "step"))
        R = c.rates
        with st.block() as block:
            @block.sync
            def _(sp):
                sp.dma_start(ws[:], a["w_rates"]).then_inc(loads, 16)
                sp.dma_start(bias[:, 0:SSM_H], a["ssm_dt_bias_2"].to_broadcast([P, SSM_H])).then_inc(loads, 16)
                sp.dma_start(bias[:, SSM_H:], a["gdn_dt_bias_2"].to_broadcast([P, GDN_H])).then_inc(loads, 16)
                sp.dma_start(alog[:, 0:SSM_H], a["ssm_A_log_2"].to_broadcast([P, SSM_H])).then_inc(loads, 16)
                sp.dma_start(alog[:, SSM_H:], a["gdn_A_log_2"].to_broadcast([P, GDN_H])).then_inc(loads, 16)
                sp.dma_start(R[:, R_SKIP, :, 0:SSM_H], a["ssm_D_2"].unsqueeze(1).to_broadcast([P, T4, SSM_H])).then_inc(loads, 16)

            @block.tensor
            def _(pe):
                pe.wait_ge(loads, 97)
                for t in range(T4):
                    for k in range(KT):
                        for h in (c.hT.hi, c.hT.lo):
                            last = nc.tensor.matmul(c.ps[:, 0, t * 64:(t + 1) * 64], h[:, k, t * P:(t + 1) * P].bitcast(F32), ws[:, k, :],
                                                    start=k == 0 and h is c.hT.hi, stop=k == KT - 1 and h is c.hT.lo)
                last.then_inc(full, 1)
                pe.wait_ge(ready, 2)
                for n, m in enumerate((c.upto, c.after, c.ones)):
                    for t in range(T4):
                        last = nc.tensor.matmul(c.ps[:, 1 + n, t * NH:(t + 1) * NH], m, R[:, R_LOG, t, :], start=True, stop=True)
                    last.then_inc(cums, 1)

            @block.scalar
            def _(act):
                act.wait_ge(full, 2)
                nc.scalar.activation(raw[:], c.ps[:, 0, 0:T4 * 64].rearrange("p (t n) -> p t n", t=T4), ACT.Copy).then_inc(taken, 1)
                act.wait_ge(loads, 97)
                nc.scalar.activation(alog[:], alog[:], ACT.Exp).then_inc(taken, 1)
                act.wait_ge(taken, 2)
                nc.scalar.activation(e[:], raw[:, :, 32:48], ACT.Exp, scale=-1.0).then_inc(taken, 1)
                act.wait_ge(summed, 2)
                nc.scalar.activation(v[:], u[:], ACT.Abs).then_inc(soft, 1)
                act.wait_ge(soft, 2)
                nc.scalar.activation(v[:], v[:], ACT.Exp, scale=-1.0).then_inc(soft, 1)
                act.wait_ge(soft, 3)
                nc.scalar.activation(v[:], v[:], ACT.Ln, bias=1.0).then_inc(soft, 1)
                for n, k in enumerate((R_IN, R_OUT, R_LAST)):
                    act.wait_ge(cums, n + 2)
                    nc.scalar.activation(R[:, k], c.ps[:, 1 + n, 0:T4 * NH].rearrange("p (t n) -> p t n", t=T4), ACT.Exp).then_inc(soft, 1)

            @block.vector
            def _(dve):
                link = Chain(dve, step)
                dve.wait_ge(taken, 2)
                nc.vector.tensor_tensor(u[:, :, 0:SSM_H], raw[:, :, 0:SSM_H], bias[:, 0:SSM_H].unsqueeze(1).to_broadcast([P, T4, SSM_H]), ALU.add)
                nc.vector.tensor_tensor(u[:, :, SSM_H:], raw[:, :, 48:64], bias[:, SSM_H:].unsqueeze(1).to_broadcast([P, T4, GDN_H]), ALU.add).then_inc(summed, 1)
                dve.wait_ge(soft, 4)
                link(nc.vector.scalar_tensor_tensor(out=w[:], in0=u[:], scalar=0.0, in1=v[:], op0=ALU.max, op1=ALU.add))
                dve.wait_ge(taken, 4)
                nc.vector.tensor_copy(R[:, R_STEP, :, 0:SSM_H], w[:, :, 0:SSM_H])
                nc.vector.scalar_tensor_tensor(out=R[:, R_LOG], in0=w[:], scalar=-1.0, in1=alog[:].unsqueeze(1).to_broadcast([P, T4, NH]),
                                               op0=ALU.mult, op1=ALU.mult).then_inc(ready, 1)
                link(nc.vector.tensor_scalar(e[:], e[:], 1.0, None, ALU.add))
                link(nc.vector.reciprocal(R[:, R_STEP, :, SSM_H:], e[:]))
                dve.wait_ge(soft, 6)
                link(nc.vector.tensor_tensor(R[:, R_STEP_OUT], R[:, R_STEP], R[:, R_OUT], ALU.mult))
                nc.vector.memset(R[:, R_SKIP, :, SSM_H:], 0.0)


def scan_products(c, pe, i, u, took):
    nc, ring = c.nc, c.ring
    if not (isinstance(i, int) and i == 0 and u < 2):
        pe.wait_ge(took, i * 6 + u)
    w, freed = ring.slab(pe, i, u)
    for k in range(KT):
        last = product3(nc, c.ps[:, 6 + u % 2, :], w[:, k * P:(k + 1) * P], c.hT[:, k, :], k == 0, k == KT - 1)
    last.then_inc(freed, 1)


def z_products(c, pe, i, n0, n1, took, z_full):
    nc, ring = c.nc, c.ring
    if i is None:
        return
    for n in range(n0, n1):
        t, k = n // KT, n % KT
        if n == 0:
            ring.slab(pe, i, 5)
        if n % 16 == 0:
            pe.wait_ge(took, i * 6 + 3 + n // 16 + 1)
        at = (t % 2) * 256
        last = product3(nc, c.ps[:, 6 + t // 2, at:at + 256], c.hT[:, k, t * P:(t + 1) * P],
                        ring.pair(4 + k // 4)[:, (k % 4) * 256:(k % 4 + 1) * 256], k == 0, k == KT - 1)
        if n == 15:
            last.then_inc(z_full, 1)
        elif n in (27, 31):
            last.then_inc(ring.freed, 1)


def scan_takes(c, act, i, u, took, z_full, conv_done, gated, xin, zs):
    nc, ring = c.nc, c.ring
    later = not (isinstance(i, int) and i == 0)
    if u < 4:
        ring.wait_used(act, i, u)
        if later:
            act.wait_ge(conv_done, i * 4 + u - 2)
        nc.scalar.activation(xin[:, u, 3:], c.ps[:, 6 + u % 2, :], ACT.Copy).then_inc(took, 1)
        return
    if u == 4:
        act.wait_ge(z_full, i + 2)
        if later:
            act.wait_ge(gated, i + 1)
    else:
        ring.wait_used(act, i, 5)
    nc.scalar.activation(zs[:, 2 * (u - 4):2 * (u - 4) + 2, :], c.ps[:, 2 + u, :].rearrange("p (t f) -> p t f", t=2), ACT.Silu).then_inc(took, 1)


def convolve(c, dve, link, g, xin, acc, par, took, sil_ready, conv_done):
    nc = c.nc
    for j in range(4):
        dve.wait_ge(took, g * 6 + j + 2)
        if j >= 2 or not (isinstance(g, int) and g == 0):
            dve.wait_ge(sil_ready, (g * 4 + max(j - 1, 0) if j >= 1 else g * 4) + 1)
        link(nc.vector.tensor_scalar(acc[:, j % 2, :], xin[:, j, 0:LAT], par[:, 4 * j:4 * j + 1], None, ALU.mult))
        for tap in range(1, 4):
            ins = nc.vector.scalar_tensor_tensor(out=acc[:, j % 2, :], in0=xin[:, j, tap:tap + LAT], scalar=par[:, 4 * j + tap:4 * j + tap + 1],
                                                 in1=acc[:, j % 2, :], op0=ALU.mult, op1=ALU.add)
            if tap < 3:
                link(ins)
            else:
                ins.then_inc(conv_done, 1)


def run_groups(act, takes, scan):
    for u in range(6):
        takes(0, u)
    with act.Fori(1, GROUPS) as i:
        for part in range(6):
            scan(i - 1, part)
            takes(i, part)
    for part in range(6):
        scan(GROUPS - 1, part)


def ssm(c, name, a, ysT):
    nc, ring = c.nc, c.ring
    T4, PER = LAT_TILES, 26
    with Stage(c, name) as st:
        sb, sem = st.sb, st.sem
        xin = sb("xin", [P, 4, LAT + 3])
        acc = sb("acc", [P, 2, LAT])
        par = sb("par", [P, 20])
        tab = sb("tab", [P, 7, T4, 4])
        sil = c.x[:, 0:CTX_TILES, :].rearrange("p t d -> p (t d)").rearrange("p (j f) -> p j f", j=4)
        zs = sb("zs", [P, T4, 256])
        am = sb("am", [P, T4, 4, P])
        dec = sb("dec", [P, T4, 4, P])
        cbm = sb("cbm", [P, T4, P])
        btok = sb("btok", [P, T4, P])
        xdt, xw, xd, y = (sb(x, [P, T4, 256]) for x in ("xdt", "xw", "xd", "y"))
        S = sb("S", [P, 4, 256])
        sq = sb("sq", [P, 256])
        stat = sb("stat", [P, 3, T4])
        names = ("took", "z_full", "conv_done", "gated", "sil_ready", "am_ready", "dec_full", "dec_ready", "xs_turned", "xs_read",
                 "b_turned", "btok_ready", "cb_full", "m_ready", "p_full", "y_full", "s_ready", "yo_full", "y_sq", "root",
                 "yn_ready", "yt_full", "placed", "step", "y_ready", "zeroed")
        (took, z_full, conv_done, gated, sil_ready, am_ready, dec_full, dec_ready, xs_turned, xs_read, b_turned, btok_ready,
         cb_full, m_ready, p_full, y_full, s_ready, yo_full, y_sq, root, yn_ready, yt_full, placed, step, y_ready,
         zeroed) = (sem(x) for x in names)

        def half(bank, ch):
            return c.ps[:, bank + ch // 2, (ch % 2) * 256:(ch % 2) * 256 + 256]

        with st.block() as block:
            @block.sync
            def _(sp):
                c.ring.stream(sp, name)

            @block.tensor
            def _(pe):
                def products(i, u):
                    scan_products(c, pe, i, u, took)

                def z(i, n0, n1):
                    z_products(c, pe, i, n0, n1, took, z_full)

                def scan(g, part, i):
                    if part == 1:
                        pe.wait_ge(am_ready, g + 2)
                        pe.wait_ge(placed, g * 2 + 1)
                        for ch in range(T4):
                            nc.tensor.matmul(c.ps[:, ch, :], c.after, am[:, ch].rearrange("p h f -> p (h f)"), start=True, stop=True).then_inc(dec_full, 1)
                        pe.wait_ge(sil_ready, g * 4 + 3)
                        for b in range(2):
                            for ch in (2 * b, 2 * b + 1):
                                for j in range(2):
                                    last = nc.tensor.transpose(half(4, ch)[:, j * P:(j + 1) * P], sil[:, j, ch * P:(ch + 1) * P], c.ident)
                            last.then_inc(xs_turned, 1)
                    if part == 2:
                        pe.wait_ge(sil_ready, g * 4 + 5)
                        pe.wait_ge(dec_ready, g * 4 + 3)
                        for ch in range(T4):
                            last = nc.tensor.transpose(c.ps[:, 0, ch * P:(ch + 1) * P], sil[:, 2, ch * P:(ch + 1) * P], c.ident)
                        last.then_inc(b_turned, 1)
                        for ch in range(T4):
                            last = nc.tensor.matmul(c.ps[:, 1, ch * P:(ch + 1) * P], sil[:, 2, ch * P:(ch + 1) * P],
                                                    sil[:, 3, ch * P:(ch + 1) * P], start=True, stop=True)
                        last.then_inc(cb_full, 1)
                    if part == 3:
                        z(i, 0, 4)
                        pe.wait_ge(btok_ready, g + 2)
                        pe.wait_ge(xs_read, g * 2 + 3)
                        pe.wait_ge(m_ready, g * 4 + 2)
                        for ch in range(3):
                            last = nc.tensor.matmul(half(0, ch), btok[:, ch, :], xw[:, ch, :], start=True, stop=True)
                        last.then_inc(p_full, 1)
                        pe.wait_ge(dec_ready, g * 4 + 5)
                        for ch in range(T4):
                            pe.wait_ge(m_ready, g * 4 + ch + 2)
                            for h in range(4):
                                last = nc.tensor.matmul(half(2, ch)[:, h * 64:(h + 1) * 64], dec[:, ch, h, :], xdt[:, ch, h * 64:(h + 1) * 64],
                                                        start=True, stop=True)
                            if ch % 2:
                                last.then_inc(y_full, 1)
                    if part == 4:
                        for ch in range(1, T4):
                            z(i, 4 * ch, 4 * ch + 4)
                            pe.wait_ge(s_ready, g * 3 + ch + 1)
                            nc.tensor.matmul(half(4, ch), sil[:, 3, ch * P:(ch + 1) * P], S[:, ch, :], start=True, stop=True).then_inc(yo_full, 1)
                    if part == 5:
                        z(i, 16, 32)
                        pe.wait_ge(yn_ready, g + 2)
                        for j in range(2):
                            for ch in range(T4):
                                last = nc.tensor.transpose(c.ps[:, j, ch * P:(ch + 1) * P], y[:, ch, j * P:(j + 1) * P], c.ident)
                            last.then_inc(yt_full, 1)

                for u in range(4):
                    products(0, u)
                z(0, 0, 32)
                with pe.Fori(1, GROUPS) as i:
                    products(i, 0)
                    products(i, 1)
                    scan(i - 1, 1, i)
                    products(i, 2)
                    scan(i - 1, 2, i)
                    products(i, 3)
                    for part in range(3, 6):
                        scan(i - 1, part, i)
                for part in range(1, 6):
                    scan(GROUPS - 1, part, None)

            @block.scalar
            def _(act):
                def takes(i, u):
                    scan_takes(c, act, i, u, took, z_full, conv_done, gated, xin, zs)

                def scan(g, part):
                    if part == 0:
                        act.wait_ge(yt_full, g * 2 + 1)
                        for j in range(4):
                            act.wait_ge(conv_done, g * 4 + j + 2)
                            nc.scalar.activation(sil[:, j, :], acc[:, j % 2, :], ACT.Silu, bias=par[:, 16 + j:17 + j]).then_inc(sil_ready, 1)
                    if part == 1:
                        for ch in range(T4):
                            act.wait_ge(dec_full, g * 4 + ch + 2)
                            nc.scalar.activation(dec[:, ch].rearrange("p h f -> p (h f)"), c.ps[:, ch, :], ACT.Exp).then_inc(dec_ready, 1)
                    if part == 2:
                        act.wait_ge(b_turned, g + 2)
                        nc.scalar.activation(btok[:].rearrange("p t f -> p (t f)"), c.ps[:, 0, :], ACT.Copy).then_inc(btok_ready, 1)
                    if part == 4:
                        for ch in range(T4):
                            act.wait_ge(y_ready, g * 4 + ch + 2)
                            if ch:
                                act.wait_ge(y_sq, g * 4 + ch + 1)
                            nc.scalar.activation(sq[:], y[:, ch, :], ACT.Square, accum_out=stat[:, 0, ch:ch + 1]).then_inc(y_sq, 1)
                        act.wait_ge(y_sq, g * 4 + 5)
                        nc.scalar.activation(stat[:, 1, :], stat[:, 0, :], ACT.Sqrt, bias=c.eps, scale=1.0 / 256).then_inc(root, 1)
                    if part == 5:
                        for j in range(2):
                            act.wait_ge(yt_full, g * 2 + j + 2)
                            nc.scalar.activation(ysT[:, bass.ds(g * 2 + j, 1), :].rearrange("p a f -> p (a f)"), c.ps[:, j, :], ACT.Copy,
                                                 scale=c.small(0, "ssm_norm_w_2")[:, bass.ds(g * 2 + j, 1)]).then_inc(placed, 1)

                act.wait_ge(zeroed, 2)
                run_groups(act, takes, scan)

            @block.gpsimd
            def _(pool):
                with pool.Fori(0, GROUPS) as i:
                    for u in range(6):
                        ring.round_slab(pool, i, u)
                        ring.split_slab(pool, i, u)

            @block.vector
            def _(dve):
                link = Chain(dve, step)
                nc.vector.memset(xin[:, :, 0:3], 0.0).then_inc(zeroed, 1)
                link.enter_loop()
                with dve.Fori(0, GROUPS) as g:
                    link.iteration(g, PER)
                    dve.wait_ge(sil_ready, g * 4 + 1)
                    nc.vector.tensor_copy(par[:], c.small(0, "ssm_par")[:, bass.ds(g * 20, 20)])
                    link(nc.vector.tensor_copy(tab[:].rearrange("p a t h -> p (a t) h"),
                                               c.rates[:].rearrange("p a t h -> p (a t) h")[:, :, bass.ds(g * 4, 4)]))
                    convolve(c, dve, link, g, xin, acc, par, took, sil_ready, conv_done)
                    for ch in range(T4):
                        last = nc.vector.tensor_tensor(am[:, ch], c.upto.unsqueeze(1).to_broadcast([P, 4, P]),
                                                       tab[:, R_LOG, ch, :].unsqueeze(2).to_broadcast([P, 4, P]), ALU.mult)
                    last.then_inc(am_ready, 1)
                    for b in range(2):
                        dve.wait_ge(xs_turned, g * 2 + b + 2)
                        src = c.ps[:, 4 + b, :].rearrange("p (n e) -> p n e", e=64)
                        for out, k in ((xdt, R_STEP), (xw, R_STEP_OUT), (xd, R_SKIP)):
                            f = tab[:, k].rearrange("p t h -> p (t h)")[:, 8 * b:8 * b + 8].unsqueeze(2).to_broadcast([P, 8, 64])
                            last = nc.vector.tensor_tensor(out[:, 2 * b:2 * b + 2, :].rearrange("p t (h e) -> p (t h) e", e=64), src, f, ALU.mult)
                        last.then_inc(xs_read, 1)
                    dve.wait_ge(cb_full, g + 2)
                    link(nc.vector.tensor_tensor(cbm[:], c.ps[:, 1, :].rearrange("p (t f) -> p t f", t=T4),
                                                 c.upto.unsqueeze(1).to_broadcast([P, T4, P]), ALU.mult))
                    for ch in range(T4):
                        dve.wait_ge(dec_ready, g * 4 + ch + 2)
                        nc.vector.tensor_tensor(dec[:, ch], dec[:, ch], cbm[:, ch].unsqueeze(1).to_broadcast([P, 4, P]), ALU.mult).then_inc(m_ready, 1)
                    dve.wait_ge(p_full, g + 2)
                    nc.vector.tensor_copy(S[:, 1, :], half(0, 0)).then_inc(s_ready, 1)
                    for ch in (1, 2):
                        dve.wait_ge(s_ready, g * 3 + ch + 1)
                        link(nc.vector.tensor_tensor(S[:, ch + 1, :].rearrange("p (h e) -> p h e", h=4), S[:, ch, :].rearrange("p (h e) -> p h e", h=4),
                                                     tab[:, R_LAST, ch, :].unsqueeze(2).to_broadcast([P, 4, 64]), ALU.mult))
                        nc.vector.tensor_tensor(S[:, ch + 1, :], S[:, ch + 1, :], half(0, ch), ALU.add).then_inc(s_ready, 1)
                    for ch in range(T4):
                        dve.wait_ge(y_full, g * 2 + ch // 2 + 2)
                        link(nc.vector.tensor_tensor(y[:, ch, :], half(2, ch), xd[:, ch, :], ALU.add))
                        if ch:
                            dve.wait_ge(yo_full, (g * 3 + (1 if ch == 1 else 3)) + 1)
                            link(nc.vector.tensor_tensor(xd[:, ch, :].rearrange("p (h e) -> p h e", h=4), half(4, ch).rearrange("p (h e) -> p h e", h=4),
                                                         tab[:, R_IN, ch, :].unsqueeze(2).to_broadcast([P, 4, 64]), ALU.mult))
                            link(nc.vector.tensor_tensor(y[:, ch, :], y[:, ch, :], xd[:, ch, :], ALU.add))
                        if ch == 0:
                            dve.wait_ge(took, g * 6 + 7)
                        nc.vector.tensor_tensor(y[:, ch, :], y[:, ch, :], zs[:, ch, :], ALU.mult).then_inc(y_ready, 1)
                    dve.wait_ge(y_ready, g * 4 + 5)
                    dve.wait_ge(root, g + 2)
                    nc.vector.reciprocal(stat[:, 2, :], stat[:, 1, :]).then_inc(gated, 1)
                    dve.wait_ge(gated, g + 2)
                    for ch in range(T4):
                        last = nc.vector.tensor_scalar(y[:, ch, :], y[:, ch, :], stat[:, 2, ch:ch + 1], None, ALU.mult)
                    last.then_inc(yn_ready, 1)
                link.leave_loop(GROUPS, PER)
    c.ring.close()


def gdn(c, name, a, ogT):
    nc, ring = c.nc, c.ring
    T4, PER = LAT_TILES, 29
    with Stage(c, name) as st:
        sb, sem = st.sb, st.sem
        xin = sb("xin", [P, 4, LAT + 3])
        acc = sb("acc", [P, 2, LAT])
        par = sb("par", [P, 16])
        tab = sb("tab", [P, 7, T4, 2])
        sil = c.x[:, 0:CTX_TILES, :].rearrange("p t d -> p (t d)").rearrange("p (j f) -> p j f", j=4)
        vtok, zs = (sb(x, [P, T4, 256]) for x in ("vtok", "zs"))
        dec = sb("dec", [P, T4, 2, P])
        ktok = sb("ktok", [P, T4, P])
        U, Um, X, Y, W, att = (sb(x, [P, T4, 2, P]) for x in ("U", "Um", "X", "Y", "W", "att"))
        sq = Um[:].rearrange("p t h f -> p (t h f)").rearrange("p (a f) -> p a f", a=2)
        rn = W[:].rearrange("p t h f -> p (t h f)").rearrange("p (a f) -> p a f", a=2)
        am = X[:]
        S = sb("S", [P, 2, 256])
        R_, vn, vw = (sb(x, [P, 256]) for x in ("R", "vn", "vw"))
        o = U[:].rearrange("p t h f -> p t (h f)")
        stat = sb("stat", [P, 3, T4 * 2])
        names = ("took", "z_full", "conv_done", "gated", "sil_ready", "am_ready", "dec_full", "dec_ready", "qk_sq", "sums", "qk_root",
                 "qk_ready", "k_turned", "v_turned", "kk_full", "kq_full", "ktok_ready", "vtok_ready", "um_ready", "w_full", "w_ready",
                 "xy_full", "xy_ready", "ks_full", "r_ready", "vn_full", "vn_ready", "p_full", "s_ready", "o_full", "o_ready",
                 "o_sq", "root", "yn_ready", "yt_full", "placed", "step", "zeroed")
        sems = {x: sem(x) for x in names}
        (took, z_full, conv_done, gated, sil_ready, am_ready, dec_full, dec_ready, qk_sq, sums, qk_root, qk_ready, k_turned, v_turned,
         kk_full, kq_full, ktok_ready, vtok_ready, um_ready, w_full, w_ready, xy_full, xy_ready, ks_full, r_ready, vn_full, vn_ready,
         p_full, s_ready, o_full, o_ready, o_sq, root, yn_ready, yt_full, placed, step, zeroed) = (sems[x] for x in names)

        def split(x):
            return x.rearrange("p (h f) -> p h f", h=2)

        steps = [0, 2, 3, 4, 6, 7, 8, 10, 11, 12, 14, 15, 16]

        def chunk(ch):
            return slice(ch * P, (ch + 1) * P)

        def prob(hf):
            return [(2 * hf + e // 2, e % 2) for e in range(4)]

        with st.block() as block:
            @block.sync
            def _(sp):
                c.ring.stream(sp, name)

            @block.tensor
            def _(pe):
                def products(i, u):
                    scan_products(c, pe, i, u, took)

                def z(i, n0, n1):
                    z_products(c, pe, i, n0, n1, took, z_full)

                def level(g, lev):
                    for hf in range(2):
                        pe.wait_ge(um_ready, g * 7 + lev + 2)
                        if lev:
                            pe.wait_ge(xy_ready, (g * 7 + lev - 1) * 2 + hf + 2)
                        for e, (ch, h) in enumerate(prob(hf)):
                            last = nc.tensor.matmul(c.ps[:, 3 * hf, e * P:(e + 1) * P], Um[:, ch, h, :], X[:, ch, h, :] if lev else c.ident,
                                                    start=True, stop=True)
                        last.then_inc(w_full, 1)
                    if lev:
                        for hf in range(2):
                            pe.wait_ge(w_ready, (g * 6 + lev - 1) * 2 + hf + 2)
                            if lev < LEVELS - 1:
                                for e, (ch, h) in enumerate(prob(hf)):
                                    nc.tensor.matmul(c.ps[:, 3 * hf + 1, e * P:(e + 1) * P], Y[:, ch, h, :], W[:, ch, h, :], start=True, stop=True)
                            for e, (ch, h) in enumerate(prob(hf)):
                                last = nc.tensor.matmul(c.ps[:, 3 * hf + 2, e * P:(e + 1) * P], W[:, ch, h, :], Y[:, ch, h, :], start=True, stop=True)
                            last.then_inc(xy_full, 1)

                def scan(g, part, i):
                    if part == 0:
                        pe.wait_ge(placed, g * 2 + 1)
                        for j in range(2):
                            pe.wait_ge(qk_sq, g * 2 + j + 2)
                            nc.tensor.matmul(c.ps[:, j, :], c.ones, sq[:, j, :], start=True, stop=True).then_inc(sums, 1)
                        pe.wait_ge(am_ready, g + 2)
                        for b in range(2):
                            nc.tensor.matmul(c.ps[:, 2 + b, :], c.after, am[:, 2 * b:2 * b + 2].rearrange("p t h f -> p (t h f)"),
                                             start=True, stop=True).then_inc(dec_full, 1)
                    if part == 1:
                        pe.wait_ge(sil_ready, g * 4 + 5)
                        pe.wait_ge(qk_root, g * 2 + 3)
                        for b in range(2):
                            for ch in (2 * b, 2 * b + 1):
                                for j in range(2):
                                    last = nc.tensor.transpose(c.ps[:, b, (ch % 2) * 256 + j * P:(ch % 2) * 256 + (j + 1) * P], sil[:, 2 + j, chunk(ch)], c.ident)
                            last.then_inc(v_turned, 1)
                        pe.wait_ge(qk_ready, g + 2)
                        for ch in range(T4):
                            last = nc.tensor.transpose(c.ps[:, 4, chunk(ch)], sil[:, 1, chunk(ch)], c.ident)
                        last.then_inc(k_turned, 1)
                        for ch in range(T4):
                            last = nc.tensor.matmul(c.ps[:, 5, chunk(ch)], sil[:, 1, chunk(ch)], sil[:, 1, chunk(ch)], start=True, stop=True)
                        last.then_inc(kk_full, 1)
                        pe.wait_ge(dec_ready, g * 2 + 2)
                        for ch in range(T4):
                            last = nc.tensor.matmul(c.ps[:, 2, chunk(ch)], sil[:, 1, chunk(ch)], sil[:, 0, chunk(ch)], start=True, stop=True)
                        last.then_inc(kq_full, 1)
                    if part == 2:
                        pe.wait_ge(vtok_ready, g * 2 + 3)
                        pe.wait_ge(ktok_ready, g + 2)
                        pe.wait_ge(dec_ready, g * 2 + 3)
                        level(g, 0)
                        level(g, 1)
                        level(g, 2)
                    if part == 3:
                        for lev in range(3, LEVELS):
                            level(g, lev)
                    if part == 4:
                        for ch in range(T4):
                            z(i, *steps[3 * ch:3 * ch + 2])
                            if ch:
                                pe.wait_ge(s_ready, g * 3 + ch + 1)
                                nc.tensor.matmul(c.ps[:, 0, 0:256], sil[:, 1, chunk(ch)], S[:, ch % 2, :], start=True, stop=True).then_inc(ks_full, 1)
                                if ch > 1:
                                    pe.wait_ge(o_ready, g * 4 + ch + 1)
                                nc.tensor.matmul(c.ps[:, 3, 0:256], sil[:, 0, chunk(ch)], S[:, ch % 2, :], start=True, stop=True)
                            z(i, *steps[3 * ch + 1:3 * ch + 3])
                            pe.wait_ge(r_ready, g * 4 + ch + 2)
                            if ch == 0:
                                pe.wait_ge(xy_ready, (g * 7 + 6) * 2 + 3)
                            for h in range(2):
                                last = nc.tensor.matmul(c.ps[:, 1, h * P:(h + 1) * P], Y[:, ch, h, :], R_[:, h * P:(h + 1) * P], start=True, stop=True)
                            last.then_inc(vn_full, 1)
                            z(i, *steps[3 * ch + 2:3 * ch + 4])
                            pe.wait_ge(vn_ready, g * 4 + ch + 2)
                            if ch < 3:
                                nc.tensor.matmul(c.ps[:, 2, 0:256], ktok[:, ch, :], vw[:], start=True, stop=True).then_inc(p_full, 1)
                            if ch:
                                pe.wait_ge(o_ready, g * 4 + ch + 1)
                            for h in range(2):
                                last = nc.tensor.matmul(c.ps[:, 4, h * P:(h + 1) * P], att[:, ch, h, :], vn[:, h * P:(h + 1) * P], start=True, stop=True)
                            last.then_inc(o_full, 1)
                    if part == 5:
                        z(i, 16, 32)
                        pe.wait_ge(yn_ready, g + 2)
                        for j in range(2):
                            for ch in range(T4):
                                last = nc.tensor.transpose(c.ps[:, j, chunk(ch)], o[:, ch, j * P:(j + 1) * P], c.ident)
                            last.then_inc(yt_full, 1)

                for u in range(4):
                    products(0, u)
                z(0, 0, 32)
                with pe.Fori(1, GROUPS) as i:
                    products(i, 0)
                    products(i, 1)
                    scan(i - 1, 0, i)
                    products(i, 2)
                    scan(i - 1, 1, i)
                    products(i, 3)
                    for part in range(2, 6):
                        scan(i - 1, part, i)
                for part in range(6):
                    scan(GROUPS - 1, part, None)

            @block.scalar
            def _(act):
                def takes(i, u):
                    scan_takes(c, act, i, u, took, z_full, conv_done, gated, xin, zs)

                def level(g, lev):
                    if lev:
                        for hf in range(2):
                            act.wait_ge(w_full, (g * 7 + lev) * 2 + hf + 2)
                            nc.scalar.activation(W[:, 2 * hf:2 * hf + 2].rearrange("p t h f -> p (t h f)"), c.ps[:, 3 * hf, :], ACT.Copy).then_inc(w_ready, 1)

                def scan(g, part):
                    if part == 0:
                        act.wait_ge(yt_full, g * 2 + 1)
                        for j in range(4):
                            act.wait_ge(conv_done, g * 4 + j + 2)
                            nc.scalar.activation(sil[:, j, :], acc[:, j % 2, :], ACT.Silu).then_inc(sil_ready, 1)
                            if j < 2:
                                act.wait_ge(sil_ready, g * 4 + j + 2)
                                nc.scalar.activation(sq[:, j, :], sil[:, j, :], ACT.Square).then_inc(qk_sq, 1)
                        for j in range(2):
                            act.wait_ge(sums, g * 2 + j + 2)
                            nc.scalar.activation(rn[:, j, :], c.ps[:, j, :], ACT.Sqrt, bias=c.eps if j else c.eps_k,
                                                 scale=1.0 if j else float(P)).then_inc(qk_root, 1)
                        for b in range(2):
                            act.wait_ge(dec_full, g * 2 + b + 2)
                            nc.scalar.activation(dec[:, 2 * b:2 * b + 2].rearrange("p t h f -> p (t h f)"), c.ps[:, 2 + b, :], ACT.Exp).then_inc(dec_ready, 1)
                    if part == 1:
                        for b in range(2):
                            act.wait_ge(v_turned, g * 2 + b + 2)
                            nc.scalar.activation(vtok[:, 2 * b:2 * b + 2, :], c.ps[:, b, :].rearrange("p (t f) -> p t f", t=2), ACT.Copy).then_inc(vtok_ready, 1)
                        act.wait_ge(k_turned, g + 2)
                        nc.scalar.activation(ktok[:].rearrange("p t f -> p (t f)"), c.ps[:, 4, :], ACT.Copy).then_inc(ktok_ready, 1)
                    if part == 2:
                        for lev in range(3):
                            level(g, lev)
                    if part == 3:
                        for lev in range(3, LEVELS):
                            level(g, lev)
                    if part == 4:
                        act.wait_ge(o_ready, g * 4 + 5)
                        act.wait_ge(w_ready, g * 12 + 13)
                        nc.scalar.activation(W[:].rearrange("p t h f -> p (t h f)"), U[:].rearrange("p t h f -> p (t h f)"), ACT.Square).then_inc(o_sq, 1)
                        act.wait_ge(gated, g + 2)
                        nc.scalar.activation(stat[:, 1, :], stat[:, 0, :], ACT.Sqrt, bias=c.eps, scale=1.0 / P).then_inc(root, 1)
                    if part == 5:
                        for j in range(2):
                            act.wait_ge(yt_full, g * 2 + j + 2)
                            nc.scalar.activation(ogT[:, bass.ds(g * 2 + j, 1), :].rearrange("p a f -> p (a f)"), c.ps[:, j, :], ACT.Copy,
                                                 scale=c.small(0, "gdn_norm_w_2")).then_inc(placed, 1)

                act.wait_ge(zeroed, 2)
                run_groups(act, takes, scan)

            @block.gpsimd
            def _(pool):
                def slabs(i, us):
                    for u in us:
                        ring.round_slab(pool, i, u)
                        ring.split_slab(pool, i, u)

                def masks(g, levels):
                    for lev in levels:
                        if lev == 1:
                            pool.wait_ge(um_ready, g * 7 + 2)
                        pool.wait_ge(w_full, (g * 7 + lev) * 2 + 1)
                        for ch in range(T4):
                            last = nc.gpsimd.tensor_tensor(Um[:, ch], U[:, ch], c.mask_f[:, lev, :].unsqueeze(1).to_broadcast([P, 2, P]), ALU.mult)
                        last.then_inc(um_ready, 1)

                slabs(0, range(6))
                with pool.Fori(1, GROUPS) as i:
                    slabs(i, range(4))
                    masks(i - 1, range(1, 4))
                    slabs(i, range(4, 5))
                    masks(i - 1, range(4, LEVELS))
                    slabs(i, range(5, 6))
                masks(GROUPS - 1, range(1, LEVELS))

            @block.vector
            def _(dve):
                link = Chain(dve, step)
                nc.vector.memset(xin[:, :, 0:3], 0.0).then_inc(zeroed, 1)
                link.enter_loop()
                with dve.Fori(0, GROUPS) as g:
                    link.iteration(g, PER)
                    nc.vector.tensor_copy(par[:], c.small(0, "gdn_par")[:, bass.ds(g * 16, 16)])
                    link(nc.vector.tensor_copy(tab[:].rearrange("p a t h -> p (a t) h"),
                                               c.rates[:].rearrange("p a t h -> p (a t) h")[:, :, bass.ds(g * 2 + SSM_H, 2)]))
                    convolve(c, dve, link, g, xin, acc, par, took, sil_ready, conv_done)
                    for ch in range(T4):
                        last = nc.vector.tensor_tensor(am[:, ch], c.upto.unsqueeze(1).to_broadcast([P, 2, P]),
                                                       tab[:, R_LOG, ch, :].unsqueeze(2).to_broadcast([P, 2, P]), ALU.mult)
                    last.then_inc(am_ready, 1)
                    for j in range(2):
                        dve.wait_ge(qk_root, g * 2 + j + 2)
                        link(nc.vector.reciprocal(rn[:, j, :], rn[:, j, :]))
                        last = nc.vector.tensor_tensor(sil[:, j, :], sil[:, j, :], rn[:, j, :], ALU.mult)
                    last.then_inc(qk_ready, 1)
                    for ch in range(T4):
                        if ch % 2 == 0:
                            dve.wait_ge(dec_ready, g * 2 + ch // 2 + 2)
                        last = nc.vector.tensor_tensor(dec[:, ch], dec[:, ch], c.upto.unsqueeze(1).to_broadcast([P, 2, P]), ALU.mult)
                    link(last)
                    dve.wait_ge(kk_full, g + 2)
                    for ch in range(T4):
                        last = nc.vector.tensor_tensor(U[:, ch], dec[:, ch], c.ps[:, 5, chunk(ch)].unsqueeze(1).to_broadcast([P, 2, P]), ALU.mult)
                    link(last)
                    link(nc.vector.tensor_tensor(U[:].rearrange("p t h f -> p (t h) f"), U[:].rearrange("p t h f -> p (t h) f"),
                                                 tab[:, R_STEP].rearrange("p t h -> p (t h)").unsqueeze(2).to_broadcast([P, 8, P]), ALU.mult))
                    link(nc.vector.tensor_tensor(Um[:].rearrange("p t h f -> p (t h) f"), U[:].rearrange("p t h f -> p (t h) f"),
                                                 c.mask_f[:, 0, :].unsqueeze(1).to_broadcast([P, 8, P]), ALU.mult))
                    nc.vector.tensor_tensor(Y[:].rearrange("p t h f -> p (t h) f"), c.ident.unsqueeze(1).to_broadcast([P, 8, P]),
                                            Um[:].rearrange("p t h f -> p (t h) f"), ALU.subtract).then_inc(um_ready, 1)
                    dve.wait_ge(kq_full, g + 2)
                    for ch in range(T4):
                        last = nc.vector.tensor_tensor(att[:, ch], dec[:, ch], c.ps[:, 2, chunk(ch)].unsqueeze(1).to_broadcast([P, 2, P]), ALU.mult)
                    link(last)
                    for lev in range(LEVELS):
                        for hf in range(2):
                            part = lambda M: M[:, 2 * hf:2 * hf + 2].rearrange("p t h f -> p (t h f)")
                            if lev == 0:
                                dve.wait_ge(w_full, g * 14 + hf + 2)
                                nc.vector.tensor_tensor(X[:, 2 * hf:2 * hf + 2].rearrange("p t h f -> p (t h) f"), c.ident.unsqueeze(1).to_broadcast([P, 4, P]),
                                                        c.ps[:, 3 * hf, :].rearrange("p (e f) -> p e f", e=4), ALU.subtract).then_inc(xy_ready, 1)
                                continue
                            dve.wait_ge(xy_full, (g * 6 + lev - 1) * 2 + hf + 2)
                            if lev < LEVELS - 1:
                                nc.vector.tensor_tensor(part(X), part(X), c.ps[:, 3 * hf + 1, :], ALU.subtract)
                            nc.vector.tensor_tensor(part(Y), part(Y), c.ps[:, 3 * hf + 2, :], ALU.subtract).then_inc(xy_ready, 1)
                    tb = lambda k, ch: tab[:, k, ch, :].unsqueeze(2).to_broadcast([P, 2, P])
                    for ch in range(T4):
                        if ch:
                            dve.wait_ge(ks_full, g * 3 + ch + 1)
                            link(nc.vector.tensor_tensor(split(R_[:]), split(c.ps[:, 0, 0:256]), tb(R_IN, ch), ALU.mult))
                            nc.vector.tensor_tensor(R_[:], vtok[:, ch, :], R_[:], ALU.subtract).then_inc(r_ready, 1)
                        else:
                            nc.vector.tensor_copy(R_[:], vtok[:, 0, :]).then_inc(r_ready, 1)
                        dve.wait_ge(vn_full, g * 4 + ch + 2)
                        nc.vector.tensor_tensor(split(vn[:]), split(c.ps[:, 1, 0:256]), tb(R_STEP, ch), ALU.mult)
                        nc.vector.tensor_tensor(split(vw[:]), split(c.ps[:, 1, 0:256]), tb(R_STEP_OUT, ch), ALU.mult).then_inc(vn_ready, 1)
                        if ch == 0:
                            dve.wait_ge(p_full, g * 3 + 2)
                            nc.vector.tensor_copy(S[:, 1, :], c.ps[:, 2, 0:256]).then_inc(s_ready, 1)
                        elif ch < 3:
                            link(nc.vector.tensor_tensor(split(S[:, (ch + 1) % 2, :]), split(S[:, ch % 2, :]), tb(R_LAST, ch), ALU.mult))
                            dve.wait_ge(p_full, g * 3 + ch + 2)
                            nc.vector.tensor_tensor(S[:, (ch + 1) % 2, :], S[:, (ch + 1) % 2, :], c.ps[:, 2, 0:256], ALU.add).then_inc(s_ready, 1)
                        dve.wait_ge(o_full, g * 4 + ch + 2)
                        if ch:
                            link(nc.vector.tensor_tensor(split(o[:, ch, :]), split(c.ps[:, 3, 0:256]), tb(R_IN, ch), ALU.mult))
                            nc.vector.tensor_tensor(o[:, ch, :], o[:, ch, :], c.ps[:, 4, 0:256], ALU.add).then_inc(o_ready, 1)
                        else:
                            nc.vector.tensor_copy(o[:, 0, :], c.ps[:, 4, 0:256]).then_inc(o_ready, 1)
                    dve.wait_ge(o_sq, g + 2)
                    nc.vector.tensor_reduce(stat[:, 0, :], W[:].rearrange("p t h f -> p (t h) f"), AX, ALU.add)
                    dve.wait_ge(took, g * 6 + 7)
                    nc.vector.tensor_tensor(o, o, zs[:], ALU.mult).then_inc(gated, 1)
                    dve.wait_ge(gated, g + 2)
                    dve.wait_ge(root, g + 2)
                    link(nc.vector.reciprocal(stat[:, 2, :], stat[:, 1, :]))
                    nc.vector.tensor_tensor(U[:].rearrange("p t h f -> p (t h) f"), U[:].rearrange("p t h f -> p (t h) f"),
                                            stat[:, 2, :].unsqueeze(2).to_broadcast([P, 8, P]), ALU.mult).then_inc(yn_ready, 1)
                link.leave_loop(GROUPS, PER)
    c.ring.close()


def merge(c, name, src, mT, first_branch):
    nc, ring = c.nc, c.ring
    with Stage(c, name) as st:
        ring.fourth_pair(st)
        sg = st.sb("sg", [P, KT, LAT])
        m = st.sb("m", [P, 2, LAT])
        half = sbuf_pair(st.held.enter_context, nc, f"{name}_half", [P, KT, LAT])
        sig_ready, rounded, split, up_read, added = (st.sem(x) for x in ("sig_ready", "rounded", "split", "up_read", "added"))
        with st.block() as block:
            @block.sync
            def _(sp):
                ring.stream(sp, name)

            @block.gpsimd
            def _(pool):
                ring.split_all(pool)

            @block.tensor
            def _(pe):
                for u in range(24):
                    w, freed = ring.slab(pe, 0, u)
                    if 2 <= u < 8:
                        pe.wait_ge(sig_ready, u)
                    elif u == 8:
                        pe.wait_ge(sig_ready, 9)
                    elif u >= 10:
                        pe.wait_ge(up_read, u - 8)
                    for k in range(KT):
                        if u in (8, 16):
                            pe.wait_ge(split, u - 8 + k + 2)
                        x = c.hT if u < 8 else half
                        last = product3(nc, c.ps[:, u % 2, :], w[:, k * P:(k + 1) * P], x[:, k, :], k == 0, k == KT - 1)
                    last.then_inc(freed, 1)

            @block.scalar
            def _(act):
                ring.round_first(act, 0)
                for u in range(24):
                    if u < 8:
                        nc.scalar.activation(half.hi[:, u, :], src[:, u, :], ACT.Copy).then_inc(rounded, 1)
                        ring.wait_used(act, 0, u)
                        nc.scalar.activation(sg[:, u, :], c.ps[:, u % 2, :], ACT.Sigmoid).then_inc(sig_ready, 1)
                    ring.round_next(act, 0, u)
                    if u == 15:
                        ring.wait_used(act, 0, 15)
                        for k in range(KT):
                            nc.scalar.activation(half.hi[:, k, :], src[:, KT + k, :], ACT.Copy).then_inc(rounded, 1)

            @block.vector
            def _(dve):
                def lo(n):
                    dve.wait_ge(rounded, n + 2)
                    nc.vector.tensor_tensor(half.lo[:, n % KT, :], src[:, n, :], half.hi[:, n % KT, :].bitcast(F32), ALU.subtract).then_inc(split, 1)

                for k in range(KT):
                    lo(k)
                for u in range(8, 24):
                    j, n = u % 8, u - 8
                    ring.wait_used(dve, 0, u)
                    dve.wait_ge(sig_ready, j + 2)
                    if first_branch and n < 8:
                        nc.vector.tensor_tensor(mT[:, j, :], c.ps[:, u % 2, :], sg[:, j, :], ALU.mult).then_inc(up_read, 1)
                    else:
                        nc.vector.tensor_tensor(m[:, u % 2, :], c.ps[:, u % 2, :], sg[:, j, :], ALU.mult).then_inc(up_read, 1)
                        dve.wait_ge(up_read, n + 2)
                        nc.vector.tensor_tensor(mT[:, j, :], mT[:, j, :], m[:, u % 2, :], ALU.add).then_inc(added, 1)
                        dve.wait_ge(added, n + 1 - 8 * first_branch + 1)
                    if u == 15:
                        for k in range(KT):
                            lo(KT + k)
    ring.close()


def split_merged(c, name, mT):
    nc = c.nc
    with Stage(c, name) as st:
        rounded, split = st.sem("rounded"), st.sem("split")
        with st.block() as block:
            @block.scalar
            def _(act):
                for k in range(KT):
                    nc.scalar.activation(c.mix.hi[:, k, :], mT[:, k, :], ACT.Copy).then_inc(rounded, 1)

            @block.vector
            def _(dve):
                for k in range(KT):
                    dve.wait_ge(rounded, k + 2)
                    nc.vector.tensor_tensor(c.mix.lo[:, k, :], mT[:, k, :], c.mix.hi[:, k, :].bitcast(F32), ALU.subtract).then_inc(split, 1)
                dve.wait_ge(split, KT + 1)


def second_block(c, a):
    nc = c.nc
    first = CTX_TILES
    pair = lambda held, what: sbuf_pair(held.enter_context, nc, what, [P, KT, LAT])
    c.hT_at = CTX
    final_norm(c, "final", a)
    modulation_end(c, "ada", (0, 6), c.small(0, "b_ada_2"), [(0, c.small(0, "norm_mix_pre_2")), (1, c.small(0, "norm_mlp_pre_2"))])
    with ExitStack() as held:
        c.hT = pair(held, "hT2")
        norm_transpose(c, "norm2", 0, first)
        mT = held.enter_context(nc.sbuf_tensor("mT", [P, KT, LAT], F32))
        c.rates = held.enter_context(nc.sbuf_tensor("rates", [P, 7, LAT_TILES, NH], F32))
        rates(c, "rate", a)
        for n, (scan, branch) in enumerate(((ssm, "ssm"), (gdn, "gdn"))):
            with ExitStack() as inner:
                outT = inner.enter_context(nc.sbuf_tensor(f"{branch}T", [P, 2 * GROUPS, LAT], F32))
                scan(c, branch, a, outT)
                merge(c, f"merge_{branch}", outT, mT, n == 0)
        c.mix = pair(held, "mix2")
        split_merged(c, "split2", mT)
        y = held.enter_context(nc.sbuf_tensor("y2", [P, TILES, D], F32))
        out_product(c, "out2", first, y)
        residual(c, "res2", 2, first, y, a["norm_mix_post_2"])
    with ExitStack() as held:
        y = held.enter_context(nc.sbuf_tensor("y3", [P, TILES, D], F32))
        c.hT = pair(held, "hT3")
        norm_transpose(c, "norm_mlp2", 1, first)
        mlp(c, "mlp2", first, y)
        residual(c, "res_mlp2", 5, first, y, a["norm_mlp_post_2"])


COLS = {}


def build(nc, a, out):
    with ExitStack() as ctx:
        c = Core()
        c.nc = nc
        streams = [("mod0", a["s_mod0"], 16, 1), ("proj0", a["s_in0"], 48, 1), ("out0", a["s_out0"], 24, 1),
                   ("mlp0", a["s_mlp0"], 24, PASSES), ("proj1", a["s_in1"], 16, 1), ("out1", a["s_out1"], 24, 1),
                   ("mlp1", a["s_mlp1"], 24, PASSES), ("ssm", a["s_ssm"], 6, GROUPS), ("merge_ssm", a["s_merge_ssm"], 24, 1),
                   ("gdn", a["s_gdn"], 6, GROUPS), ("merge_gdn", a["s_merge_gdn"], 24, 1), ("out2", a["s_out2"], 8, 1), ("mlp2", a["s_mlp2"], 16, PASSES)]
        c.ring = Ring(nc, ctx, streams)
        c.small = lambda l, name: c.cols[:, COLS[name][0] + l * COLS[name][1]:COLS[name][0] + (l + 1) * COLS[name][1]]
        setup(c, a, ctx)
        first_layer(c, a, 0, True)
        first_layer(c, a, 1, False)
        second_block(c, a)
        with Stage(c, "store") as st:
            stored = st.sem("stored")
            with st.block() as block:
                @block.sync
                def _(sp):
                    sp.dma_start(out.rearrange("a (t p) d -> p (a t) d", p=P), c.x[:, CTX_TILES:, :]).then_inc(stored, 16)
                    sp.wait_ge(stored, 17)


def _column_slabs(w):
    K, N = w.shape
    return w.reshape(K // D, KT, P, N // P, P).transpose(3, 0, 2, 1, 4).reshape(-1, P, D)


def _row_slabs(w):
    K, N = w.shape
    return w.reshape(K // 256, 2, P, N // HALF, HALF).transpose(3, 0, 2, 1, 4).reshape(-1, P, D)


def _z_slabs(w):
    return w.reshape(2, 4, P, 256).transpose(0, 2, 1, 3).reshape(2, P, D)


def _mlp_slabs(up, down):
    u = _column_slabs(up).reshape(PASSES, 8, P, D)
    d = np.stack([_row_slabs(down[q * D:(q + 1) * D]) for q in range(PASSES)])
    return np.concatenate([u, d], 1).reshape(-1, P, D)


def _beside(x, m, n):
    return np.concatenate([x[:, None], m.reshape(len(x), n, P, D)], 1).reshape(-1, P, D)


def _columns(v):
    return v.reshape(-1, P).T


def _constants():
    s, f = np.arange(P)[:, None], np.arange(P)[None, :]
    parts = [s == f, s <= f, s >= f, s > f, (s >= 0) & (f >= 0), s // 64 == f // 64]
    joins = [(s // (2 * m) == f // (2 * m)) & (s % (2 * m) < m) & (f % (2 * m) >= m) for m in (1 << n for n in range(LEVELS))]
    parts += joins + [x.T for x in joins]
    eps = np.zeros((P, 2), np.float32)
    eps[:, 0], eps[:, 1] = EPS, P * EPS
    return np.concatenate([x.astype(np.float32) for x in parts] + [eps], 1)


def _bands():
    out = np.zeros((P, 5, 4, P), np.float32)
    for g, w in enumerate((2, 4, 8, 16)):
        M = np.zeros((LAT, LAT))
        for t in range(LAT):
            lo, hi = max(t - w // 2, 0), min(t + w // 2 - 1, LAT - 1)
            M[lo:hi + 1, t] = 1.0 / (hi - lo + 1)
            M[t, t] -= 1
        out[:, 0, g], out[:, 1, g], out[:, 2, g] = M[:P, :P], M[P:2 * P, P:2 * P], M[3 * P:, 3 * P:]
        out[:, 3, g], out[:, 4, g] = M[:P, P:2 * P], M[2 * P:3 * P, P:2 * P]
    return out.reshape(P, -1)


def _rope():
    half = HD // 2
    inv = (10000.0 ** (-np.arange(0, half, 2, dtype=np.float32) / half)).astype(np.float32)
    n = np.arange(LAT)
    ang = np.stack([(n // 64)[:, None].astype(np.float32) * inv, (n % 64)[:, None].astype(np.float32) * inv], 1)
    out = np.stack([np.cos(ang), np.sin(ang)], 0).reshape(2, LAT_TILES, P, 32).transpose(2, 0, 1, 3)
    return out.reshape(P, -1).astype(np.float32)


def _layout(i):
    r = {}
    vec = [np.stack([_columns(i["c"][0]), _columns(i["c_ctx"])], -1).reshape(P, 16),
           np.stack([_columns(i["c_2"][0])] * 2, -1).reshape(P, 16)]
    at = 32

    def add(name, x, width):
        nonlocal at
        COLS[name] = (at, width)
        vec.append(x)
        at += x.shape[1]

    for n in ("b_mod", "g_mix", "g_mlp", "s_pool"):
        x = _columns(i[n])
        add(n, x, x.shape[1] // 2)
    for n in ("b_ada_2", "norm_mix_pre_2", "norm_mlp_pre_2", "ssm_norm_w_2", "gdn_norm_w_2"):
        x = _columns(i[n])
        add(n, x, x.shape[1])
    taps = i["ssm_conv_w_2"][0].reshape(4, 32, P).transpose(2, 1, 0)
    bias = _columns(i["ssm_conv_b_2"])
    of = [[2 * q, 2 * q + 1, 16 + q, 24 + q] for q in range(GROUPS)]
    add("ssm_par", np.concatenate([y for t in of for y in (taps[:, t].reshape(P, 16), bias[:, t])], 1), 20 * GROUPS)
    taps = i["gdn_conv_w_2"][0].reshape(4, 32, P).transpose(2, 1, 0)
    of = [[q, 8 + q, 16 + 2 * q, 17 + 2 * q] for q in range(GROUPS)]
    add("gdn_par", np.concatenate([taps[:, t].reshape(P, 16) for t in of], 1), 16 * GROUPS)
    r["cols"] = np.concatenate(vec, 1)
    r["const"], r["band"], r["rope"] = _constants(), _bands(), _rope()
    mods = [_row_slabs(w) for w in (i["w_mod"][0], i["w_mod"][1], i["w_ada_2"][0])]
    r["s_mod0"] = mods[0][:16]
    for l in range(2):
        w = i["w_in"][l]
        x = np.concatenate([_column_slabs(w[:, 256:768]), _row_slabs(np.concatenate([w[:, :256], w[:, 768:1280], w[:, 1312:2080]], 1))])
        r[f"s_in{l}"] = _beside(x, mods[0][16:], 2) if l == 0 else x
        r[f"s_out{l}"] = _beside(_row_slabs(i["w_out"][l]), mods[l + 1][:16], 2)
        x, m = _mlp_slabs(i["w_up"][l], i["w_down"][l]).reshape(PASSES, 16, P, D), mods[l + 1][16:].reshape(PASSES, 8, P, D)
        r[f"s_mlp{l}"] = np.stack([np.concatenate([x[q, :8], _beside(x[q, 8:], m[q], 1)]) for q in range(PASSES)]).reshape(-1, P, D)
    r["w_r"] = i["w_in"][:, :, 1280:1312].reshape(2, KT, P, 32).transpose(0, 2, 1, 3)
    w = i["w_in_2"][0]
    z_ssm, xs, B, C, dt, q, k, v, z_gdn, ba, g_ssm, g_gdn = np.split(
        w, np.cumsum([2048, 2048, 1024, 1024, 32, 1024, 1024, 2048, 2048, 32, 1024]), axis=1)
    r["s_ssm"] = np.concatenate([y for n in range(GROUPS) for y in (
        _column_slabs(xs[:, 256 * n:256 * n + 256]), _column_slabs(B[:, P * n:P * n + P]), _column_slabs(C[:, P * n:P * n + P]),
        _z_slabs(z_ssm[:, 256 * n:256 * n + 256]))])
    r["s_gdn"] = np.concatenate([y for n in range(GROUPS) for y in (
        _column_slabs(q[:, P * n:P * n + P]), _column_slabs(k[:, P * n:P * n + P]), _column_slabs(v[:, 256 * n:256 * n + 256]),
        _z_slabs(z_gdn[:, 256 * n:256 * n + 256]))])
    for n, g, up in (("ssm", g_ssm, i["w_ssm_up_2"][0]), ("gdn", g_gdn, i["w_gdn_up_2"][0])):
        halves = [_column_slabs(up[D * h:D * h + D]) for h in range(2)]
        r[f"s_merge_{n}"] = np.concatenate([_column_slabs(g)] + halves)
    r["w_rates"] = np.concatenate([dt, ba], 1).reshape(KT, P, 64).transpose(1, 0, 2)
    r["s_out2"] = _row_slabs(i["w_out_2"][0])
    r["s_mlp2"] = _mlp_slabs(i["w_mlp_up_2"][0], i["w_mlp_down_2"][0])
    for n in ("g_final", "ssm_dt_bias_2", "gdn_dt_bias_2", "ssm_A_log_2", "gdn_A_log_2", "ssm_D_2", "norm_mix_post_2",
              "norm_mlp_post_2", "x", "ctx", "w_pool", "w_gate", "b_gate", "g_gla", "g_q", "g_k"):
        r[n] = i[n]
    return r


def kernel(**inputs):
    import concourse.bacc as _bacc
    from concourse.bass_utils import run_bass_kernel_spmd as _run

    laid = _layout({k: np.asarray(v) for k, v in inputs.items()})
    nc = _bacc.Bacc("TRN2", target_bir_lowering=False, num_devices=1, dynamic_dma_scratch_size=1024)
    arrays, a = {}, {}
    for name, x in laid.items():
        arrays[f"in_{name}_dram"] = np.ascontiguousarray(x)
        a[name] = nc.dram_tensor(f"in_{name}_dram", x.shape, F32, kind="ExternalInput").ap()
    out = nc.dram_tensor("out_0_dram", (1, LAT, D), F32, kind="ExternalOutput").ap()
    build(nc, a, out)
    return _run(nc, [arrays], core_ids=[0]).results[0]["out_0_dram"]
```
